# Optimizing a Trainium2 kernel written in Bass

```python
import math, functools
import jax, jax.numpy as jnp
from jax import lax
import numpy as np

D_MODEL = 1024
BATCH = 1
SEQ = 256
DEPTH = 1
DEC_BATCH = 8
DEC_SEQ = 8
PAST_LEN = 1024
PAGE_SIZE = 128

N_META = 16
RMS_EPS = 1e-6
D_INNER = 2 * D_MODEL
SSD_HEADDIM = 64
SSD_HEADS = D_INNER // SSD_HEADDIM
SSD_GROUPS = 8
D_STATE = 128
CONV_W = 4
CONV_DIM = D_INNER + 2 * SSD_GROUPS * D_STATE
SSD_CHUNK = 128
ATTN_HEADS = 16
ATTN_KV_HEADS = 4
HEAD_DIM = 64
ATTN_REP = ATTN_HEADS // ATTN_KV_HEADS
ATTN_DIM = ATTN_HEADS * HEAD_DIM
KV_DIM = ATTN_KV_HEADS * HEAD_DIM
ATTN_SCALE = HEAD_DIM ** -0.5
Q_BLOCK = 128
FORGET_BIAS = 8.0
IN_DIM = D_INNER + CONV_DIM + SSD_HEADS + ATTN_DIM + 2 * KV_DIM + ATTN_HEADS + 2 * D_MODEL
N_EXPERT_GROUPS = 4
EXPERTS_PER_GROUP = 8
N_EXPERTS = N_EXPERT_GROUPS * EXPERTS_PER_GROUP
TOP_K = 2
D_EXPERT = 512
MOE_BLOCK = 128

kernel_name = 'hybrid_ssd_fox_hmoe_decoder_step'

def rmsnorm(x, g):
    xf = x.astype(jnp.float32)
    xf = xf * lax.rsqrt(jnp.mean(xf * xf, axis=-1, keepdims=True) + RMS_EPS)
    return xf.astype(x.dtype) * g

def grouped_rmsnorm(y, g):
    yf = y.astype(jnp.float32).reshape(y.shape[:-1] + (SSD_GROUPS, D_INNER // SSD_GROUPS))
    yf = yf * lax.rsqrt(jnp.mean(yf * yf, axis=-1, keepdims=True) + RMS_EPS)
    return yf.reshape(y.shape).astype(y.dtype) * g

def causal_dwconv(xpad, w, b):
    l = xpad.shape[1] - (CONV_W - 1)
    out = b
    for i in range(CONV_W):
        out = out + xpad[:, i:i + l] * w[i]
    return out

def ssd_chunked(x, dt, A, Bm, Cm, h0, chunk):
    b, l, nh, p = x.shape
    g, n = Bm.shape[2], Bm.shape[3]
    r = nh // g
    c = l // chunk
    f32 = jnp.float32
    xc = x.astype(f32).reshape(b, c, chunk, g, r, p)
    dtc = dt.astype(f32).reshape(b, c, chunk, g, r)
    Bc = Bm.astype(f32).reshape(b, c, chunk, g, n)
    Cc = Cm.astype(f32).reshape(b, c, chunk, g, n)
    acum = jnp.cumsum(dtc * A.reshape(g, r), axis=2)
    mask = jnp.tril(jnp.ones((chunk, chunk), bool))[:, :, None, None]
    seg = acum[:, :, :, None] - acum[:, :, None, :]
    lmat = jnp.exp(jnp.where(mask, seg, -jnp.inf))
    cb = jnp.einsum('bcign,bcjgn->bcijg', Cc, Bc)
    y_diag = jnp.einsum('bcijgr,bcjgrp->bcigrp', cb[..., None] * lmat * dtc[:, :, None], xc)
    decay_to_end = jnp.exp(acum[:, :, -1:] - acum)
    states = jnp.einsum('bcjgn,bcjgr,bcjgrp->bcgrpn', Bc, decay_to_end * dtc, xc)
    chunk_decay = jnp.exp(acum[:, :, -1])

    def step(h, inp):
        st, dec = inp
        return dec[..., None, None] * h + st, h

    h_last, h_starts = lax.scan(step, h0.astype(f32).reshape(b, g, r, p, n),
                                (jnp.moveaxis(states, 1, 0), jnp.moveaxis(chunk_decay, 1, 0)))
    y_off = jnp.einsum('bcign,bcigr,bcgrpn->bcigrp', Cc, jnp.exp(acum), jnp.moveaxis(h_starts, 0, 1))
    return (y_diag + y_off).reshape(b, l, nh, p), h_last.reshape(b, nh, p, n)

def ssd_prompt(x, dt, A, Bm, Cm):
    h0 = jnp.zeros((x.shape[0], SSD_HEADS, SSD_HEADDIM, D_STATE), jnp.float32)
    m = N_META
    y_m, h_m = ssd_chunked(x[:, :m], dt[:, :m], A, Bm[:, :m], Cm[:, :m], h0, m)
    y_r, h_r = ssd_chunked(x[:, m:], dt[:, m:], A, Bm[:, m:], Cm[:, m:], h_m, SSD_CHUNK)
    return jnp.concatenate([y_m, y_r], axis=1), h_r

def ssd_sample(h0, x, dt, A, Bm, Cm):
    return ssd_chunked(x, dt, A, Bm, Cm, h0, x.shape[1])

def fox_prompt(q, k, v, logf):
    b, l = q.shape[:2]
    nb = -(-l // Q_BLOCK)
    lp = nb * Q_BLOCK
    padw = ((0, 0), (0, lp - l), (0, 0), (0, 0))
    qp = jnp.pad(q, padw).reshape(b, nb, Q_BLOCK, ATTN_KV_HEADS, ATTN_REP, HEAD_DIM)
    kp = jnp.pad(k, padw)
    vp = jnp.pad(v, padw)
    c = jnp.cumsum(jnp.pad(logf, ((0, 0), (0, lp - l), (0, 0))), axis=1).reshape(b, lp, ATTN_KV_HEADS, ATTN_REP)
    c_key = jnp.transpose(c, (0, 2, 3, 1))[:, :, :, None, :]
    c_qry = jnp.moveaxis(c.reshape(b, nb, Q_BLOCK, ATTN_KV_HEADS, ATTN_REP), 1, 0)
    kpos = jnp.arange(lp)

    def block(args):
        qi, ci, i = args
        s = jnp.einsum('bqgrd,bkgd->bgrqk', qi, kp, preferred_element_type=jnp.float32) * ATTN_SCALE
        s = s + jnp.transpose(ci, (0, 2, 3, 1))[..., None] - c_key
        qpos = i * Q_BLOCK + jnp.arange(Q_BLOCK)
        s = jnp.where(kpos[None, :] <= qpos[:, None], s, -jnp.inf)
        p = jax.nn.softmax(s, axis=-1)
        return jnp.einsum('bgrqk,bkgd->bqgrd', p.astype(vp.dtype), vp)

    o = lax.map(block, (jnp.moveaxis(qp, 1, 0), c_qry, jnp.arange(nb)))
    return jnp.moveaxis(o, 0, 1).reshape(b, lp, ATTN_DIM)[:, :l]

def fox_sample(cache_k, cache_v, cache_logf, page_table, layer, q, k, v, logf):
    b, s_new = q.shape[:2]
    past = page_table.shape[1] * PAGE_SIZE
    kp = cache_k[layer][page_table].reshape(b, past, ATTN_KV_HEADS, HEAD_DIM)
    vp = cache_v[layer][page_table].reshape(b, past, ATTN_KV_HEADS, HEAD_DIM)
    lfp = cache_logf[layer][page_table].reshape(b, past, ATTN_HEADS).astype(jnp.float32)
    r = lax.cumsum(lfp, axis=1, reverse=True) - lfp
    cn = jnp.cumsum(logf.astype(jnp.float32), axis=1)
    r_key = jnp.transpose(r.reshape(b, past, ATTN_KV_HEADS, ATTN_REP), (0, 2, 3, 1))[:, :, :, None, :]
    cn_t = jnp.transpose(cn.reshape(b, s_new, ATTN_KV_HEADS, ATTN_REP), (0, 2, 3, 1))
    qg = q.reshape(b, s_new, ATTN_KV_HEADS, ATTN_REP, HEAD_DIM)
    s_past = jnp.einsum('bqgrd,bkgd->bgrqk', qg, kp, preferred_element_type=jnp.float32) * ATTN_SCALE
    s_past = s_past + r_key + cn_t[..., None]
    s_self = jnp.einsum('bqgrd,bkgd->bgrqk', qg, k, preferred_element_type=jnp.float32) * ATTN_SCALE
    s_self = s_self + cn_t[..., :, None] - cn_t[..., None, :]
    s_self = jnp.where(jnp.tril(jnp.ones((s_new, s_new), bool)), s_self, -jnp.inf)
    p = jax.nn.softmax(jnp.concatenate([s_past, s_self], axis=-1), axis=-1)
    o = (jnp.einsum('bgrqk,bkgd->bqgrd', p[..., :past].astype(vp.dtype), vp)
         + jnp.einsum('bgrqk,bkgd->bqgrd', p[..., past:].astype(v.dtype), v))
    return o.reshape(b, s_new, ATTN_DIM)

def grouped_experts(x2, eid, w, w_gate, w_up, w_down):
    t = x2.shape[0]
    a = t * TOP_K
    fe = eid.reshape(a)
    ft = jnp.broadcast_to(jnp.arange(t, dtype=jnp.int32)[:, None], (t, TOP_K)).reshape(a)
    fw = w.reshape(a)
    order = jnp.argsort(fe)
    se = fe[order]
    counts = jnp.bincount(fe, length=N_EXPERTS)
    padded = (counts + MOE_BLOCK - 1) // MOE_BLOCK * MOE_BLOCK
    start = jnp.cumsum(counts) - counts
    pend = jnp.cumsum(padded)
    dest = (pend - padded)[se] + jnp.arange(a) - start[se]
    n_blocks = (a + N_EXPERTS * (MOE_BLOCK - 1) + MOE_BLOCK - 1) // MOE_BLOCK
    rows = n_blocks * MOE_BLOCK
    row_tok = jnp.zeros((rows,), jnp.int32).at[dest].set(ft[order])
    row_w = jnp.zeros((rows,), x2.dtype).at[dest].set(fw[order].astype(x2.dtype))
    block_e = jnp.minimum(jnp.searchsorted(pend, jnp.arange(n_blocks) * MOE_BLOCK, side='right'), N_EXPERTS - 1)

    def block(args):
        tok, wr, e = args
        xb = x2[tok]
        hb = jax.nn.silu(xb @ w_gate[e]) * (xb @ w_up[e])
        return (hb @ w_down[e]) * wr[:, None]

    y_rows = lax.map(block, (row_tok.reshape(n_blocks, MOE_BLOCK), row_w.reshape(n_blocks, MOE_BLOCK), block_e))
    return jax.ops.segment_sum(y_rows.reshape(rows, D_MODEL), row_tok, num_segments=t)

def hier_moe(x2, w_rg, b_rg, w_re, b_re, w_eg, w_eu, w_ed):
    t = x2.shape[0]
    tid = jnp.arange(t)
    gl = (x2 @ w_rg).astype(jnp.float32) + b_rg
    pg = jax.nn.softmax(gl, axis=-1)
    gsel = jnp.argmax(gl, axis=-1)
    wgrp = pg[tid, gsel]
    el = ((x2 @ w_re).astype(jnp.float32) + b_re).reshape(t, N_EXPERT_GROUPS, EXPERTS_PER_GROUP)
    el_sel = el[tid, gsel]
    topl, topi = lax.top_k(el_sel, TOP_K)
    topw = jax.nn.softmax(topl, axis=-1) * wgrp[:, None]
    eid = gsel[:, None] * EXPERTS_PER_GROUP + topi
    return grouped_experts(x2, eid, topw, w_eg, w_eu, w_ed)

def decoder_layer(h, conv_prev, ssm_run, attn_run, norm1_g, w_in, conv_w, conv_b, dt_bias, a_log, d_skip,
                  ssd_norm_g, b_forget, w_ssd_br, w_attn_br, w_out, norm2_g, w_router_group, b_router_group,
                  w_router_expert, b_router_expert, w_exp_gate, w_exp_up, w_exp_down):
    b, l, _ = h.shape
    u = rmsnorm(h, norm1_g) @ w_in
    splits = np.cumsum([D_INNER, CONV_DIM, SSD_HEADS, ATTN_DIM, KV_DIM, KV_DIM, ATTN_HEADS, D_MODEL]).tolist()
    z, xbc, dt_raw, q, k, v, f_raw, gate_s, gate_a = jnp.split(u, splits, axis=-1)
    xpad = jnp.concatenate([conv_prev.astype(xbc.dtype), xbc], axis=1)
    conv_state = xpad[:, -(CONV_W - 1):]
    xbc = jax.nn.silu(causal_dwconv(xpad, conv_w, conv_b))
    xs, bm, cm = jnp.split(xbc, [D_INNER, D_INNER + SSD_GROUPS * D_STATE], axis=-1)
    xs = xs.reshape(b, l, SSD_HEADS, SSD_HEADDIM)
    dt = jax.nn.softplus(dt_raw.astype(jnp.float32) + dt_bias)
    A = -jnp.exp(a_log.astype(jnp.float32))
    y, ssm_state = ssm_run(xs, dt, A, bm.reshape(b, l, SSD_GROUPS, D_STATE), cm.reshape(b, l, SSD_GROUPS, D_STATE))
    y = y.astype(xs.dtype) + d_skip[:, None] * xs
    y = grouped_rmsnorm(y.reshape(b, l, D_INNER) * jax.nn.silu(z), ssd_norm_g)
    logf = jax.nn.log_sigmoid(f_raw.astype(jnp.float32) + b_forget)
    k = k.reshape(b, l, ATTN_KV_HEADS, HEAD_DIM)
    v = v.reshape(b, l, ATTN_KV_HEADS, HEAD_DIM)
    o = attn_run(q.reshape(b, l, ATTN_HEADS, HEAD_DIM), k, v, logf)
    mix = jax.nn.sigmoid(gate_s) * (y @ w_ssd_br) + jax.nn.sigmoid(gate_a) * (o @ w_attn_br)
    h = h + mix @ w_out
    hn = rmsnorm(h, norm2_g).reshape(b * l, D_MODEL)
    h = h + hier_moe(hn, w_router_group, b_router_group, w_router_expert, b_router_expert,
                     w_exp_gate, w_exp_up, w_exp_down).reshape(b, l, D_MODEL)
    return h, (k, v, logf.astype(k.dtype), ssm_state.astype(xs.dtype), conv_state)

def setup_inputs(seed: int = 0) -> dict:
    key = jax.random.key(seed)
    ks = iter(jax.random.split(key, 40))

    def nrm(shape, scale=1.0):
        return jax.random.normal(next(ks), shape, jnp.float32) * scale

    n_pages = PAST_LEN // PAGE_SIZE
    n_used = DEC_BATCH * n_pages
    n_pool = n_used + max(1, n_used // 4)
    x_prompt = nrm((BATCH, SEQ, D_MODEL))
    x_sample = nrm((DEC_BATCH, DEC_SEQ, D_MODEL))
    cache_k = nrm((DEPTH, n_pool, PAGE_SIZE, ATTN_KV_HEADS, HEAD_DIM))
    cache_v = nrm((DEPTH, n_pool, PAGE_SIZE, ATTN_KV_HEADS, HEAD_DIM))
    cache_logf = jax.nn.log_sigmoid(FORGET_BIAS + nrm((DEPTH, n_pool, PAGE_SIZE, ATTN_HEADS)))
    state_ssm = nrm((DEPTH, DEC_BATCH, SSD_HEADS, SSD_HEADDIM, D_STATE), 0.5)
    state_conv = nrm((DEPTH, DEC_BATCH, CONV_W - 1, CONV_DIM))
    page_table = jax.random.permutation(next(ks), n_pool)[:n_used].reshape(DEC_BATCH, n_pages).astype(jnp.int32)
    dt0 = jnp.exp(jax.random.uniform(next(ks), (DEPTH, SSD_HEADS), jnp.float32, math.log(1e-3), math.log(1e-1)))
    dt_bias = dt0 + jnp.log(-jnp.expm1(-dt0))
    a_log = jnp.log(jax.random.uniform(next(ks), (DEPTH, SSD_HEADS), jnp.float32, 1.0, 16.0))
    return {
        'x_prompt': x_prompt,
        'x_sample': x_sample,
        'cache_k': cache_k,
        'cache_v': cache_v,
        'cache_logf': cache_logf,
        'state_ssm': state_ssm,
        'state_conv': state_conv,
        'page_table': page_table,
        'meta_tokens': nrm((N_META, D_MODEL)),
        'norm1_g': 1.0 + nrm((DEPTH, D_MODEL), 0.02),
        'w_in': nrm((DEPTH, D_MODEL, IN_DIM), D_MODEL ** -0.5),
        'conv_w': nrm((DEPTH, CONV_W, CONV_DIM), CONV_W ** -0.5),
        'conv_b': nrm((DEPTH, CONV_DIM), 0.01),
        'dt_bias': dt_bias,
        'a_log': a_log,
        'd_skip': 1.0 + nrm((DEPTH, SSD_HEADS), 0.01),
        'ssd_norm_g': 1.0 + nrm((DEPTH, D_INNER), 0.02),
        'b_forget': FORGET_BIAS + nrm((DEPTH, ATTN_HEADS), 0.1),
        'w_ssd_br': nrm((DEPTH, D_INNER, D_MODEL), D_INNER ** -0.5),
        'w_attn_br': nrm((DEPTH, ATTN_DIM, D_MODEL), ATTN_DIM ** -0.5),
        'w_out': nrm((DEPTH, D_MODEL, D_MODEL), D_MODEL ** -0.5),
        'norm2_g': 1.0 + nrm((DEPTH, D_MODEL), 0.02),
        'w_router_group': nrm((DEPTH, D_MODEL, N_EXPERT_GROUPS), D_MODEL ** -0.5),
        'b_router_group': nrm((DEPTH, N_EXPERT_GROUPS), 0.01),
        'w_router_expert': nrm((DEPTH, D_MODEL, N_EXPERTS), D_MODEL ** -0.5),
        'b_router_expert': nrm((DEPTH, N_EXPERTS), 0.01),
        'w_exp_gate': nrm((DEPTH, N_EXPERTS, D_MODEL, D_EXPERT), D_MODEL ** -0.5),
        'w_exp_up': nrm((DEPTH, N_EXPERTS, D_MODEL, D_EXPERT), D_MODEL ** -0.5),
        'w_exp_down': nrm((DEPTH, N_EXPERTS, D_EXPERT, D_MODEL), D_EXPERT ** -0.5),
        'final_norm_g': 1.0 + nrm((D_MODEL,), 0.02),
    }

def reference(x_prompt, x_sample, cache_k, cache_v, cache_logf, state_ssm, state_conv, page_table, meta_tokens,
              norm1_g, w_in, conv_w, conv_b, dt_bias, a_log, d_skip, ssd_norm_g, b_forget, w_ssd_br, w_attn_br,
              w_out, norm2_g, w_router_group, b_router_group, w_router_expert, b_router_expert, w_exp_gate,
              w_exp_up, w_exp_down, final_norm_g):
    bp = x_prompt.shape[0]
    meta = jnp.broadcast_to(meta_tokens[None].astype(x_prompt.dtype), (bp, N_META, D_MODEL))
    hp = jnp.concatenate([meta, x_prompt], axis=1)
    hs = x_sample
    st_p, st_s = [], []
    for layer in range(DEPTH):
        lw = (norm1_g[layer], w_in[layer], conv_w[layer], conv_b[layer], dt_bias[layer], a_log[layer],
              d_skip[layer], ssd_norm_g[layer], b_forget[layer], w_ssd_br[layer], w_attn_br[layer],
              w_out[layer], norm2_g[layer], w_router_group[layer], b_router_group[layer],
              w_router_expert[layer], b_router_expert[layer], w_exp_gate[layer], w_exp_up[layer],
              w_exp_down[layer])
        conv0 = jnp.zeros((bp, CONV_W - 1, CONV_DIM), hp.dtype)
        hp, sp = decoder_layer(hp, conv0, ssd_prompt, fox_prompt, *lw)
        hs, ss = decoder_layer(hs, state_conv[layer], functools.partial(ssd_sample, state_ssm[layer]),
                               functools.partial(fox_sample, cache_k, cache_v, cache_logf, page_table, layer), *lw)
        st_p.append(sp)
        st_s.append(ss)
    k_prompt, v_prompt, logf_prompt, ssm_prompt, conv_prompt = [jnp.stack(a) for a in zip(*st_p)]
    k_sample, v_sample, logf_sample, ssm_sample, conv_sample = [jnp.stack(a) for a in zip(*st_s)]
    y_prompt = rmsnorm(hp, final_norm_g)[:, N_META:]
    y_sample = rmsnorm(hs, final_norm_g)
    return (y_prompt, y_sample, k_prompt, v_prompt, logf_prompt, ssm_prompt, conv_prompt,
            k_sample, v_sample, logf_sample, ssm_sample, conv_sample)


_drawn_inputs = setup_inputs


def setup_inputs(seed=0):
    import zlib

    import numpy as np

    out = dict(_drawn_inputs(seed))
    spreads = {}
    factors = {'cache_logf': 64.0,
     'conv_b': 3.022,
     'd_skip': 5.948,
     'ssd_norm_g': 2.738,
     'norm2_g': 2.758,
     'b_router_group': 8.0,
     'b_router_expert': 3.34,
     'final_norm_g': 8.585}
    for name, (base, spread) in spreads.items():
        noise = np.random.default_rng([zlib.crc32(name.encode()), seed]).standard_normal(out[name].shape)
        drawn = base * np.exp(spread * noise) if base else spread * noise
        out[name] = __import__('jax').numpy.asarray(drawn.astype(out[name].dtype))
    for name, factor in factors.items():
        out[name] = (out[name] * factor).astype(out[name].dtype)
    return out
```

```python
import concourse.bass as bass
from concourse import mybir
from contextlib import ExitStack

F32 = mybir.dt.float32
I32 = mybir.dt.int32
U32 = mybir.dt.uint32
ALU = mybir.AluOpType
ACT = mybir.ActivationFunctionType
AX = mybir.AxisListType

P = 128
D = 1024
KT = D // P
N_META = 16
SEQ = 256
LP = SEQ + N_META
NSEQ = 8
NEW = 8
NS = NSEQ * NEW
T = LP + NS
ROWS = [128, 128, 80]
COL = [0, 128, 256]
TAIL = LP - 256
TAIL_COL = 320
D_INNER = 2048
HP = 64
NH = 32
G = 8
N = 128
CONV_DIM = 4096
AH = 16
KVH = 4
HD = 64
PAST = 1024
PAGE = 128
NPG = PAST // PAGE
POOL = 80
C_Z, C_X, C_DT, C_Q, C_K, C_F, C_GS = 0, 2048, 6144, 6176, 7200, 7712, 7728
C_B = C_X + D_INNER
C_C = C_B + G * N
EPS = 1e-6
NEG = -1e30
NE = 32
DE = 512
BLK = 64
NBLK = NE + (2 * T) // BLK
SLOTS = NBLK * BLK


def bc(ap, shape):
    return ap.to_broadcast(list(shape))


def setup_phase(nc, A, S, sem):
    with ExitStack() as ctx:
        def tsb(name, shape, dt=F32):
            return ctx.enter_context(nc.sbuf_tensor(name, shape, dt))

        rows64 = tsb("param_rows", [64, P])
        convw_rows = tsb("convw_rows", [P, P])
        sc_rows = tsb("sc_rows", [P, 6, P])
        brow = tsb("brow", [P, 112])
        w_dt = tsb("w_dt", [P, KT, 32])
        w_kvf = tsb("w_kvf", [P, KT, 528])
        xsq = tsb("xsq", [P, D])
        xn = tsb("xn", [P, 3, D])
        ss = tsb("ss", [P, 4])
        small = tsb("small", [P, 3, 48])
        sp_e = tsb("sp_e", [P, 3, 48])
        sp_w = tsb("sp_w", [P, 3, 48])
        sp_l = tsb("sp_l", [P, 3, 48])
        sp_d = tsb("sp_d", [P, 3, 48])
        sp_z = tsb("sp_z", [P, 3, 48])
        dta_rep = tsb("dta_rep", [NS, NH, HP])
        a_neg = tsb("a_neg", [P, 32])
        ps = [ctx.enter_context(nc.psum_tensor(f"ps{i}", [P, 512], F32)) for i in range(8)]
        x_in, par_in, w_in_ready, kv_out = sem("x_in"), sem("par_in"), sem("small_w_in"), sem("kv_out")
        consts, xn_ok, tr_ps, tr_ev = sem("consts"), sem("xn_ok"), sem("tr_ps"), sem("tr_ev")
        par_ps, par_ev = sem("par_ps"), sem("par_ev")
        ssq, rstd_ok = S["row_squares_ok"], S["row_rstd_ok"]
        dt_ps, kv_ps, dtf_ev, ab_exp, sp_exp, sp_ln = (sem("dt_ps"), sem("kv_ps"), sem("dtf_ev"), sem("ab_exp"),
                                                       sem("sp_exp"), sem("sp_ln"))
        dt_ok, kv_ev, cum_ps, cum_ev, kt_ps = (sem("dt_ok"), sem("kv_ev"), sem("cum_ps"), sem("cum_ev"),
                                               sem("kt_ps"))
        win = A["w_in"].rearrange("a (t p) c -> p (a t) c", p=P)
        block = ctx.enter_context(nc.Block())

        @block.sync
        def _(sp):
            xp = A["x_prompt"].rearrange("a s d -> (a s) d")
            sp.dma_start(S["xtok"][0:16, 0, :], A["meta_tokens"]).then_inc(x_in, 16)
            sp.dma_start(S["xtok"][16:128, 0, :], xp[0:112, :]).then_inc(x_in, 16)
            sp.dma_start(S["xtok"][:, 1, :], xp[112:240, :]).then_inc(x_in, 16)
            sp.dma_start(S["xtok"][0:64, 2, :], A["x_sample"].rearrange("a s d -> (a s) d")).then_inc(x_in, 16)
            sp.dma_start(S["xtok"][64:80, 2, :], xp[240:256, :]).then_inc(x_in, 16)
            sp.dma_start(w_dt[:, :, :], win[:, :, C_DT:C_DT + 32]).then_inc(w_in_ready, 16)
            sp.dma_start(w_kvf[:, :, :], win[:, :, C_K:C_K + 528]).then_inc(w_in_ready, 16)
            sp.wait_ge(kv_ev, 6)
            for src, op, os in (("k", "k_p", "k_s"), ("v", "v_p", "v_s")):
                o = A[op].rearrange("a b l g d -> (a b l) (g d)")
                sp.dma_start(o[0:256, :].rearrange("(t p) c -> p t c", p=P), S[src][:, 0:2, :]).then_inc(kv_out, 16)
                sp.dma_start(o[256:272, :], S[src][64:80, 2, :]).then_inc(kv_out, 16)
                sp.dma_start(A[os].rearrange("a b l g d -> (a b l) (g d)"), S[src][0:64, 2, :]).then_inc(kv_out, 16)
            sp.wait_ge(dt_ok, 1)
            o = A["lf_p"].rearrange("a b l h -> (a b l) h")
            sp.dma_start(o[0:256, :].rearrange("(t p) c -> p t c", p=P), S["lf"][:, 0:2, :]).then_inc(kv_out, 16)
            sp.dma_start(o[256:272, :], S["lf"][64:80, 2, :]).then_inc(kv_out, 16)
            sp.dma_start(A["lf_s"].rearrange("a b l h -> (a b l) h"), S["lf"][0:64, 2, :]).then_inc(kv_out, 16)
            sp.wait_ge(kv_out, 144)

        @block.gpsimd
        def _(pool):
            pool.memset(S["ident"][:, :], 0.0)
            pool.memset(S["ones"][:, :], 1.0)
            pool.memset(S["mhalf"][:, :], -0.5)
            pool.memset(S["tri_le"][:, :], 1.0)
            pool.memset(S["tri_gt"][:, :], 1.0)
            pool.memset(S["tri_le2"][:, :], 1.0)
            pool.memset(S["tri_gt2"][:, :], 1.0)
            pool.memset(S["tailrow"][:, :], 0.0)
            pool.memset(S["seg8"][:, :], 1.0)
            pool.drain()
            pool.memset(S["tailrow"][64:80, :], 1.0)
            pool.drain()

            def keep(t, pattern, base, cm, fill=0.0, op=ALU.is_ge):
                pool.affine_select(out=t, in_=t, pattern=pattern, compare_op=op, fill=fill, base=base,
                                   channel_multiplier=cm)

            keep(S["ident"][:, :], [[-1, P]], 0, 1, fill=1.0, op=ALU.not_equal)
            keep(S["tri_le"][:, :], [[1, P]], 0, -1)
            keep(S["tri_gt"][:, :], [[-1, P]], -1, 1)
            keep(S["tri_le2"][:, :], [[1, 80]], 0, -1)
            keep(S["tri_gt2"][:, :], [[-1, 80]], -1, 1)
            keep(S["seg8"][:, :], [[-8, 8]], 0, 1)
            pool.drain()
            v8 = S["tri_le2"][:, 0:64].rearrange("k (s j) -> k s j", j=8)
            keep(v8, [[-8, 8], [0, 8]], 0, 1)
            keep(S["tri_le2"][:, 64:80], [[0, 16]], -64, 1)
            keep(S["tri_gt2"][:, 0:64].rearrange("k (s j) -> k s j", j=8), [[8, 8], [0, 8]], 7, -1)
            keep(S["seg8"][:, :], [[8, 8]], 7, -1)
            pool.drain()
            pool.memset(S["mask_d"][:, :], 0.0)
            pool.memset(S["mask_t"][:, :], 0.0)
            pool.drain()
            keep(S["mask_d"][:, 128:256], [[-1, P]], 0, 1, fill=NEG)
            pool.memset(S["mask_t"][:, 256:320], NEG)
            keep(S["mask_t"][:, 320:336], [[-1, 16]], 0, 1, fill=NEG)
            pool.memset(S["self01"][:, :, :], 1.0)
            pool.drain()
            m4 = S["self01"][:, :, :].rearrange("k s (h q) -> k s h q", q=8)
            keep(m4, [[8, 8], [0, 16], [1, 8]], 0, -1)
            pool.drain()
            keep(m4, [[-8, 8], [0, 16], [0, 8]], 0, 1)
            pool.drain()
            pool.memset(ss[:, 3:4], 1.0).then_inc(consts, 1)
            for t, r in enumerate(ROWS):
                pool.wait_ge(ssq, t + 1)
                pool.tensor_scalar(ss[0:r, t:t + 1], ss[0:r, t:t + 1], 1.0 / D, EPS, ALU.mult, ALU.add)
                pool.drain()
                pool.tensor_tensor(ss[0:r, t:t + 1], ss[0:r, t:t + 1], S["mhalf"][0:r, 0:1], ALU.pow).then_inc(rstd_ok, 1)

        @block.scalar
        def _(act):
            act.dma_start(rows64[0:32, :], A["conv_b"].rearrange("a (t p) -> (a t) p", p=P)).then_inc(par_in, 16)
            act.dma_start(rows64[32:48, :], A["ssd_norm_g"].rearrange("a (t p) -> (a t) p", p=P)).then_inc(par_in, 16)
            act.dma_start(rows64[48:56, :], A["norm1_g"].rearrange("a (t p) -> (a t) p", p=P)).then_inc(par_in, 16)
            act.dma_start(rows64[56:64, :], A["norm2_g"].rearrange("a (t p) -> (a t) p", p=P)).then_inc(par_in, 16)
            act.dma_start(convw_rows[:, :], A["conv_w"].rearrange("a w (t p) -> (a w t) p", p=P)).then_inc(par_in, 16)
            act.dma_start(sc_rows[:, :, :], A["state_conv"].rearrange("a s w (t p) -> (a s w t) p", p=P)
                          .rearrange("(r q) p -> q r p", q=P)).then_inc(par_in, 16)
            for i, (n, w) in enumerate((("dt_bias", 32), ("a_log", 32), ("d_skip", 32), ("b_forget", 16))):
                act.dma_start(brow[:, 32 * i:32 * i + w], A[n][0, :].partition_broadcast(P)).then_inc(par_in, 16)
            act.wait_ge(x_in, 80)
            for t, r in enumerate(ROWS):
                act.activation(xsq[0:r, :], S["xtok"][0:r, t, :], ACT.Square,
                               accum_out=ss[0:r, t:t + 1]).then_inc(ssq, 1)
                act.drain()
            act.wait_ge(par_in, 160)
            act.activation(a_neg[:, :], brow[:, 32:64], ACT.Exp).then_inc(ab_exp, 1)
            act.wait_ge(dtf_ev, 1)
            act.activation(sp_e[:, :, :], sp_z[:, :, :], ACT.Exp, scale=-1.0).then_inc(sp_exp, 1)
            act.wait_ge(dtf_ev, 2)
            act.activation(sp_l[:, :, :], sp_w[:, :, :], ACT.Ln).then_inc(sp_ln, 1)
            act.wait_ge(cum_ps, 1)
            for t, r in enumerate(ROWS):
                act.activation(S["eac"][0:r, t, :], ps[0][0:r, 32 * t:32 * t + 32], ACT.Exp)
                act.activation(S["w_end"][0:r, t, :], ps[1][0:r, 32 * t:32 * t + 32], ACT.Exp)
                act.activation(S["dec"][:, t, :], ps[2][:, 32 * t:32 * t + 32], ACT.Exp).then_inc(cum_ev, 1)
            act.wait_ge(cum_ps, 2)
            act.activation(S["dec_s"][:, :, :], ps[3][:, 0:128].rearrange("p (a s) -> p a s", s=8),
                           ACT.Exp).then_inc(cum_ev, 1)

        @block.vector
        def _(v):
            v.wait_ge(consts, 1)
            v.memset(small[:, :, :], 0.0).then_inc(consts, 1)
            for t, r in enumerate(ROWS):
                v.wait_ge(rstd_ok, t + 1)
                v.tensor_scalar(xn[0:r, t, :], S["xtok"][0:r, t, :], ss[0:r, t:t + 1], None,
                                ALU.mult).then_inc(xn_ok, 1)
            v.wait_ge(par_ps, 2)
            v.tensor_scalar(S["conv_bh"][:, :], ps[6][:, 0:32], 0.5, None, ALU.mult)
            v.tensor_copy(S["gcol"][:, :], ps[6][:, 32:64])
            v.tensor_scalar(S["conv_wh"][:, :, :], ps[6][:, 64:192].rearrange("p (w t) -> p w t", w=4), 0.5, None,
                            ALU.mult).then_inc(par_ev, 1)
            scv = S["sc_t"][:, :, :, :].rearrange("p s w t -> p (s w t)")
            v.tensor_copy(scv[:, 0:512], ps[7][:, :])
            v.tensor_copy(scv[:, 512:768], ps[6][:, 192:448]).then_inc(par_ev, 1)
            v.drain()
            for t, r in enumerate(ROWS):
                for h in range(2):
                    v.wait_ge(tr_ps, 2 * t + h + 1)
                    v.tensor_tensor(S["xnT"][:, 4 * h:4 * h + 4, COL[t]:COL[t] + r],
                                    ps[2 * (t % 2) + h][:, :].rearrange("p (k c) -> p k c", c=P)[:, :, 0:r],
                                    bc(S["gcol"][:, 16 + 4 * h:20 + 4 * h].unsqueeze(2), [P, 4, r]),
                                    ALU.mult).then_inc(tr_ev, 1)
            for t, r in enumerate(ROWS):
                v.wait_ge(kv_ps, t + 1)
                v.tensor_copy(S["k"][0:r, t, :], ps[4 + t][0:r, 0:256]).then_inc(kv_ev, 1)
                v.tensor_copy(S["v"][0:r, t, :], ps[4 + t][0:r, 256:512]).then_inc(kv_ev, 1)
            v.wait_ge(dt_ps, 1)
            v.wait_ge(par_in, 160)
            for t, r in enumerate(ROWS):
                v.tensor_tensor(small[0:r, t, 0:32], ps[0][0:r, 64 * t:64 * t + 32], brow[0:r, 0:32], ALU.add)
                v.tensor_tensor(small[0:r, t, 32:48], ps[0][0:r, 64 * t + 32:64 * t + 48], brow[0:r, 96:112], ALU.add)
            v.drain()
            v.tensor_scalar(small[:, :, 32:48], small[:, :, 32:48], -1.0, None, ALU.mult)
            v.drain()
            v.scalar_tensor_tensor(sp_z[:, :, :], small[:, :, :], -1.0, small[:, :, :], ALU.mult,
                                   ALU.max).then_inc(dtf_ev, 1)
            v.wait_ge(sp_exp, 1)
            v.tensor_scalar(sp_w[:, :, :], sp_e[:, :, :], 1.0, None, ALU.add).then_inc(dtf_ev, 1)
            v.drain()
            v.tensor_scalar(sp_d[:, :, :], sp_w[:, :, :], 1.0, 1e-30, ALU.subtract, ALU.max)
            v.drain()
            v.reciprocal(sp_d[:, :, :], sp_d[:, :, :])
            v.tensor_scalar(sp_z[:, :, :], sp_w[:, :, :], 1.0, None, ALU.is_equal)
            v.drain()
            v.wait_ge(sp_ln, 1)
            v.tensor_tensor(sp_l[:, :, :], sp_l[:, :, :], sp_d[:, :, :], ALU.mult)
            v.drain()
            v.tensor_tensor(sp_l[:, :, :], sp_l[:, :, :], sp_z[:, :, :], ALU.add)
            v.drain()
            v.tensor_tensor(sp_l[:, :, :], sp_l[:, :, :], sp_e[:, :, :], ALU.mult)
            v.tensor_scalar(small[:, :, :], small[:, :, :], 0.0, None, ALU.max)
            v.drain()
            v.tensor_tensor(small[:, :, :], small[:, :, :], sp_l[:, :, :], ALU.add)
            v.drain()
            v.tensor_scalar(S["lf"][:, :, :], small[:, :, 32:48], -1.0, None, ALU.mult).then_inc(dt_ok, 1)
            v.tensor_copy(S["dt"][:, :, :], small[:, :, 0:32])
            v.tensor_copy(S["dskip"][:, :], brow[:, 64:96])
            v.wait_ge(ab_exp, 1)
            v.scalar_tensor_tensor(S["dta"][:, :, :], small[:, :, 0:32], -1.0,
                                   bc(a_neg[:, :].unsqueeze(1), [P, 3, 32]), ALU.mult, ALU.mult)
            v.drain()
            v.tensor_copy(dta_rep[:, :, :], bc(S["dta"][0:NS, 2, :].unsqueeze(2), [NS, NH, HP])).then_inc(dt_ok, 1)
            v.wait_ge(cum_ps, 3)
            v.tensor_copy(S["c_q"][:, 0:2, :], ps[7][:, 128:160].rearrange("p (t h) -> p t h", t=2))
            v.tensor_copy(S["c_q"][0:16, 2, :], ps[7][0:16, 160:176])
            v.tensor_scalar(S["ncT"][:, :], ps[4][0:16, 0:336], -1.0, None, ALU.mult)
            v.tensor_copy(S["lf_rep"][:, :, :], bc(S["lf"][0:64, 2, :].unsqueeze(2), [64, 16, 8]))
            v.wait_ge(kt_ps, 1)
            for p in range(2):
                v.tensor_copy(S["kT"][:, p, :], ps[5 + p][:, 0:336])
            v.wait_ge(cum_ev, 3)
            for t, r in enumerate(ROWS):
                v.tensor_tensor(S["w_end"][0:r, t, :], S["w_end"][0:r, t, :], S["dt"][0:r, t, :], ALU.mult)

        @block.tensor
        def _(pe):
            pe.wait_ge(consts, 1)
            pe.wait_ge(par_in, 160)
            pe.transpose(ps[6][:, 0:64], rows64[:, :], S["ident"][0:64, 0:64])
            pe.transpose(ps[6][:, 64:192], convw_rows[:, :], S["ident"][:, :]).then_inc(par_ps, 1)
            for i in range(6):
                o = ps[7][:, P * i:P * i + P] if i < 4 else ps[6][:, 192 + P * (i - 4):320 + P * (i - 4)]
                mm = pe.transpose(o, sc_rows[:, i, :], S["ident"][:, :])
            mm.then_inc(par_ps, 1)
            for t, r in enumerate(ROWS):
                pe.wait_ge(xn_ok, t + 1)
                if t == 2:
                    pe.wait_ge(tr_ev, 2)
                for h in range(2):
                    for k in range(4):
                        mm = pe.transpose(ps[2 * (t % 2) + h][:, P * k:P * k + r],
                                          xn[0:r, t, P * (4 * h + k):P * (4 * h + k + 1)], S["ident"][0:r, 0:r])
                    mm.then_inc(tr_ps, 1)
            pe.wait_ge(w_in_ready, 32)
            pe.wait_ge(tr_ev, 6)
            pe.wait_ge(par_ev, 2)
            for t, r in enumerate(ROWS):
                for k in range(KT):
                    mm = pe.matmul(ps[4 + t][0:r, :], S["xnT"][:, k, COL[t]:COL[t] + r], w_kvf[:, k, 0:512],
                                   start=(k == 0), stop=(k == KT - 1))
                mm.then_inc(kv_ps, 1)
                for w, c0, c1 in ((w_dt, 0, 32), (w_kvf, 512, 528)):
                    o = 64 * t + (0 if w is w_dt else 32)
                    for k in range(KT):
                        mm = pe.matmul(ps[0][0:r, o:o + c1 - c0], S["xnT"][:, k, COL[t]:COL[t] + r],
                                       w[:, k, c0:c1], start=(k == 0), stop=(k == KT - 1))
            mm.then_inc(dt_ps, 1)
            pe.wait_ge(dt_ok, 2)
            le = [S["tri_le"], S["tri_le"], S["tri_le2"]]
            gt = [S["tri_gt"], S["tri_gt"], S["tri_gt2"]]
            tot = [S["ones"], S["ones"], S["tailrow"]]
            for t, r in enumerate(ROWS):
                da = S["dta"][0:r, t, :]
                pe.matmul(ps[0][0:r, 32 * t:32 * t + 32], le[t][0:r, 0:r], da, start=True, stop=True)
                pe.matmul(ps[1][0:r, 32 * t:32 * t + 32], gt[t][0:r, 0:r], da, start=True, stop=True)
                mm = pe.matmul(ps[2][:, 32 * t:32 * t + 32], tot[t][0:r, :], da, start=True, stop=True)
            mm.then_inc(cum_ps, 1)
            for a in range(16):
                mm = pe.matmul(ps[3][:, 8 * a:8 * a + 8], dta_rep[:, 2 * a:2 * a + 2, :], S["seg8"][:, :],
                               start=True, stop=True)
            mm.then_inc(cum_ps, 1)
            lf = S["lf"]
            o = ps[7]
            pe.matmul(o[:, 128:144], S["tri_le"][:, :], lf[:, 0, :], start=True, stop=True)
            pe.matmul(o[:, 144:160], S["ones"][:, :], lf[:, 0, :], start=True, stop=False)
            pe.matmul(o[:, 144:160], S["tri_le"][:, :], lf[:, 1, :], start=False, stop=True)
            pe.matmul(o[0:16, 160:176], S["ones"][:, 0:16], lf[:, 0, :], start=True, stop=False)
            pe.matmul(o[0:16, 160:176], S["ones"][:, 0:16], lf[:, 1, :], start=False, stop=False)
            pe.matmul(o[0:16, 160:176], S["tri_le2"][:, 64:80], lf[0:80, 2, :], start=False, stop=True)
            pe.wait_ge(kv_ev, 2)
            o = ps[4][0:16, :]
            pe.matmul(o[:, 0:128], lf[:, 0, :], S["tri_le"][:, :], start=True, stop=True)
            pe.matmul(o[:, 128:256], lf[:, 0, :], S["ones"][:, :], start=True, stop=False)
            pe.matmul(o[:, 128:256], lf[:, 1, :], S["tri_le"][:, :], start=False, stop=True)
            pe.matmul(o[:, 256:336], lf[:, 0, :], S["ones"][:, 0:80], start=True, stop=False)
            pe.matmul(o[:, 256:336], lf[:, 1, :], S["ones"][:, 0:80], start=False, stop=False)
            pe.matmul(o[:, 256:336], lf[0:80, 2, :], S["tri_le2"][:, :], start=False, stop=True).then_inc(cum_ps, 1)
            pe.wait_ge(kv_ev, 6)
            for p in range(2):
                for t, r in enumerate(ROWS):
                    mm = pe.transpose(ps[5 + p][:, COL[t]:COL[t] + r], S["k"][0:r, t, P * p:P * p + P],
                                      S["ident"][0:r, 0:r])
            mm.then_inc(kt_ps, 1)


def ssd_phase(nc, A, S, sem):
    with ExitStack() as ctx:
        def tsb(name, shape, dt=F32):
            return ctx.enter_context(nc.sbuf_tensor(name, shape, dt))

        wg = tsb("w_group", [P, KT, 768])
        zt, zz = tsb("z_tanh", [P, 3, 256]), tsb("z_gate", [P, 3, 256])
        xp = tsb("x_padded", [P, 4, 363])
        xc, xt = tsb("x_conv", [P, 4, 360]), tsb("x_tanh", [P, 4, 360])
        xs = tsb("x_silu", [P, 4, 360])
        xs2 = tsb("x_tile2", [P, 4, 80])
        tok = tsb("x_b_rows", [P, 3, 384])
        h0 = tsb("h0", [P, 2, NSEQ, N])
        h0t = tsb("h0_t", [P, NSEQ, 256])
        cx = tsb("c_spread", [P, 9, 80])
        r4, e4 = tsb("dta_tri", [P, 3, 512]), tsb("decay", [P, 3, 512])
        cbm = tsb("cb_masked", [P, 3, P])
        xdt, xw, dx = tsb("x_dt", [P, 3, 256]), tsb("x_wend", [P, 3, 256]), tsb("x_skip", [P, 3, 256])
        bm = tsb("b_by_seq", [NS, NSEQ, N])
        hp = tsb("h_prompt", [P, 3, 256])
        hpo = tsb("h_prompt_out", [P, 2, N])
        hso = tsb("h_sample_out", [P, 2, NSEQ, N])
        yo, y = tsb("y_off", [P, 3, 256]), tsb("y_rows", [P, 3, 256])
        ysq, yss, cv_p, cv_s = (tsb("y_sq", [P, 256]), tsb("y_ss", [P, 3]), tsb("conv_p_t", [P, 3, 32]),
                                tsb("conv_s_t", [P, NSEQ, 3, 32]))
        cvo = xt[:, :, :].rearrange("p m c -> p (m c)")[:, 0:7 * P].rearrange("p (a n) -> p a n", n=P)
        ps = [ctx.enter_context(nc.psum_tensor(f"psg{i}", [P, 512], F32)) for i in range(8)]
        wf_in, wz_in, h0_in = sem("w_channels_in"), sem("w_z_in"), sem("h0_in")
        z_ps, z_th, z_ev, f_ps, f_ev, f_pad, tap0, taps, f_th, silu, compact = (
            sem(n) for n in ("z_ps", "z_th", "z_ev", "f_ps", "f_ev", "f_pad", "tap0", "taps", "f_th", "silu",
                             "compact"))
        tok_ps, tok_ev, r4_ok, seg_ps, e4_ok, cb_ps, cbm_ok, m_ok, x_ok, b_ok = (
            sem(n) for n in ("tok_ps", "tok_ev", "r4_ok", "seg_ps", "e4_ok", "cb_ps", "cbm_ok", "m_ok", "x_ok",
                             "b_ok"))
        ht_ps, ht_ev, st_ps, hp_ok, y_ps, y_raw, y_sqd, y_rs, y_n, yt_ps, yt_ev = (
            sem(n) for n in ("ht_ps", "ht_ev", "st_ps", "hp_ok", "y_ps", "y_raw", "y_sqd", "y_rs", "y_n", "yt_ps",
                             "yt_ev"))
        hs_ps, hs_ev, hf_ps, hf_ev, states_sent, cv_ps, cv_ev, cv_sent = (
            sem(n) for n in ("hs_ps", "hs_ev", "hf_ps", "hf_ev", "states_sent", "cv_ps", "cv_ev", "cv_sent"))
        pool_passed = S["pool_passed"]
        zero_ok, h0_used = sem("zero_ok"), sem("h0_used")
        win = A["w_in"].rearrange("a (t p) c -> p (a t) c", p=P)
        ssm_in = A["state_ssm"].rearrange("a s h p n -> (a s) (h p) n")
        ssm_s = A["ssm_s"].rearrange("a s h p n -> (a s) (h p) n")
        ssm_p = A["ssm_p"].rearrange("a b h p n -> (a b h p) n")
        le = [S["tri_le"], S["tri_le"], S["tri_le2"]]
        gt = [S["tri_gt"], S["tri_gt"], S["tri_gt2"]]
        block = ctx.enter_context(nc.Block())

        def tile_of(g, m):
            return [2 * g, 2 * g + 1, 16 + g, 24 + g][m]

        @block.sync
        def _(sp):
            sp.sem_inc(states_sent, 48)

            def load_w(g):
                for d, c, w in ((0, C_X, 256), (256, C_B, 128), (384, C_C, 128)):
                    sp.dma_start(wg[:, :, d:d + w], win[:, :, bass.ds(g * w + c, w)]).then_inc(wf_in, 16)

            def load_wz(g):
                sp.dma_start(wg[:, :, 512:768], win[:, :, bass.ds(g * 256 + C_Z, 256)]).then_inc(wz_in, 16)

            def load_h(g):
                for a in range(2):
                    sp.dma_start(h0[:, a, :, :], ssm_in[:, bass.ds(g * 256 + a * P, P), :]
                                 .rearrange("s q n -> q s n")).then_inc(h0_in, 16)

            def send_h(g):
                sp.wait_ge(hs_ev, 2 * g + 4)
                for a in range(2):
                    sp.dma_start(ssm_s[:, bass.ds(g * 256 + a * P, P), :].rearrange("s q n -> q s n"),
                                 hso[:, a, :, :]).then_inc(states_sent, 16)
                sp.dma_start(ssm_p[bass.ds(g * 256, 256), :].rearrange("(a q) n -> q a n", q=P),
                             hpo[:, :, :]).then_inc(states_sent, 16)

            load_w(0)
            load_wz(0)
            load_h(0)
            with sp.Fori(1, G) as g:
                sp.wait_ge(f_ps, 4 * g)
                load_w(g)
                sp.wait_ge(z_ps, 3 * g)
                sp.sem_inc(pool_passed)
                load_wz(g)
                sp.wait_ge(hs_ev, 2 * g + 2)
                load_h(g)
                send_h(g - 1)
            send_h(G - 1)
            sp.wait_ge(cv_ev, 2)
            sp.dma_start(A["conv_p"].rearrange("a b w (t p) -> (a b w t) p", p=P), cvo[0:96, 6, :]).then_inc(cv_sent, 16)
            sp.dma_start(A["conv_s"].rearrange("a b w (t p) -> (a b w t) p", p=P)
                         .rearrange("(r q) p -> q r p", q=P), cvo[:, 0:6, :]).then_inc(cv_sent, 16)
            sp.wait_ge(cv_sent, 32)
            sp.wait_ge(states_sent, 48 * (G + 1))
            sp.wait_ge(wf_in, 48 * G)
            sp.wait_ge(wz_in, 16 * G)
            sp.wait_ge(h0_in, 32 * G)

        @block.gpsimd
        def _(pool):
            pool.memset(xp[:, :, 0:3], 0.0)
            pool.memset(cx[:, :, :], 0.0)
            pool.memset(hp[:, 0, :], 0.0)
            pool.drain()
            pool.memset(yss[:, :], 1.0).then_inc(zero_ok, 1)
            with pool.Fori(0, G) as g:
                for t, r in enumerate(ROWS):
                    pool.tensor_tensor(r4[0:r, t, :].rearrange("k (h i) -> k h i", h=4)[:, :, 0:r],
                                       bc(le[t][0:r, 0:r].unsqueeze(1), [r, 4, r]),
                                       bc(S["dta"][0:r, t, bass.ds(4 * g, 4)].unsqueeze(2), [r, 4, r]),
                                       ALU.mult).then_inc(r4_ok, 1)
                for m in range(4):
                    pool.tensor_copy(xp[:, m, 275:363].rearrange("p (s w) -> p s w", w=11)[:, :, 0:3],
                                     S["sc_t"][:, :, :, bass.ds(tile_of(g, m), 1)]
                                     .rearrange("p s w o -> p s (w o)")).then_inc(f_pad, 1)
                pool.wait_ge(f_ev, 4 * g + 4)
                pool.sem_inc(pool_passed)
                for m in range(4):
                    o = tile_of(g, m)
                    pool.tensor_copy(cv_p[:, :, bass.ds(o, 1)].rearrange("p w o -> p (w o)"), xp[:, m, 272:275])
                    pool.tensor_copy(cv_s[:, :, :, bass.ds(o, 1)].rearrange("p s w o -> p s (w o)"),
                                     xp[:, m, 275:363].rearrange("p (s w) -> p s w", w=11)[:, :, 8:11])
                pool.wait_ge(silu, g + 1)
                pool.sem_inc(pool_passed)
                pool.tensor_copy(xs2[:, :, 0:64].rearrange("p m (s j) -> p m s j", j=8),
                                 gapped(xs))
                pool.tensor_copy(xs2[:, :, 64:80], xs[:, :, 256:272]).then_inc(compact, 1)
                pool.drain()
                pool.tensor_copy(diag8(cx), xs2[:, 3, 0:64].rearrange("n (s j) -> n s j", j=8))
                pool.tensor_copy(cx[:, 8, 64:80], xs2[:, 3, 64:80]).then_inc(compact, 1)
                for t, r in enumerate(ROWS):
                    pool.wait_ge(tok_ev, 3 * g + t + 1)
                    x4 = tok[0:r, t, 0:256].rearrange("k (h p) -> k h p", h=4)
                    for dst, by in ((xdt, S["dt"][0:r, t, bass.ds(4 * g, 4)]),
                                    (xw, S["w_end"][0:r, t, bass.ds(4 * g, 4)]),
                                    (dx, S["dskip"][0:r, bass.ds(4 * g, 4)])):
                        i = pool.tensor_tensor(dst[0:r, t, :].rearrange("k (h p) -> k h p", h=4), x4,
                                               bc(by.unsqueeze(2), [r, 4, HP]), ALU.mult)
                    i.then_inc(x_ok, 1)
                pool.tensor_tensor(bm[:, :, :], bc(tok[0:64, 2, 256:384].unsqueeze(1), [NS, NSEQ, N]),
                                   bc(S["seg8"][:, :].unsqueeze(2), [NS, NSEQ, N]), ALU.mult).then_inc(b_ok, 1)
                for t, r in enumerate(ROWS):
                    pool.wait_ge(y_sqd, 3 * g + t + 1)
                    pool.sem_inc(pool_passed)
                    pool.tensor_scalar(yss[0:r, t:t + 1], yss[0:r, t:t + 1], 1.0 / 256, EPS, ALU.mult, ALU.add)
                    pool.drain()
                    pool.tensor_tensor(yss[0:r, t:t + 1], yss[0:r, t:t + 1], S["mhalf"][0:r, 0:1],
                                       ALU.pow).then_inc(y_rs, 1)

        @block.scalar
        def _(act):
            act.wait_ge(zero_ok, 1)

            def channels_out(g):
                for m in range(4):
                    act.wait_ge(f_ps, 4 * g + m + 1)
                    act.activation(xp[:, m, 3:259], ps[m][:, 0:256], ACT.Copy)
                    act.activation(xp[:, m, 259:275], ps[m][:, 320:336], ACT.Copy)
                    act.activation(xp[:, m, 275:363].rearrange("p (s w) -> p s w", w=11)[:, :, 3:11],
                                   ps[m][:, 256:320].rearrange("p (s j) -> p s j", j=8), ACT.Copy).then_inc(f_ev, 1)
                    act.drain()
                    act.wait_ge(f_pad, 4 * g + m + 1)
                    o = tile_of(g, m)
                    act.activation(xc[:, m, :], xp[:, m, 0:360], ACT.Identity,
                                   bias=S["conv_bh"][:, bass.ds(o, 1)],
                                   scale=S["conv_wh"][:, 0, bass.ds(o, 1)]).then_inc(tap0, 1)

            def chunks(g):
                act.wait_ge(taps, 4 * g + 4)
                act.activation(xt[:, :, :], xc[:, :, :], ACT.Tanh).then_inc(f_th, 1)
                for t, r in enumerate(ROWS):
                    act.wait_ge(z_ps, 3 * g + max(t + 1, 2))
                    src = ps[4 + t // 2][0:r, 256 * (t % 2):256 * (t % 2) + 256]
                    act.activation(zt[0:r, t, :], src, ACT.Tanh, scale=0.5).then_inc(z_th, 1)
                for t, r in enumerate(ROWS):
                    act.wait_ge(tok_ps, 3 * g + t + 1)
                    act.activation(tok[0:r, t, :], ps[t][0:r, 0:384], ACT.Copy).then_inc(tok_ev, 1)
                for t, r in enumerate(ROWS):
                    act.wait_ge(seg_ps, 3 * g + t + 1)
                    act.activation(e4[0:r, t, :].rearrange("k (h i) -> k h i", h=4)[:, :, 0:r],
                                   ps[4 + t][0:r, 0:4 * r].rearrange("k (h i) -> k h i", h=4),
                                   ACT.Exp).then_inc(e4_ok, 1)
                for b in range(4):
                    act.wait_ge(ht_ps, 4 * g + b + 1)
                    act.activation(h0t[:, 2 * b:2 * b + 2, :], ps[(b + 3) % 4][:, :], ACT.Copy).then_inc(ht_ev, 1)
                for t, r in enumerate(ROWS):
                    act.wait_ge(y_raw, 3 * g + t + 1)
                    act.activation(ysq[0:r, :], y[0:r, t, :], ACT.Square,
                                   accum_out=yss[0:r, t:t + 1]).then_inc(y_sqd, 1)
                    act.drain()

            def y_out(g):
                for h in range(2):
                    act.wait_ge(yt_ps, 2 * g + h + 1)
                    act.activation(S["yT"][:, bass.ds(2 * g + h, 1), :], ps[6 + h][:, 0:T].unsqueeze(1), ACT.Identity,
                                   scale=S["gcol"][:, bass.ds(2 * g + h, 1)]).then_inc(yt_ev, 1)

            channels_out(0)
            with act.Fori(0, G - 1) as g:
                chunks(g)
                channels_out(g + 1)
                y_out(g)
            chunks(G - 1)
            y_out(G - 1)

        @block.vector
        def _(v):
            v.sem_inc(hs_ev, 2)
            v.wait_ge(zero_ok, 1)
            with v.Fori(0, G) as g:
                for m in range(4):
                    o = tile_of(g, m)
                    v.wait_ge(tap0, 4 * g + m + 1)
                    for w in range(1, 4):
                        i = v.scalar_tensor_tensor(xc[:, m, :], xp[:, m, w:w + 360],
                                                   S["conv_wh"][:, w, bass.ds(o, 1)], xc[:, m, :], ALU.mult, ALU.add)
                        if w == 3:
                            i.then_inc(taps, 1)
                        v.drain()
                v.wait_ge(f_th, g + 1)
                v.scalar_tensor_tensor(xs[:, :, :], xt[:, :, :], 1.0, xc[:, :, :], ALU.add, ALU.mult).then_inc(silu, 1)
                for t, r in enumerate(ROWS):
                    v.wait_ge(z_th, 3 * g + max(t + 1, 2))
                    src = ps[4 + t // 2][0:r, 256 * (t % 2):256 * (t % 2) + 256]
                    v.scalar_tensor_tensor(zz[0:r, t, :], zt[0:r, t, :], 1.0, src, ALU.add,
                                           ALU.mult).then_inc(z_ev, 1)
                for t, r in enumerate(ROWS):
                    v.wait_ge(cb_ps, 3 * g + 3)
                    v.tensor_tensor(cbm[0:r, t, 0:r], ps[7][0:r, P * t:P * t + r], le[t][0:r, 0:r],
                                    ALU.mult).then_inc(cbm_ok, 1)
                v.drain()
                for t, r in enumerate(ROWS):
                    v.wait_ge(e4_ok, 3 * g + t + 1)
                    e = e4[0:r, t, :].rearrange("k (h i) -> k h i", h=4)[:, :, 0:r]
                    v.tensor_tensor(e, e, bc(cbm[0:r, t, 0:r].unsqueeze(1), [r, 4, r]), ALU.mult).then_inc(m_ok, 1)
                for t in range(3):
                    v.wait_ge(st_ps, 3 * g + max(t + 1, 2))
                    src = ps[7][:, 256 * t:256 * t + 256] if t < 2 else ps[3][:, 0:256]
                    if t == 0:
                        v.tensor_copy(hp[:, 0, :], src).then_inc(hp_ok, 1)
                        v.drain()
                    else:
                        v.tensor_tensor(hp[:, t, :].rearrange("n (h p) -> n h p", h=4),
                                        hp[:, t - 1, :].rearrange("n (h p) -> n h p", h=4),
                                        bc(S["dec"][:, t, bass.ds(4 * g, 4)].unsqueeze(2), [P, 4, HP]), ALU.mult)
                        v.drain()
                        v.tensor_tensor(hp[:, t, :], hp[:, t, :], src, ALU.add).then_inc(hp_ok, 1)
                        v.drain()
                for t, r in enumerate(ROWS):
                    v.wait_ge(y_ps, 3 * g + t + 1)
                    if t == 0:
                        v.tensor_tensor(y[0:r, t, :], ps[4 + t][0:r, 0:256], dx[0:r, t, :], ALU.add)
                    else:
                        v.tensor_tensor(yo[0:r, t, :].rearrange("k (h p) -> k h p", h=4),
                                        ps[4 + t][0:r, 256:512].rearrange("k (h p) -> k h p", h=4),
                                        bc(S["eac"][0:r, t, bass.ds(4 * g, 4)].unsqueeze(2), [r, 4, HP]), ALU.mult)
                        v.drain()
                        v.tensor_tensor(y[0:r, t, :], ps[4 + t][0:r, 0:256], yo[0:r, t, :], ALU.add)
                        v.drain()
                        v.tensor_tensor(y[0:r, t, :], y[0:r, t, :], dx[0:r, t, :], ALU.add)
                    v.drain()
                    v.scalar_tensor_tensor(y[0:r, t, :], y[0:r, t, :], 0.5, zz[0:r, t, :], ALU.mult,
                                           ALU.mult).then_inc(y_raw, 1)
                v.wait_ge(h0_in, 32 * g + 32)
                v.wait_ge(states_sent, 48 * g + 48)
                v.wait_ge(hf_ps, g + 1)
                v.tensor_copy(hpo[:, :, :], ps[3][:, 256:512].rearrange("p (a n) -> p a n", a=2)).then_inc(hf_ev, 1)
                for a in range(2):
                    v.tensor_tensor(hso[:, a, :, :], h0[:, a, :, :],
                                    bc(S["dec_s"][:, bass.ds(2 * g + a, 1), :].rearrange("p o s -> p (o s)")
                                       .unsqueeze(2), [P, NSEQ, N]), ALU.mult)
                    v.drain()
                    for b in range(2):
                        v.wait_ge(hs_ps, 4 * g + 2 * a + b + 1)
                        i = v.tensor_tensor(hso[:, a, 4 * b:4 * b + 4, :], hso[:, a, 4 * b:4 * b + 4, :],
                                            ps[(2 * a + b)][:, :].rearrange("p (s n) -> p s n", n=N), ALU.add)
                    i.then_inc(hs_ev, 1)
                for t, r in enumerate(ROWS):
                    v.wait_ge(y_rs, 3 * g + t + 1)
                    v.tensor_scalar(y[0:r, t, :], y[0:r, t, :], yss[0:r, t:t + 1], None, ALU.mult).then_inc(y_n, 1)
            v.wait_ge(cv_ps, 1)
            v.tensor_copy(cvo[:, 0:4, :], ps[0][:, :].rearrange("p (a n) -> p a n", n=P)).then_inc(cv_ev, 1)
            v.tensor_copy(cvo[:, 4:6, :], ps[1][:, 0:256].rearrange("p (a n) -> p a n", n=P))
            v.tensor_copy(cvo[0:96, 6, :], ps[1][0:96, 256:384]).then_inc(cv_ev, 1)

        @block.tensor
        def _(pe):
            idn = S["ident"]

            def channels(g):
                pe.wait_ge(wf_in, 48 * g + 48)
                for m in range(4):
                    if m % 2 == 0:
                        pe.wait_ge(hs_ev, 2 * g + m // 2 + 1)
                    for k in range(KT):
                        mm = pe.matmul(ps[m][:, 0:T], wg[:, k, P * m:P * m + P], S["xnT"][:, k, :],
                                       start=(k == 0), stop=(k == KT - 1))
                    mm.then_inc(f_ps, 1)

            def chunks(g):
                pe.wait_ge(wz_in, 16 * g + 16)
                for t, r in enumerate(ROWS):
                    for k in range(KT):
                        mm = pe.matmul(ps[4 + t // 2][0:r, 256 * (t % 2):256 * (t % 2) + 256],
                                       S["xnT"][:, k, COL[t]:COL[t] + r], wg[:, k, 512:768],
                                       start=(k == 0), stop=(k == KT - 1))
                    mm.then_inc(z_ps, 1)
                pe.wait_ge(f_ev, 4 * g + 4)
                pe.wait_ge(silu, g + 1)
                for t, r in enumerate(ROWS):
                    if t == 2:
                        pe.wait_ge(compact, 2 * g + 1)
                    for m in range(3):
                        src = xs[:, m, COL[t]:COL[t] + r] if t < 2 else xs2[:, m, :]
                        mm = pe.transpose(ps[t][0:r, P * m:P * m + P], src, idn[:, :])
                    mm.then_inc(tok_ps, 1)
                for t, r in enumerate(ROWS):
                    b_, c_ = ((xs[:, m, COL[t]:COL[t] + r] if t < 2 else xs2[:, m, :]) for m in (2, 3))
                    mm = pe.matmul(ps[7][0:r, P * t:P * t + r], b_, c_, start=True, stop=True)
                    mm.then_inc(cb_ps, 1)
                pe.wait_ge(z_ev, 3 * g + 3)
                for t, r in enumerate(ROWS):
                    pe.wait_ge(r4_ok, 3 * g + t + 1)
                    pe.matmul(ps[4 + t][0:r, 0:4 * r], gt[t][0:r, 0:r],
                              r4[0:r, t, :].rearrange("k (h i) -> k h i", h=4)[:, :, 0:r],
                              start=True, stop=True).then_inc(seg_ps, 1)
                pe.wait_ge(h0_in, 32 * g + 32)
                for b in range(4):
                    if b:
                        pe.wait_ge(tok_ev, 3 * g + b)
                    for s in (2 * b, 2 * b + 1):
                        for a in range(2):
                            o = 256 * (s % 2) + P * a
                            mm = pe.transpose(ps[(b + 3) % 4][:, o:o + P], h0[:, a, s, :], idn[:, :])
                    mm.then_inc(ht_ps, 1)
                pe.wait_ge(cbm_ok, 3 * g + 3)
                pe.wait_ge(ht_ev, 4 * g + 1)
                for t, r in enumerate(ROWS):
                    pe.wait_ge(x_ok, 3 * g + t + 1)
                    k0 = 64 if t == 2 else 0
                    o = ps[7][:, 256 * t:256 * t + 256] if t < 2 else ps[3][:, 0:256]
                    pe.matmul(o, tok[k0:r, t, 256:384], xw[k0:r, t, :], start=True, stop=True).then_inc(st_ps, 1)
                for t, r in enumerate(ROWS):
                    pe.wait_ge(m_ok, 3 * g + t + 1)
                    for h in range(4):
                        mm = pe.matmul(ps[4 + t][0:r, HP * h:HP * h + HP], e4[0:r, t, P * h:P * h + r],
                                       xdt[0:r, t, HP * h:HP * h + HP], start=True, stop=True)
                    if t == 1:
                        pe.wait_ge(hp_ok, 3 * g + 1)
                        mm = pe.matmul(ps[5][:, 256:512], xs[:, 3, P:2 * P], hp[:, 0, :], start=True, stop=True)
                    if t == 2:
                        pe.wait_ge(compact, 2 * g + 2)
                        pe.wait_ge(hp_ok, 3 * g + 2)
                        pe.wait_ge(ht_ev, 4 * g + 4)
                        pe.matmul(ps[6][0:80, 256:512], cx[:, 8, :], hp[:, 1, :], start=True, stop=False)
                        for s in range(NSEQ):
                            mm = pe.matmul(ps[6][0:80, 256:512], cx[:, s, :], h0t[:, s, :], start=False,
                                           stop=(s == NSEQ - 1))
                    mm.then_inc(y_ps, 1)
                pe.wait_ge(hp_ok, 3 * g + 3)
                for a in range(2):
                    mm = pe.transpose(ps[3][:, 256 + P * a:256 + P * a + P], hp[:, 2, P * a:P * a + P], idn[:, :])
                mm.then_inc(hf_ps, 1)
                pe.wait_ge(b_ok, g + 1)
                for a in range(2):
                    for b in range(2):
                        if 2 * a + b == 3:
                            pe.wait_ge(hf_ev, g + 1)
                        pe.matmul(ps[2 * a + b][:, :], xw[0:64, 2, P * a:P * a + P], bm[:, 4 * b:4 * b + 4, :],
                                  start=True, stop=True).then_inc(hs_ps, 1)

            def turn_y(g):
                for h in range(2):
                    for t, r in enumerate(ROWS):
                        pe.wait_ge(y_n, 3 * g + t + 1)
                        mm = pe.transpose(ps[6 + h][:, COL[t]:COL[t] + r], y[0:r, t, P * h:P * h + P],
                                          idn[0:r, 0:r])
                    mm.then_inc(yt_ps, 1)

            channels(0)
            with pe.Fori(0, G - 1) as g:
                chunks(g)
                channels(g + 1)
                turn_y(g)
            chunks(G - 1)
            turn_y(G - 1)
            pe.wait_ge(yt_ev, 2 * G)
            for i in range(6):
                o = ps[i // 4][:, P * (i % 4):P * (i % 4) + P]
                pe.transpose(o, cv_s[:, :, :, :].rearrange("p s w t -> p (s w t)")[:, P * i:P * i + P], idn[:, :])
            pe.transpose(ps[1][0:96, 256:384], cv_p[:, :, :].rearrange("p w t -> p (w t)"),
                         idn[:, :]).then_inc(cv_ps, 1)


def gapped(xs):
    return xs[:, :, 272:360].rearrange("p m (s w) -> p m s w", w=11)[:, :, :, 3:11]


def diag8(cx):
    return cx[:, :, :].rearrange("n s c -> n (s c)")[:, 0:704].rearrange("n (s q) -> n s q", q=88)[:, :, 0:8]


def attention_phase(nc, A, S, sem):
    with ExitStack() as ctx:
        def tsb(name, shape, dt=F32):
            return ctx.enter_context(nc.sbuf_tensor(name, shape, dt))

        wq = tsb("w_q", [P, KT, 2, HD])
        qpad = tsb("q_pad", [P, 2, T])
        qblk = tsb("q_blocks", [P, NSEQ, 2, P])
        ncm = tsb("neg_c_head", [16, 2, T])
        sc = tsb("scores", [P, 2, 3, T])
        nm, rs = tsb("neg_max", [P, 6]), tsb("row_sum", [P, 6])
        pt01, pt2 = tsb("p_t", [P, 2, 384]), tsb("p_t_tail", [P, 2, 48])
        orow = tsb("o_rows", [P, 3, P])
        ptab = tsb("page_table", [1, NSEQ * NPG], I32)
        lfp = tsb("logf_pages", [P, NPG, NSEQ, 16])
        rall = tsb("r_past", [P, PAST])
        kpg, vpg = tsb("k_pages", [P, 2, NPG, 256]), tsb("v_pages", [P, 2, NPG, 256])
        kts = tsb("k_pages_t", [P, 2, PAST])
        selfneg = tsb("self_neg", [NS, NSEQ, P])
        ntri = tsb("neg_tri2", [NS, NS])
        qcur, mcur, scur, lcur = (tsb("q_cur", [P, 2, P]), tsb("mask_cur", [NS, P]), tsb("sel_cur", [P, P]),
                                  tsb("lf_cur", [NS, P]))
        pr = tsb("p_rows", [P, PAST + NS])
        pts, ptself = tsb("p_pages_t", [P, NPG, P]), tsb("p_self_t", [NS, P])
        mx, sm = tsb("maxes", [P, 8]), tsb("sums", [P, 4])
        oe = tsb("o_seq", [P, P])
        ps = [ctx.enter_context(nc.psum_tensor(f"psa{i}", [P, 512], F32)) for i in range(4)]
        psc = ctx.enter_context(nc.psum_tensor("psa_s", [P, 2, 512], F32))
        ps += [psc[:, 0, :], psc[:, 1, :]]
        ps += [ctx.enter_context(nc.psum_tensor(f"psa{i}", [P, 512], F32)) for i in (6, 7)]
        (wq_in, tab_in, lf_in, q_ps, q_ev, q_blk, ncm_ok, s_ps, s_ev, nm_ok, p_ok, pt_ps, pt_ev, o_ps,
         o_ev, ot_ps, ot_ev, zero_ok) = (sem(n) for n in (
             "wq_in", "tab_in", "lf_in", "q_ps", "q_ev", "q_blk", "ncm_ok", "s_ps", "s_ev", "nm_ok",
             "p_ok", "pt_ps", "pt_ev", "o_ps", "o_ev", "ot_ps", "ot_ev", "azero_ok"))
        (r_ps, r_ev, kt_ps2, kt_ev, kt_evb, cur_ok, ss_ps, m_ok2, e_ok, pp_ps, pp_ev, so_ps, so_ev, sot_ps,
         sot_ev) = (sem(n) for n in (
             "r_ps", "r_ev", "ktp_ps", "ktp_ev", "ktp_evb", "cur_ok", "ss_ps", "smax_ok", "sexp_ok", "pp_ps", "pp_ev",
             "so_ps", "so_ev", "sot_ps", "sot_ev"))
        cur_free = sem("cur_free")
        kv_half = [sem("kv_in_even"), sem("kv_in_odd")]
        gate = S["pool_passed"]
        win = A["w_in"].rearrange("a (t p) c -> p (a t) c", p=P)
        ck = A["cache_k"].rearrange("a n s g d -> s (a n) (g d)")
        cv = A["cache_v"].rearrange("a n s g d -> s (a n) (g d)")
        cl = A["cache_logf"].rearrange("a n s h -> s (a n) h")
        idn = S["ident"]
        keys = [128, 256, T]
        qrows = [128, 128, TAIL]
        qcol = [0, 128, TAIL_COL]

        def head(t, g2):
            return (t // 4) * 8 + 4 * g2 + t % 4

        def score_bank(g2, t):
            b = ps[1 + 2 * g2] if t < 2 else ps[2 + 2 * g2]
            c = 128 if t == 1 else 0
            return b[0:qrows[t], c:c + keys[t]]

        block = ctx.enter_context(nc.Block())

        def load_wq(eng, t):
            for g2 in range(2):
                eng.dma_start(wq[:, :, g2, :], win[:, :, bass.ds(head(t, g2) * HD + C_Q, HD)]).then_inc(wq_in, 16)

        @block.sync
        def _(sp):
            sp.dma_start(ptab[:, :], A["page_table"].rearrange("(a s) b -> a (s b)", a=1)).then_inc(tab_in, 16)
            sp.wait_ge(tab_in, 16)

            def load_kv(s, half):
                for b in range(NPG):
                    pg = sp.value_load(ptab[0:1, bass.ds(s * NPG + b, 1)], min_val=0, max_val=POOL - 1)
                    sp.dma_start(kpg[:, half, b, :].unsqueeze(1), ck[:, bass.ds(pg, 1), :]).then_inc(kv_half[half], 16)
                    sp.dma_start(vpg[:, half, b, :].unsqueeze(1), cv[:, bass.ds(pg, 1), :]).then_inc(kv_half[half], 16)

            with sp.Fori(0, NSEQ) as s:
                for b in range(NPG):
                    pg = sp.value_load(ptab[0:1, bass.ds(s * NPG + b, 1)], min_val=0, max_val=POOL - 1)
                    sp.dma_start(lfp[:, b, bass.ds(s, 1), :], cl[:, bass.ds(pg, 1), :]).then_inc(lf_in, 16)
            for half in range(2):
                load_kv(half, half)
            with sp.Fori(1, NSEQ // 2) as i:
                for half in range(2):
                    sp.wait_ge(so_ps, 2 * i + half - 1)
                    load_kv(2 * i + half, half)

        @block.gpsimd
        def _(pool):
            load_wq(pool, 0)
            pool.memset(qpad[:, :, :], 0.0)
            pool.memset(qblk[:, :, :, :], 0.0)
            pool.tensor_scalar(ntri[:, :], S["tri_le2"][0:64, 0:64], -1.0, None, ALU.mult)
            pool.tensor_scalar(selfneg[:, :, :], S["self01"][:, :, :], 1.0, -NEG, ALU.subtract, ALU.mult)
            pool.memset(sc[:, :, :, :], 0.0)
            pool.drain()
            pool.memset(mx[:, :], 0.0).then_inc(zero_ok, 1)
            with pool.Fori(1, 8) as t:
                pool.wait_ge(q_ps, t)
                load_wq(pool, t)
            pool.wait_ge(q_blk, 16)
            with pool.Fori(0, NSEQ) as s:
                pool.wait_ge(cur_free, s + 1)
                pool.sem_inc(gate)
                pool.tensor_copy(qcur[:, :, :], qblk[:, bass.ds(s, 1), :, :].rearrange("p o a c -> p (o a) c"))
                pool.tensor_copy(mcur[:, :], selfneg[:, bass.ds(s, 1), :].rearrange("k o c -> k (o c)"))
                pool.tensor_copy(scur[:, :].rearrange("k (h q) -> k h q", q=8),
                                 bc(idn[:, bass.ds(16 * s, 16)].unsqueeze(2), [P, 16, 8]))
                pool.tensor_tensor(lcur[:, :], S["lf_rep"][:, :, :].rearrange("k h q -> k (h q)"),
                                   S["self01"][:, bass.ds(s, 1), :].rearrange("k o c -> k (o c)"),
                                   ALU.mult).then_inc(cur_ok, 1)

        @block.scalar
        def _(act):
            act.wait_ge(zero_ok, 1)

            def q_out(t):
                act.wait_ge(q_ps, t + 1)
                for g2 in range(2):
                    q_ = slice(64 * g2, 64 * g2 + 64)
                    act.activation(qpad[q_, g2, :], ps[0][q_, 0:T], ACT.Copy, scale=HD ** -0.5).then_inc(q_ev, 1)

            def probs(t):
                for g2 in range(2):
                    for c in range(3):
                        k = 3 * g2 + c
                        r = qrows[c]
                        act.wait_ge(nm_ok, 6 * t + k + 1)
                        act.activation(sc[0:r, g2, c, 0:keys[c]], sc[0:r, g2, c, 0:keys[c]], ACT.Exp,
                                       bias=nm[0:r, k:k + 1], accum_out=rs[0:r, k:k + 1]).then_inc(p_ok, 1)
                for g2 in range(2):
                    act.wait_ge(pt_ps, 2 * t + g2 + 1)
                    act.activation(pt01[:, g2, :], ps[5 + 2 * g2][:, 0:384], ACT.Copy)
                    act.activation(pt2[:, g2, 0:32], ps[5 + 2 * g2][:, 384:416], ACT.Copy)
                    act.activation(pt2[0:80, g2, 32:48], ps[5 + 2 * g2][0:80, 416:432], ACT.Copy).then_inc(pt_ev, 1)

            def o_out(t):
                act.wait_ge(ot_ps, t + 1)
                act.activation(S["oT"][:, bass.ds(t, 1), 0:256], ps[2][:, 0:256].unsqueeze(1), ACT.Copy)
                act.activation(S["oT"][:, bass.ds(t, 1), 320:336], ps[2][:, 256:272].unsqueeze(1),
                               ACT.Copy).then_inc(ot_ev, 1)

            q_out(0)
            with act.Fori(0, 7) as t:
                probs(t)
                q_out(t + 1)
                o_out(t)
            probs(7)
            o_out(7)

            def keys_out(s):
                for b in range(2):
                    act.wait_ge(kt_ps2, 4 * s + b + 1)
                    act.activation(kts[:, 0, 512 * b:512 * b + 512], ps[b][:, :], ACT.Copy).then_inc(kt_ev, 1)

            def seq(s):
                act.wait_ge(m_ok2, s + 1)
                act.activation(pr[:, 0:PAST].rearrange("p (a c) -> p a c", a=2), psc[:, :, :], ACT.Exp,
                               bias=mx[:, 4:5], accum_out=sm[:, 0:1]).then_inc(e_ok, 1)
                act.activation(pr[:, PAST:PAST + NS], ps[6][:, 0:NS], ACT.Exp, bias=mx[:, 4:5],
                               accum_out=sm[:, 1:2]).then_inc(e_ok, 1)
                act.wait_ge(pp_ps, 3 * s + 1)
                act.activation(pts[:, 0:4, :], psc[:, 0, :].rearrange("p (b c) -> p b c", c=P), ACT.Copy)
                act.drain()
                act.wait_ge(pp_ps, 3 * s + 3)
                act.activation(ptself[:, :], ps[6][0:NS, P:2 * P], ACT.Copy).then_inc(pp_ev, 1)

            keys_out(0)
            with act.Fori(0, NSEQ - 1) as s:
                seq(s)
                keys_out(s + 1)
            seq(NSEQ - 1)

        @block.vector
        def _(v):
            v.wait_ge(zero_ok, 1)
            v.sem_inc(cur_free, 1)
            with v.Fori(0, 8) as t:
                for g2 in range(2):
                    h = head(t, g2)
                    v.tensor_scalar(ncm[:, g2, :], S["ncT"][:, :], idn[0:16, bass.ds(h, 1)], None,
                                    ALU.mult).then_inc(ncm_ok, 1)
                for g2 in range(2):
                    q_ = slice(64 * g2, 64 * g2 + 64)
                    v.wait_ge(q_ev, 2 * t + g2 + 1)
                    v.tensor_copy(qblk[q_, :, :, :].rearrange("p s a c -> p s (a c)")[
                        :, :, bass.ds((t // 4) * 192 + (t % 4) * 8 + 32 * g2, 8)],
                        qpad[q_, g2, 256:320].rearrange("p (s q) -> p s q", q=8)).then_inc(q_blk, 1)
                for g2 in range(2):
                    h = head(t, g2)
                    v.wait_ge(s_ps, 2 * t + g2 + 1)
                    for c in range(3):
                        r, n = qrows[c], keys[c]
                        mask = (S["mask_d"][:, 128:256], S["mask_d"][:, :], S["mask_t"][:, :])[c]
                        i = v.scalar_tensor_tensor(sc[0:r, g2, c, 0:n], score_bank(g2, c),
                                                   S["c_q"][0:r, c, bass.ds(h, 1)], mask, ALU.add, ALU.add)
                    i.then_inc(s_ev, 1)
                    v.drain()
                    for c in range(3):
                        r, n = qrows[c], keys[c]
                        v.tensor_reduce(nm[0:r, 3 * g2 + c:3 * g2 + c + 1], sc[0:r, g2, c, 0:n], AX.X, ALU.max,
                                        negate=True).then_inc(nm_ok, 1)
                v.wait_ge(p_ok, 6 * t + 6)
                for c in range(3):
                    v.reciprocal(rs[0:qrows[c], c::3], rs[0:qrows[c], c::3])
                v.drain()
                v.wait_ge(o_ps, t + 1)
                for c in range(3):
                    r = qrows[c]
                    i = v.tensor_tensor(orow[0:r, c, :].rearrange("q (g d) -> q g d", g=2),
                                        ps[6][0:r, P * c:P * c + P].rearrange("q (g d) -> q g d", g=2),
                                        bc(rs[0:r, c::3].unsqueeze(2), [r, 2, HD]), ALU.mult)
                i.then_inc(o_ev, 1)
            for b in range(2):
                v.wait_ge(r_ps, 1)
                v.tensor_copy(rall[:, 512 * b:512 * b + 512], psc[:, b, :]).then_inc(r_ev, 1)
            def keys_out(s):
                for b in range(2):
                    v.wait_ge(kt_ps2, 4 * s + b + 3)
                    v.tensor_copy(kts[:, 1, 512 * b:512 * b + 512], ps[2 + b][:, :]).then_inc(kt_evb, 1)

            def seq(s, ahead):
                v.wait_ge(ss_ps, s + 1)
                v.tensor_reduce(mx[:, 0:1], psc[:, :, :].rearrange("p a c -> p (a c)"), AX.X,
                                ALU.max).then_inc(cur_free, 1)
                v.tensor_reduce(mx[:, 1:2], ps[6][:, 0:NS], AX.X, ALU.max)
                v.tensor_copy(mx[:, 2:3], ps[6][:, NS:NS + 1])
                v.drain()
                v.scalar_tensor_tensor(mx[:, 3:4], mx[:, 0:1], mx[:, 1:2], mx[:, 2:3], ALU.max, ALU.add)
                v.drain()
                v.tensor_tensor(mx[:, 4:5], mx[:, 2:3], mx[:, 3:4], ALU.subtract).then_inc(m_ok2, 1)
                if ahead:
                    keys_out(s + 1)
                v.wait_ge(pp_ps, 3 * s + 2)
                v.tensor_copy(pts[:, 4:8, :], psc[:, 1, :].rearrange("p (b c) -> p b c", c=P)).then_inc(pp_ev, 1)
                v.wait_ge(e_ok, 2 * s + 2)
                v.tensor_tensor(sm[:, 2:3], sm[:, 0:1], sm[:, 1:2], ALU.add)
                v.drain()
                v.reciprocal(sm[:, 2:3], sm[:, 2:3])
                v.drain()
                v.wait_ge(so_ps, s + 1)
                for a in range(2):
                    q_ = slice(64 * a, 64 * a + 64)
                    v.tensor_scalar(oe[q_, :], ps[7][q_, P * a:P * a + P], sm[q_, 2:3], None,
                                    ALU.mult).then_inc(so_ev, 1)
                v.wait_ge(sot_ps, s + 1)
                for g2 in range(2):
                    q_ = slice(64 * g2, 64 * g2 + 64)
                    v.tensor_copy(S["oT"][q_, :, bass.ds(8 * s + 256, 8)].rearrange("p (a r) q -> p a r q", a=2),
                                  ps[7][q_, 256:384].rearrange("p (a g r q) -> p a g r q", a=2, g=2, q=8)[:, :, g2]
                                  ).then_inc(sot_ev, 1)

            keys_out(0)
            with v.Fori(0, NSEQ - 1) as s:
                seq(s, True)
            seq(NSEQ - 1, False)

        @block.tensor
        def _(pe):
            def project_q(t):
                pe.wait_ge(wq_in, 32 * t + 32)
                for k in range(KT):
                    mm = pe.matmul(ps[0][:, 0:T], wq[:, k, :, :], S["xnT"][:, k, :], start=(k == 0),
                                   stop=(k == KT - 1))
                mm.then_inc(q_ps, 1)

            def scores(t):
                pe.wait_ge(q_ev, 2 * t + 2)
                pe.wait_ge(ncm_ok, 2 * t + 2)
                for g2 in range(2):
                    for c in range(3):
                        r, n = qrows[c], keys[c]
                        o = score_bank(g2, c)
                        kt = S["kT"][:, bass.ds(t // 4, 1), 0:n].rearrange("p o c -> p (o c)")
                        pe.matmul(o, S["ones"][0:16, 0:r], ncm[:, g2, 0:n], start=True, stop=False)
                        mm = pe.matmul(o, qpad[:, g2, qcol[c]:qcol[c] + r], kt, start=False, stop=True)
                    mm.then_inc(s_ps, 1)

            def outputs(t):
                for g2 in range(2):
                    pe.wait_ge(p_ok, 6 * t + 3 * g2 + 3)
                    b = ps[5 + 2 * g2]
                    pe.transpose(b[:, 0:128], sc[:, g2, 0, 0:128], idn[:, :])
                    for j in range(2):
                        pe.transpose(b[:, 128 + P * j:256 + P * j], sc[:, g2, 1, P * j:P * j + P], idn[:, :])
                        pe.transpose(b[:, 384 + 16 * j:400 + 16 * j], sc[0:16, g2, 2, P * j:P * j + P],
                                     idn[0:16, 0:16])
                    pe.transpose(b[0:80, 416:432], sc[0:16, g2, 2, 256:336], idn[0:16, 0:16]).then_inc(pt_ps, 1)
                for g2 in range(2):
                    pe.wait_ge(pt_ev, 2 * t + g2 + 1)
                    vcol = (t // 4) * P + HD * g2
                    vs = [S["v"][0:r, c, bass.ds(vcol, HD)] for c, r in enumerate(ROWS)]
                    o = [ps[6][0:qrows[c], P * c + HD * g2:P * c + HD * g2 + HD] for c in range(3)]
                    pe.matmul(o[0], pt01[:, g2, 0:128], vs[0], start=True, stop=True)
                    pe.matmul(o[1], pt01[:, g2, 128:256], vs[0], start=True, stop=False)
                    pe.matmul(o[1], pt01[:, g2, 256:384], vs[1], start=False, stop=True)
                    pe.matmul(o[2], pt2[:, g2, 0:16], vs[0], start=True, stop=False)
                    pe.matmul(o[2], pt2[:, g2, 16:32], vs[1], start=False, stop=False)
                    mm = pe.matmul(o[2], pt2[0:80, g2, 32:48], vs[2], start=False, stop=True)
                mm.then_inc(o_ps, 1)
                pe.wait_ge(o_ev, t + 1)
                for c, r in enumerate(qrows):
                    mm = pe.transpose(ps[2][:, P * c:P * c + r], orow[0:r, c, :], idn[0:r, 0:r])
                mm.then_inc(ot_ps, 1)
                pe.wait_ge(ot_ev, t + 1)

            project_q(0)
            with pe.Fori(0, 7) as t:
                scores(t)
                project_q(t + 1)
                outputs(t)
            scores(7)
            outputs(7)
            pe.wait_ge(lf_in, 16 * NSEQ * NPG)
            for b in range(NPG):
                o = psc[:, b // 4, P * (b % 4):P * (b % 4) + P]
                mm = pe.matmul(o, lfp[:, b, :, :], S["tri_gt"][:, :], start=True, stop=(b == NPG - 1))
                for b2 in range(b + 1, NPG):
                    mm = pe.matmul(o, lfp[:, b2, :, :], S["ones"][:, :], start=False, stop=(b2 == NPG - 1))
            mm.then_inc(r_ps, 1)
            pe.wait_ge(r_ev, 2)
            def turn_keys(i, half):
                pe.wait_ge(kv_half[half], 32 * NPG * i + 32 * NPG)
                for a in range(2):
                    for hb in range(2):
                        for b in range(4):
                            mm = pe.transpose(ps[2 * a + hb][:, P * b:P * b + P],
                                              kpg[:, half, 4 * hb + b, P * a:P * a + P], idn[:, :])
                        mm.then_inc(kt_ps2, 1)

            def seq_scores(s):
                pe.wait_ge(cur_ok, s + 1)
                sf = ps[6][:, 0:NS]
                for a in range(2):
                    pe.matmul(sf, qcur[:, a, :], S["kT"][:, a, 256:320], start=(a == 0), stop=False)
                pe.matmul(sf, S["lf_rep"][:, :, :].rearrange("k h q -> k (h q)"), ntri[:, :], start=False,
                          stop=False)
                pe.matmul(sf, mcur[:, :], idn[0:NS, 0:NS], start=False, stop=True)
                pe.matmul(ps[6][:, NS:NS + 1], lcur[:, :], S["ones"][0:NS, 0:1], start=True, stop=True)
                for b in range(2):
                    pe.matmul(psc[:, b, :], scur[:, :], rall[:, 512 * b:512 * b + 512], start=True, stop=False)
                pe.wait_ge(kt_ev, 2 * s + 2)
                pe.wait_ge(kt_evb, 2 * s + 2)
                for b in range(2):
                    for a in range(2):
                        mm = pe.matmul(psc[:, b, :], qcur[:, a, :], kts[:, a, 512 * b:512 * b + 512],
                                       start=False, stop=(a == 1))
                mm.then_inc(ss_ps, 1)

            def seq_outputs(s, half):
                pe.wait_ge(e_ok, 2 * s + 2)
                for hb in range(2):
                    for b in range(4):
                        c = P * (4 * hb + b)
                        mm = pe.transpose(psc[:, hb, P * b:P * b + P], pr[:, c:c + P], idn[:, :])
                    mm.then_inc(pp_ps, 1)
                pe.transpose(ps[6][0:NS, P:2 * P], pr[:, PAST:PAST + NS], idn[:, :]).then_inc(pp_ps, 1)
                pe.wait_ge(pp_ev, 2 * s + 2)
                for b in range(NPG):
                    pe.matmul(ps[7][:, 0:256], pts[:, b, :], vpg[:, half, b, :], start=(b == 0), stop=False)
                pe.matmul(ps[7][:, 0:256], ptself[:, :], S["v"][0:NS, 2, :], start=False,
                          stop=True).then_inc(so_ps, 1)
                pe.wait_ge(so_ev, 2 * s + 2)
                pe.transpose(ps[7][:, 256:384], oe[:, :], idn[:, :]).then_inc(sot_ps, 1)
                pe.wait_ge(sot_ev, 2 * s + 2)

            turn_keys(0, 0)
            with pe.Fori(0, NSEQ // 2 - 1) as i:
                for half in range(2):
                    s = 2 * i + half
                    seq_scores(s)
                    turn_keys(i + half, 1 - half)
                    seq_outputs(s, half)
            seq_scores(NSEQ - 2)
            turn_keys(NSEQ // 2 - 1, 1)
            seq_outputs(NSEQ - 2, 0)
            seq_scores(NSEQ - 1)
            seq_outputs(NSEQ - 1, 1)


def merge_phase(nc, A, S, sem):
    with ExitStack() as ctx:
        def tsb(name, shape, dt=F32):
            return ctx.enter_context(nc.sbuf_tensor(name, shape, dt))

        wm = [tsb(f"w_merge{h}", [P, 40, P]) for h in range(2)]
        wo = tsb("w_out_sb", [P, KT, D])
        th = [tsb(f"gate_tanh{h}", [P, 2, T]) for h in range(2)]
        mx_ = [tsb(f"mix_part{h}", [P, 2, T]) for h in range(2)]
        mixT = tsb("mixT", [P, KT, T])
        S["mixT"] = mixT
        xsq, ss = tsb("xsq2", [P, D]), tsb("ss2", [P, 4])
        wr = tsb("w_router", [P, KT, 36])
        ps = [ctx.enter_context(nc.psum_tensor(f"psm{i}", [P, 512], F32)) for i in range(8)]
        w_half = [sem("merge_w_even"), sem("merge_w_odd")]
        wo_in, wr_in, g_ps, g_th, b_ps, mix_ok, h_ps, h_ev, hn_ok, tr_ps, tr_ev, lg_ps, lg_ev = (
            sem(n) for n in ("wo_in", "wr_in", "gate_ps", "gate_th", "branch_ps", "mix_ok", "h_ps", "h_ev",
                             "hn_ok", "hnt_ps", "hnt_ev", "logit_ps", "logit_ev"))
        ssq, rs_ok = S["row_squares_ok"], S["row_rstd_ok"]
        mix_used = sem("mix_banks_free")
        win = A["w_in"].rearrange("a (t p) c -> p (a t) c", p=P)
        wsb = A["w_ssd_br"].rearrange("a (t p) c -> p (a t) c", p=P)
        wab = A["w_attn_br"].rearrange("a (u g r d) c -> g d (a u) r c", u=2, g=2, r=4)
        block = ctx.enter_context(nc.Block())

        @block.sync
        def _(sp):
            def load(m, h):
                sp.dma_start(wm[h][:, 0:8, :], win[:, :, bass.ds(m * P + C_GS, P)]).then_inc(w_half[h], 16)
                sp.dma_start(wm[h][:, 8:16, :], win[:, :, bass.ds(m * P + C_GS + D, P)]).then_inc(w_half[h], 16)
                sp.dma_start(wm[h][:, 16:32, :], wsb[:, :, bass.ds(m * P, P)]).then_inc(w_half[h], 16)
                for g2 in range(2):
                    for u in range(2):
                        sp.dma_start(wm[h][64 * g2:64 * g2 + 64, 32 + 4 * u:36 + 4 * u, :],
                                     wab[g2, :, u, :, bass.ds(m * P, P)]).then_inc(w_half[h], 16)

            load(0, 0)
            load(1, 1)
            sp.dma_start(wo[:, :, :], A["w_out"].rearrange("a (t p) c -> p (a t) c", p=P)).then_inc(wo_in, 16)
            sp.dma_start(wr[:, :, 0:4], A["w_router_group"].rearrange("a (t p) c -> p (a t) c", p=P)).then_inc(wr_in, 16)
            sp.dma_start(wr[:, :, 4:36], A["w_router_expert"].rearrange("a (t p) c -> p (a t) c", p=P)).then_inc(wr_in, 16)
            sp.dma_start(S["rbias"][:, 0:4], A["b_router_group"][0, :].partition_broadcast(P)).then_inc(wr_in, 16)
            sp.dma_start(S["rbias"][:, 4:36], A["b_router_expert"][0, :].partition_broadcast(P)).then_inc(wr_in, 16)
            with sp.Fori(1, 4) as i:
                for h in range(2):
                    sp.wait_ge(b_ps, 2 * i + h - 1)
                    load(2 * i + h, h)

        @block.gpsimd
        def _(pool):
            for t, r in enumerate(ROWS):
                pool.wait_ge(ssq, 3 + t + 1)
                pool.tensor_scalar(ss[0:r, t:t + 1], ss[0:r, t:t + 1], 1.0 / D, EPS, ALU.mult, ALU.add)
                pool.drain()
                pool.tensor_tensor(ss[0:r, t:t + 1], ss[0:r, t:t + 1], S["mhalf"][0:r, 0:1], ALU.pow).then_inc(rs_ok, 1)

        @block.scalar
        def _(act):
            with act.Fori(0, 4) as i:
                for h in range(2):
                    m = 2 * i + h
                    for j in range(2):
                        act.wait_ge(g_ps, 2 * m + j + 1)
                        act.activation(th[h][:, j, :], ps[4 * h + j][:, 0:T], ACT.Tanh, scale=0.5).then_inc(g_th, 1)
            for t, r in enumerate(ROWS):
                act.wait_ge(h_ev, 2 * t + 2)
                act.activation(xsq[0:r, :], S["xtok"][0:r, t, :], ACT.Square,
                               accum_out=ss[0:r, t:t + 1]).then_inc(ssq, 1)
                act.drain()

        @block.vector
        def _(v):
            v.sem_inc(mix_used, 2)
            with v.Fori(0, 4) as i:
                for h in range(2):
                    m = 2 * i + h
                    v.wait_ge(g_th, 2 * m + 2)
                    v.wait_ge(b_ps, m + 1)
                    for j in range(2):
                        k = v.scalar_tensor_tensor(mx_[h][:, j, :], th[h][:, j, :], 1.0, ps[4 * h + 2 + j][:, 0:T],
                                                   ALU.add, ALU.mult)
                    k.then_inc(mix_used, 1)
                    v.drain()
                    v.tensor_tensor(mixT[:, bass.ds(m, 1), :], mx_[h][:, 0, :].unsqueeze(1),
                                    mx_[h][:, 1, :].unsqueeze(1), ALU.add).then_inc(mix_ok, 1)
            for t, r in enumerate(ROWS):
                for h in range(2):
                    v.wait_ge(h_ps, 2 * t + h + 1)
                    x = S["xtok"][0:r, t, 512 * h:512 * h + 512]
                    v.scalar_tensor_tensor(x, ps[2 * t + h][0:r, :], 0.5, x, ALU.mult, ALU.add).then_inc(h_ev, 1)
            for t, r in enumerate(ROWS):
                v.wait_ge(rs_ok, 3 + t + 1)
                v.tensor_scalar(S["hn"][0:r, t, :], S["xtok"][0:r, t, :], ss[0:r, t:t + 1], None,
                                ALU.mult).then_inc(hn_ok, 1)
            for t, r in enumerate(ROWS):
                for h in range(2):
                    v.wait_ge(tr_ps, 2 * t + h + 1)
                    v.tensor_tensor(S["hnT"][:, 4 * h:4 * h + 4, COL[t]:COL[t] + r],
                                    ps[2 * t + h][:, :].rearrange("p (k c) -> p k c", c=P)[:, :, 0:r],
                                    bc(S["gcol"][:, 24 + 4 * h:28 + 4 * h].unsqueeze(2), [P, 4, r]),
                                    ALU.mult).then_inc(tr_ev, 1)
            v.memset(S["lg"][:, :, :], 0.0)
            v.drain()
            v.wait_ge(lg_ps, 1)
            for t, r in enumerate(ROWS):
                v.tensor_tensor(S["lg"][0:r, t, :], ps[6][0:r, 64 * t:64 * t + 36], S["rbias"][0:r, :],
                                ALU.add).then_inc(lg_ev, 1)

        @block.tensor
        def _(pe):
            with pe.Fori(0, 4) as i:
                for h in range(2):
                    m = 2 * i + h
                    pe.wait_ge(w_half[h], 112 * i + 112)
                    pe.wait_ge(mix_used, m + 1)
                    for j in range(2):
                        for k in range(KT):
                            mm = pe.matmul(ps[4 * h + j][:, 0:T], wm[h][:, 8 * j + k, :], S["xnT"][:, k, :],
                                           start=(k == 0), stop=(k == KT - 1))
                        mm.then_inc(g_ps, 1)
                    for k in range(16):
                        pe.matmul(ps[4 * h + 2][:, 0:T], wm[h][:, 16 + k, :], S["yT"][:, k, :], start=(k == 0),
                                  stop=(k == 15))
                    for k in range(8):
                        mm = pe.matmul(ps[4 * h + 3][:, 0:T], wm[h][:, 32 + k, :], S["oT"][:, k, :], start=(k == 0),
                                       stop=(k == 7))
                    mm.then_inc(b_ps, 1)
            pe.wait_ge(wo_in, 16)
            pe.wait_ge(mix_ok, 8)
            for t, r in enumerate(ROWS):
                for h in range(2):
                    for k in range(KT):
                        mm = pe.matmul(ps[2 * t + h][0:r, :], mixT[:, k, COL[t]:COL[t] + r],
                                       wo[:, k, 512 * h:512 * h + 512], start=(k == 0), stop=(k == KT - 1))
                    mm.then_inc(h_ps, 1)
            pe.wait_ge(h_ev, 6)
            for t, r in enumerate(ROWS):
                pe.wait_ge(hn_ok, t + 1)
                for h in range(2):
                    for k in range(4):
                        mm = pe.transpose(ps[2 * t + h][:, P * k:P * k + r],
                                          S["hn"][0:r, t, P * (4 * h + k):P * (4 * h + k + 1)], S["ident"][0:r, 0:r])
                    mm.then_inc(tr_ps, 1)
            pe.wait_ge(tr_ev, 6)
            pe.wait_ge(wr_in, 64)
            for t, r in enumerate(ROWS):
                for k in range(KT):
                    mm = pe.matmul(ps[6][0:r, 64 * t:64 * t + 36], S["hnT"][:, k, COL[t]:COL[t] + r], wr[:, k, :],
                                   start=(k == 0), stop=(k == KT - 1))
            mm.then_inc(lg_ps, 1)


def route_phase(nc, A, S, sem):
    with ExitStack() as ctx:
        def tsb(name, shape, dt=F32):
            return ctx.enter_context(nc.sbuf_tensor(name, shape, dt))

        it32i, it32 = tsb("iota32_i", [P, 32], I32), tsb("iota32", [P, 32])
        it64i, itbi, itb = tsb("iota64_i", [P, BLK], I32), tsb("iota_blk_i", [1, NBLK], I32), tsb("iota_blk", [1, NBLK])
        g4, gm, eg, cand, cm = (tsb("g4", [P, 3, 4]), tsb("gmax", [P, 3]), tsb("g_exp", [P, 3, 4]),
                                tsb("cand", [P, 3, 32]), tsb("cmin", [P, 3]))
        og, pen = tsb("g_onehot", [P, 3, 4]), tsb("g_penalty", [P, 3, 4])
        el, l1, l2, oh = tsb("el", [P, 3, 32]), tsb("l1", [P, 3]), tsb("l2", [P, 3]), tsb("e_onehot", [P, 2, 3, 32])
        pg, dd, ee = tsb("p_group", [P, 3]), tsb("l_diff", [P, 3]), tsb("l_exp", [P, 3])
        mm_, rank, cnt, nb, pend, start = (tsb("pair_mask", [P, 3, 32]), tsb("rank", [P, 3, 32]), tsb("cnt", [P, 32]),
                                           tsb("n_blocks", [P, 32]), tsb("blocks_end", [P, 32]),
                                           tsb("blocks_start", [P, 32]))
        tmp, cmpb, bef, tri_lt = (tsb("slot_tmp", [P, 3, 32]), tsb("blk_cmp", [1, NBLK, 32]), tsb("blk_e_f", [1, NBLK]),
                                  tsb("tri_lt", [P, P]))
        ps = [ctx.enter_context(nc.psum_tensor(f"psr{i}", [P, 512], F32)) for i in range(2)]
        io_ok, gx, ge, lx, le_, mk, rk_ps, rk_ev = (sem(n) for n in ("iotas", "g_in", "g_exp_ok", "l_in", "l_exp_ok",
                                                                     "mask_ok", "rank_ps", "rank_ev"))
        block = ctx.enter_context(nc.Block())

        @block.gpsimd
        def _(pool):
            pool.iota(it32i[:, :], pattern=[[1, 32]], base=0, channel_multiplier=0)
            pool.iota(it64i[:, :], pattern=[[1, BLK]], base=0, channel_multiplier=0)
            pool.iota(itbi[:, :], pattern=[[1, NBLK]], base=0, channel_multiplier=0)
            pool.drain()
            pool.tensor_copy(it32[:, :], it32i[:, :])
            pool.tensor_copy(S["iota"][:, :], it64i[:, :])
            pool.tensor_copy(itb[:, :], itbi[:, :])
            pool.tensor_tensor(tri_lt[:, :], S["tri_le"][:, :], S["ident"][:, :], ALU.subtract).then_inc(io_ok, 1)

        @block.scalar
        def _(act):
            act.wait_ge(gx, 1)
            act.activation(eg[:, :, :], g4[:, :, :], ACT.Exp).then_inc(ge, 1)
            act.wait_ge(lx, 1)
            act.activation(ee[:, :], dd[:, :], ACT.Exp).then_inc(le_, 1)

        @block.tensor
        def _(pe):
            pe.wait_ge(mk, 1)
            m = [mm_[0:r, t, :] for t, r in enumerate(ROWS)]
            o = S["ones"]
            pe.matmul(ps[0][:, 0:32], tri_lt[:, :], m[0], start=True, stop=True)
            pe.matmul(ps[0][:, 32:64], o[:, :], m[0], start=True, stop=False)
            pe.matmul(ps[0][:, 32:64], tri_lt[:, :], m[1], start=False, stop=True)
            pe.matmul(ps[0][0:80, 64:96], o[:, 0:80], m[0], start=True, stop=False)
            pe.matmul(ps[0][0:80, 64:96], o[:, 0:80], m[1], start=False, stop=False)
            pe.matmul(ps[0][0:80, 64:96], tri_lt[0:80, 0:80], m[2], start=False, stop=True)
            pe.matmul(ps[1][:, 0:32], o[:, :], m[0], start=True, stop=False)
            pe.matmul(ps[1][:, 0:32], o[:, :], m[1], start=False, stop=False)
            pe.matmul(ps[1][:, 0:32], o[0:80, :], m[2], start=False, stop=True).then_inc(rk_ps, 1)

        @block.vector
        def _(v):
            lg = S["lg"]
            b3 = lambda a, n: bc(a.unsqueeze(2), [P, 3, n])
            i32_ = bc(it32[:, :].unsqueeze(1), [P, 3, 32])
            v.tensor_reduce(gm[:, :], lg[:, :, 0:4], AX.X, ALU.max)
            v.drain()
            v.tensor_tensor(g4[:, :, :], lg[:, :, 0:4], b3(gm[:, :], 4), ALU.subtract).then_inc(gx, 1)
            v.tensor_tensor(og[:, :, :], lg[:, :, 0:4], b3(gm[:, :], 4), ALU.is_equal)
            v.wait_ge(io_ok, 1)

            def first(onehot, eq, n):
                v.drain()
                v.scalar_tensor_tensor(cand[:, :, 0:n], eq, -100.0, bc(it32[:, 0:n].unsqueeze(1), [P, 3, n]),
                                       ALU.mult, ALU.add)
                v.drain()
                v.tensor_reduce(cm[:, :], cand[:, :, 0:n], AX.X, ALU.min)
                v.drain()
                v.tensor_tensor(onehot, cand[:, :, 0:n], b3(cm[:, :], n), ALU.is_equal)
                v.drain()

            first(og[:, :, :], og[:, :, :], 4)
            v.tensor_scalar(pen[:, :, :], og[:, :, :], 1.0, -NEG, ALU.subtract, ALU.mult)
            v.tensor_tensor(el[:, :, :].rearrange("p t (g e) -> p t g e", g=4),
                            lg[:, :, 4:36].rearrange("p t (g e) -> p t g e", g=4),
                            bc(og[:, :, :].unsqueeze(3), [P, 3, 4, 8]), ALU.mult)
            v.drain()
            v.tensor_tensor(el[:, :, :].rearrange("p t (g e) -> p t g e", g=4),
                            el[:, :, :].rearrange("p t (g e) -> p t g e", g=4),
                            bc(pen[:, :, :].unsqueeze(3), [P, 3, 4, 8]), ALU.add)
            v.drain()
            v.tensor_reduce(l1[:, :], el[:, :, :], AX.X, ALU.max)
            v.drain()
            v.tensor_tensor(oh[:, 0, :, :], el[:, :, :], b3(l1[:, :], 32), ALU.is_equal)
            first(oh[:, 0, :, :], oh[:, 0, :, :], 32)
            v.scalar_tensor_tensor(el[:, :, :], oh[:, 0, :, :], 3 * NEG, el[:, :, :], ALU.mult, ALU.add)
            v.drain()
            v.tensor_reduce(l2[:, :], el[:, :, :], AX.X, ALU.max)
            v.drain()
            v.tensor_tensor(dd[:, :], l2[:, :], l1[:, :], ALU.subtract).then_inc(lx, 1)
            v.tensor_tensor(oh[:, 1, :, :], el[:, :, :], b3(l2[:, :], 32), ALU.is_equal)
            first(oh[:, 1, :, :], oh[:, 1, :, :], 32)
            v.tensor_tensor(mm_[:, :, :], oh[:, 0, :, :], oh[:, 1, :, :], ALU.add).then_inc(mk, 1)
            v.wait_ge(ge, 1)
            v.tensor_reduce(pg[:, :], eg[:, :, :], AX.X, ALU.add)
            v.wait_ge(le_, 1)
            v.drain()
            v.reciprocal(pg[:, :], pg[:, :])
            v.tensor_scalar(dd[:, :], ee[:, :], 1.0, None, ALU.add)
            v.drain()
            v.reciprocal(dd[:, :], dd[:, :])
            v.drain()
            v.tensor_tensor(S["topw"][:, :, 0], pg[:, :], dd[:, :], ALU.mult)
            v.drain()
            v.tensor_tensor(S["topw"][:, :, 1], S["topw"][:, :, 0], ee[:, :], ALU.mult)
            v.wait_ge(rk_ps, 1)
            v.memset(rank[:, :, :], 0.0)
            v.drain()
            v.tensor_copy(rank[:, 0:2, :], ps[0][:, 0:64].rearrange("p (t e) -> p t e", t=2))
            v.tensor_copy(rank[0:80, 2, :], ps[0][0:80, 64:96])
            v.tensor_copy(cnt[:, :], ps[1][:, 0:32])
            v.drain()
            v.tensor_scalar(nb[:, :], cnt[:, :], 0.5, None, ALU.is_gt)
            v.drain()
            for k in range(1, -(-T // BLK)):
                v.scalar_tensor_tensor(nb[:, :], cnt[:, :], BLK * k + 0.5, nb[:, :], ALU.is_gt, ALU.add)
                v.drain()
            v.tensor_tensor_scan(pend[:, :], S["ones"][:, 0:32], nb[:, :], 0.0, ALU.mult, ALU.add)
            v.drain()
            v.tensor_tensor(start[:, :], pend[:, :], nb[:, :], ALU.subtract)
            v.drain()
            v.scalar_tensor_tensor(rank[:, :, :], bc(start[:, :].unsqueeze(1), [P, 3, 32]), float(BLK),
                                   rank[:, :, :], ALU.mult, ALU.add)
            v.drain()
            for j in range(2):
                v.tensor_tensor(tmp[:, :, :], oh[:, j, :, :], rank[:, :, :], ALU.mult)
                v.drain()
                v.tensor_reduce(S["slot"][:, :, j:j + 1], tmp[:, :, :], AX.X, ALU.add)
                v.drain()
            v.tensor_copy(S["slot_i"][:, :, :], S["slot"][:, :, :])
            v.tensor_tensor(cmpb[:, :, :], bc(pend[0:1, :].unsqueeze(1), [1, NBLK, 32]),
                            bc(itb[:, :].unsqueeze(2), [1, NBLK, 32]), ALU.is_le)
            v.drain()
            v.tensor_reduce(bef[:, :], cmpb[:, :, :], AX.X, ALU.add)
            v.drain()
            v.tensor_scalar(S["blk_e"][:, 0:NBLK], bef[:, :], float(NE - 1), None, ALU.min)
            v.tensor_copy(S["blk_e"][:, NBLK:NBLK + 1], pend[0:1, NE - 1:NE])


def moe_phase(nc, A, S, sem):
    with ExitStack() as ctx:
        def tsb(name, shape, dt=F32):
            return ctx.enter_context(nc.sbuf_tensor(name, shape, dt))

        w_gu = [tsb(f"w_gate_up{h}", [P, 2, KT, DE]) for h in range(2)]
        w_dn = [tsb(f"w_down{h}", [P, DE // P, D]) for h in range(2)]
        rel = tsb("slot_rel", [P, 3, 2])
        eq = tsb("slot_eq", [P, 3, 2, BLK])
        sel = tsb("block_rows", [P, 3, BLK])
        xrow = tsb("x_rows", [P, 512])
        xg = tsb("x_gathered", [P, 4, 2, BLK])
        th, hg, hrow = tsb("h_tanh", [P, 256]), tsb("h_gate", [P, 256]), tsb("h_rows", [P, 256])
        ht = tsb("h_t", [P, 2, 2, BLK])
        yr = [tsb(f"y_block{h}", [P, 512]) for h in range(2)]
        px, pxt, ph, pht = (ctx.enter_context(nc.psum_tensor(n, [P, 512], F32)) for n in ("px", "pxt", "ph", "pht"))
        py = [ctx.enter_context(nc.psum_tensor(f"py{h}", [P, 512], F32)) for h in range(2)]
        gu_in = [sem("gate_up_even"), sem("gate_up_odd")]
        dn_in = [sem("down_even"), sem("down_odd")]
        sel_ok, xr_ps, xr_ev, xt_ps, xt_ok, gu_ps, th_ok, hb_ok, ht_ps, ht_ok, y_ps, y_ev, gu_free = (
            sem(n) for n in ("sel_ok", "xrow_ps", "xrow_ev", "xt_ps", "xt_ok", "gu_ps", "hth_ok", "h_ok", "ht_t_ps",
                             "ht_ok", "yb_ps", "yb_ev", "gate_up_free"))
        y_zero = sem("y_zero")
        y_sent = [sem("y_sent_even"), sem("y_sent_odd")]
        ydram = S["ydram"].rearrange("s (j d) -> s j d", j=2)
        block = ctx.enter_context(nc.Block())

        def blocks_of(eng):
            return eng.value_load(S["blk_e"][0:1, NBLK:NBLK + 1], min_val=1, max_val=NBLK)

        @block.sync
        def _(sp):
            nblk = blocks_of(sp)
            sp.sem_inc(y_sent[0], 32)
            sp.sem_inc(y_sent[1], 32)
            with sp.Fori(0, NBLK // 2) as i:
                for h in range(2):
                    b = 2 * i + h
                    with sp.If(b < nblk):
                        e = sp.value_load(S["blk_e"][0:1, bass.ds(b, 1)], min_val=0, max_val=NE - 1)
                        sp.wait_ge(gu_free, b + 1)
                        for j, w in enumerate(("w_exp_gate", "w_exp_up")):
                            sp.dma_start(w_gu[h][:, j, :, :], A[w].rearrange("a e (t p) f -> p (a e) t f", p=P)[
                                :, bass.ds(e, 1)].rearrange("p o t f -> p (o t) f")).then_inc(gu_in[h], 16)
                        sp.wait_ge(y_ev, b + 1)
                        sp.dma_start(w_dn[h][:, :, :], A["w_exp_down"].rearrange("a e (t p) d -> p (a e) t d", p=P)[
                            :, bass.ds(e, 1)].rearrange("p o t d -> p (o t) d")).then_inc(dn_in[h], 16)

        @block.gpsimd
        def _(pool):
            for h in range(2):
                pool.memset(yr[h][:, :], 0.0).then_inc(y_zero, 1)

        @block.scalar
        def _(act):
            act.wait_ge(y_zero, 2)
            nblk = blocks_of(act)
            act.sem_inc(y_ev, 2)

            def rows_out(n):
                act.wait_ge(xr_ps, n)
                act.activation(xrow[:, :], px[:, :], ACT.Copy).then_inc(xr_ev, 1)

            rows_out(1)
            with act.Fori(0, NBLK // 2) as i:
                for h in range(2):
                    b = 2 * i + h
                    with act.If(b < nblk):
                        act.wait_ge(gu_ps, b + 1)
                        act.activation(th[:, :], ph[:, 0:256], ACT.Tanh, scale=0.5).then_inc(th_ok, 1)
                        rows_out(b + 2)
                        act.wait_ge(y_ps, b + 1)
                        act.wait_ge(y_sent[h], 32 * i + 32)
                        act.activation(yr[h][:, :], py[h][:, :], ACT.Copy).then_inc(y_ev, 1)
                    act.drain()
                    for j in range(2):
                        act.dma_start(ydram[bass.ds(BLK * b, BLK), j, :], yr[h][64 * j:64 * j + 64, :]
                                      ).then_inc(y_sent[h], 16)
            for h in range(2):
                act.wait_ge(y_sent[h], 16 * NBLK + 32)

        @block.vector
        def _(v):
            v.sem_inc(gu_free, 2)
            nblk = blocks_of(v)
            v.tensor_copy(rel[:, :, :], S["slot"][:, :, :])

            def pick():
                v.drain()
                v.tensor_tensor(eq[:, :, :, :].rearrange("p t j c -> p (t j) c"),
                                bc(S["iota"][:, :].unsqueeze(1), [P, 6, BLK]),
                                bc(rel[:, :, :].rearrange("p t j -> p (t j)").unsqueeze(2), [P, 6, BLK]),
                                ALU.is_equal)
                v.drain()
                v.tensor_tensor(sel[:, :, :], eq[:, :, 0, :], eq[:, :, 1, :], ALU.add).then_inc(sel_ok, 1)
                v.tensor_scalar(rel[:, :, :], rel[:, :, :], -float(BLK), None, ALU.add)

            def gathered(n):
                v.wait_ge(xt_ps, n)
                v.tensor_tensor(xg[:, :, :, :], pxt[:, :].rearrange("p (c j s) -> p c j s", c=4, j=2),
                                bc(S["gcol"][:, 24:32].rearrange("p (j c) -> p c j", j=2).unsqueeze(3),
                                   [P, 4, 2, BLK]), ALU.mult).then_inc(xt_ok, 1)

            pick()
            gathered(1)
            with v.Fori(0, NBLK // 2) as i:
                for h in range(2):
                    b = 2 * i + h
                    with v.If(b < nblk):
                        pick()
                        v.wait_ge(th_ok, b + 1)
                        v.scalar_tensor_tensor(hg[:, :], th[:, :], 1.0, ph[:, 0:256], ALU.add,
                                               ALU.mult).then_inc(gu_free, 1)
                        v.drain()
                        v.scalar_tensor_tensor(hrow[:, :], hg[:, :], 0.5, ph[:, 256:512], ALU.mult,
                                               ALU.mult).then_inc(hb_ok, 1)
                        v.wait_ge(ht_ps, b + 1)
                        v.tensor_copy(ht[:, :, :, :], pht[:, 0:256].rearrange("p (c j s) -> p c j s", c=2, j=2)
                                      ).then_inc(ht_ok, 1)
                        gathered(b + 2)

        @block.tensor
        def _(pe):
            nblk = blocks_of(pe)

            def gather_rows(n):
                pe.wait_ge(sel_ok, n)
                for t, r in enumerate(ROWS):
                    for j in range(2):
                        mm = pe.matmul(px[64 * j:64 * j + 64, :], sel[0:r, t, :], S["hn"][0:r, t, 512 * j:512 * j + 512],
                                       start=(t == 0), stop=(t == 2))
                mm.then_inc(xr_ps, 1)

            def gather_turn(n):
                pe.wait_ge(xr_ev, n)
                for c in range(4):
                    mm = pe.transpose(pxt[:, P * c:P * c + P], xrow[:, P * c:P * c + P], S["ident"][:, :])
                mm.then_inc(xt_ps, 1)

            gather_rows(1)
            gather_turn(1)
            with pe.Fori(0, NBLK // 2) as i:
                for h in range(2):
                    b = 2 * i + h
                    with pe.If(b < nblk):
                        pe.wait_ge(xt_ok, b + 1)
                        pe.wait_ge(gu_in[h], 32 * i + 32)
                        for k in range(KT):
                            for j in range(2):
                                mm = pe.matmul(ph[64 * j:64 * j + 64, :], xg[:, k % 4, k // 4, :],
                                               w_gu[h][:, :, k, 256 * j:256 * j + 256],
                                               start=(k == 0), stop=(k == KT - 1))
                        mm.then_inc(gu_ps, 1)
                        gather_rows(b + 2)
                        pe.wait_ge(hb_ok, b + 1)
                        for c in range(2):
                            mm = pe.transpose(pht[:, P * c:P * c + P], hrow[:, P * c:P * c + P], S["ident"][:, :])
                        mm.then_inc(ht_ps, 1)
                        gather_turn(b + 2)
                        pe.wait_ge(ht_ok, b + 1)
                        pe.wait_ge(dn_in[h], 16 * i + 16)
                        pe.wait_ge(y_ev, b + 1)
                        for k in range(4):
                            for j in range(2):
                                mm = pe.matmul(py[h][64 * j:64 * j + 64, :], ht[:, k % 2, k // 2, :],
                                               w_dn[h][:, k, 512 * j:512 * j + 512], start=(k == 0), stop=(k == 3))
                        mm.then_inc(y_ps, 1)


def final_phase(nc, A, S, sem):
    with ExitStack() as ctx:
        def tsb(name, shape, dt=F32):
            return ctx.enter_context(nc.sbuf_tensor(name, shape, dt))

        ye = tsb("y_expert", [P, 3, 2, D])
        fg = tsb("final_g", [P, D])
        xsq, ss, out = tsb("xsq3", [P, D]), tsb("ss3", [P, 4]), tsb("y_final", [P, 3, D])
        ssq, rs_ok = S["row_squares_ok"], S["row_rstd_ok"]
        ye_in, g_in, h_ok, out_ok, sent = (sem(n) for n in (
            "y_expert_in", "final_g_in", "h2_ok", "out_ok", "sent"))
        block = ctx.enter_context(nc.Block())

        @block.sync
        def _(sp):
            sp.dma_start(fg[:, :], A["final_norm_g"].partition_broadcast(P)).then_inc(g_in, 16)
            yp = A["y_p"].rearrange("a s d -> (a s) d")
            sp.wait_ge(out_ok, 1)
            sp.dma_start(yp[0:112, :], out[16:128, 0, :]).then_inc(sent, 16)
            sp.wait_ge(out_ok, 2)
            sp.dma_start(yp[112:240, :], out[:, 1, :]).then_inc(sent, 16)
            sp.wait_ge(out_ok, 3)
            sp.dma_start(A["y_s"].rearrange("a s d -> (a s) d"), out[0:64, 2, :]).then_inc(sent, 16)
            sp.dma_start(yp[240:256, :], out[64:80, 2, :]).then_inc(sent, 16)
            sp.wait_ge(sent, 64)

        @block.gpsimd
        def _(pool):
            for t, r in enumerate(ROWS):
                for j in range(2):
                    pool.indirect_dma_start(ye[0:r, t, j, :], None, S["ydram"],
                                            bass.IndirectOffsetOnAxis(ap=S["slot_i"][0:r, t, j:j + 1], axis=0)
                                            ).then_inc(ye_in, 16)
            for t, r in enumerate(ROWS):
                pool.wait_ge(ssq, 6 + t + 1)
                pool.tensor_scalar(ss[0:r, t:t + 1], ss[0:r, t:t + 1], 1.0 / D, EPS, ALU.mult, ALU.add)
                pool.drain()
                pool.tensor_tensor(ss[0:r, t:t + 1], ss[0:r, t:t + 1], S["mhalf"][0:r, 0:1], ALU.pow).then_inc(rs_ok, 1)

        @block.scalar
        def _(act):
            for t, r in enumerate(ROWS):
                act.wait_ge(h_ok, t + 1)
                act.activation(xsq[0:r, :], S["xtok"][0:r, t, :], ACT.Square,
                               accum_out=ss[0:r, t:t + 1]).then_inc(ssq, 1)
                act.drain()

        @block.vector
        def _(v):
            v.wait_ge(ye_in, 96)
            for t, r in enumerate(ROWS):
                v.tensor_scalar(ye[0:r, t, 0, :], ye[0:r, t, 0, :], S["topw"][0:r, t, 0:1], None, ALU.mult)
                v.drain()
                v.scalar_tensor_tensor(ye[0:r, t, 1, :], ye[0:r, t, 1, :], S["topw"][0:r, t, 1:2], ye[0:r, t, 0, :],
                                       ALU.mult, ALU.add)
                v.drain()
                v.tensor_tensor(S["xtok"][0:r, t, :], S["xtok"][0:r, t, :], ye[0:r, t, 1, :], ALU.add).then_inc(h_ok, 1)
            v.wait_ge(g_in, 16)
            for t, r in enumerate(ROWS):
                v.wait_ge(rs_ok, 6 + t + 1)
                v.scalar_tensor_tensor(out[0:r, t, :], S["xtok"][0:r, t, :], ss[0:r, t:t + 1], fg[0:r, :], ALU.mult,
                                       ALU.mult).then_inc(out_ok, 1)


def build_layer(nc, A):
    with ExitStack() as ctx:
        S = {}

        def sem(name):
            return ctx.enter_context(nc.semaphore(name))

        def sb(name, shape, dt=F32, stack=ctx):
            S[name] = stack.enter_context(nc.sbuf_tensor(name, shape, dt))

        for name, shape in (("ident", [P, P]), ("ones", [P, P]), ("mhalf", [P, 4]), ("gcol", [P, 32]),
                            ("xtok", [P, 3, D]), ("yT", [P, 16, T]), ("topw", [P, 3, 2]), ("slot", [P, 3, 2]),
                            ("iota", [P, BLK])):
            sb(name, shape)
        sb("slot_i", [P, 3, 2], U32)
        sb("blk_e", [1, NBLK + 1], I32)
        S["hn"] = S["yT"][:, :, :].rearrange("p k t -> p (k t)")[:, 0:3 * D].rearrange("p (t d) -> p t d", t=3)
        S["ydram"] = nc.dram_tensor("expert_rows", [SLOTS, D], F32, kind="Internal").ap()
        for name in ("pool_passed", "row_squares_ok", "row_rstd_ok"):
            S[name] = sem(name)
        with ExitStack() as front:
            for name, shape in (
                    ("tri_le", [P, P]), ("tri_gt", [P, P]), ("tri_le2", [80, 80]), ("tri_gt2", [80, 80]),
                    ("tailrow", [80, P]), ("seg8", [NS, 8]), ("mask_d", [P, 256]), ("mask_t", [16, 336]),
                    ("self01", [NS, NSEQ, P]), ("conv_wh", [P, 4, 32]), ("conv_bh", [P, 32]),
                    ("sc_t", [P, NSEQ, 3, 32]), ("xnT", [P, KT, T]), ("k", [P, 3, 256]), ("v", [P, 3, 256]),
                    ("kT", [P, 2, T]), ("lf", [P, 3, 16]), ("c_q", [P, 3, 16]), ("ncT", [16, T]),
                    ("lf_rep", [NS, 16, 8]), ("dt", [P, 3, 32]), ("dta", [P, 3, 32]), ("eac", [P, 3, 32]),
                    ("w_end", [P, 3, 32]), ("dec", [P, 3, 32]), ("dec_s", [P, 16, 8]), ("dskip", [P, 32])):
                sb(name, shape, stack=front)
            S["hnT"] = S["xnT"]
            setup_phase(nc, A, S, sem)
            ssd_phase(nc, A, S, sem)
            sb("oT", [P, 8, T], stack=front)
            attention_phase(nc, A, S, sem)
            sb("lg", [P, 3, 36], stack=front)
            sb("rbias", [P, 36], stack=front)
            merge_phase(nc, A, S, sem)
            route_phase(nc, A, S, sem)
        moe_phase(nc, A, S, sem)
        final_phase(nc, A, S, sem)


_INS = ['x_prompt', 'x_sample', 'cache_k', 'cache_v', 'cache_logf', 'state_ssm', 'state_conv', 'page_table',
        'meta_tokens', 'norm1_g', 'w_in', 'conv_w', 'conv_b', 'dt_bias', 'a_log', 'd_skip', 'ssd_norm_g',
        'b_forget', 'w_ssd_br', 'w_attn_br', 'w_out', 'norm2_g', 'w_router_group', 'b_router_group',
        'w_router_expert', 'b_router_expert', 'w_exp_gate', 'w_exp_up', 'w_exp_down', 'final_norm_g']
_OUTS = [("y_p", (1, 256, 1024)), ("y_s", (8, 8, 1024)), ("k_p", (1, 1, 272, 4, 64)), ("v_p", (1, 1, 272, 4, 64)),
         ("lf_p", (1, 1, 272, 16)), ("ssm_p", (1, 1, 32, 64, 128)), ("conv_p", (1, 1, 3, 4096)),
         ("k_s", (1, 8, 8, 4, 64)), ("v_s", (1, 8, 8, 4, 64)), ("lf_s", (1, 8, 8, 16)),
         ("ssm_s", (1, 8, 32, 64, 128)), ("conv_s", (1, 8, 3, 4096))]


def kernel(**inputs):
    import numpy as _np
    import concourse.bacc as _bacc
    from concourse import mybir as _mybir
    from concourse.bass_utils import run_bass_kernel_spmd as _run

    nc = _bacc.Bacc("TRN2", target_bir_lowering=False, num_devices=1)
    arrays, aps = {}, {}
    for name in _INS:
        a = _np.ascontiguousarray(inputs[name])
        arrays[f"in_{name}"] = a
        aps[name] = nc.dram_tensor(f"in_{name}", a.shape, _mybir.dt.from_np(a.dtype), kind="ExternalInput").ap()
    for name, shape in _OUTS:
        aps[name] = nc.dram_tensor(f"out_{name}", shape, _mybir.dt.float32, kind="ExternalOutput").ap()
    build_layer(nc, aps)
    r = _run(nc, [arrays], core_ids=[0])
    return tuple(r.results[0][f"out_{name}"] for name, _ in _OUTS)
```

```python
import concourse.bass as bass
from concourse import mybir
from contextlib import ExitStack

F32 = mybir.dt.float32
I32 = mybir.dt.int32
U32 = mybir.dt.uint32
ALU = mybir.AluOpType
ACT = mybir.ActivationFunctionType
AX = mybir.AxisListType

P = 128
D = 1024
KT = D // P
N_META = 16
SEQ = 256
LP = SEQ + N_META
NSEQ = 8
NEW = 8
NS = NSEQ * NEW
T = LP + NS
ROWS = [128, 128, 80]
COL = [0, 128, 256]
TAIL = LP - 256
TAIL_COL = 320
D_INNER = 2048
HP = 64
NH = 32
G = 8
N = 128
CONV_DIM = 4096
AH = 16
KVH = 4
HD = 64
PAST = 1024
PAGE = 128
NPG = PAST // PAGE
POOL = 80
C_Z, C_X, C_DT, C_Q, C_K, C_F, C_GS = 0, 2048, 6144, 6176, 7200, 7712, 7728
C_B = C_X + D_INNER
C_C = C_B + G * N
EPS = 1e-6
NEG = -1e30
NE = 32
DE = 512
BLK = 64
NBLK = NE + (2 * T) // BLK
SLOTS = NBLK * BLK
LEAST_BLK = 2 * T // BLK // 2 * 2


def bc(ap, shape):
    return ap.to_broadcast(list(shape))


def setup_phase(nc, A, S, sem):
    with ExitStack() as ctx:
        def tsb(name, shape, dt=F32):
            return ctx.enter_context(nc.sbuf_tensor(name, shape, dt))

        rows64 = tsb("param_rows", [64, P])
        convw_rows = tsb("convw_rows", [P, P])
        sc_rows = tsb("sc_rows", [P, 6, P])
        brow = tsb("brow", [P, 112])
        w_dt = tsb("w_dt", [P, KT, 32])
        w_kvf = tsb("w_kvf", [P, KT, 528])
        xsq = tsb("xsq", [P, D])
        xn = tsb("xn", [P, 3, D])
        ss = tsb("ss", [P, 4])
        small = tsb("small", [P, 3, 48])
        sp_e = tsb("sp_e", [P, 3, 48])
        sp_w = tsb("sp_w", [P, 3, 48])
        sp_l = tsb("sp_l", [P, 3, 48])
        sp_d = tsb("sp_d", [P, 3, 48])
        sp_z = tsb("sp_z", [P, 3, 48])
        dta_rep = tsb("dta_rep", [NS, NH, HP])
        a_neg = tsb("a_neg", [P, 32])
        ps = [ctx.enter_context(nc.psum_tensor(f"ps{i}", [P, 512], F32)) for i in range(8)]
        x_in, par_in, w_in_ready, kv_out = sem("x_in"), sem("par_in"), sem("small_w_in"), sem("kv_out")
        consts, xn_ok, tr_ps, tr_ev = sem("consts"), sem("xn_ok"), sem("tr_ps"), sem("tr_ev")
        par_ps, par_ev = sem("par_ps"), sem("par_ev")
        ssq, rstd_ok = S["row_squares_ok"], S["row_rstd_ok"]
        dt_ps, kv_ps, dtf_ev, ab_exp, sp_exp, sp_ln = (sem("dt_ps"), sem("kv_ps"), sem("dtf_ev"), sem("ab_exp"),
                                                       sem("sp_exp"), sem("sp_ln"))
        dt_ok, kv_ev, cum_ps, cum_ev, kt_ps = (sem("dt_ok"), sem("kv_ev"), sem("cum_ps"), sem("cum_ev"),
                                               sem("kt_ps"))
        win = A["w_in"].rearrange("a (t p) c -> p (a t) c", p=P)
        block = ctx.enter_context(nc.Block())

        @block.sync
        def _(sp):
            xp = A["x_prompt"].rearrange("a s d -> (a s) d")
            sp.dma_start(S["xtok"][0:16, 0, :], A["meta_tokens"]).then_inc(x_in, 16)
            sp.dma_start(S["xtok"][16:128, 0, :], xp[0:112, :]).then_inc(x_in, 16)
            sp.dma_start(S["xtok"][:, 1, :], xp[112:240, :]).then_inc(x_in, 16)
            sp.dma_start(S["xtok"][0:64, 2, :], A["x_sample"].rearrange("a s d -> (a s) d")).then_inc(x_in, 16)
            sp.dma_start(S["xtok"][64:80, 2, :], xp[240:256, :]).then_inc(x_in, 16)
            sp.dma_start(w_dt[:, :, :], win[:, :, C_DT:C_DT + 32]).then_inc(w_in_ready, 16)
            sp.dma_start(w_kvf[:, :, :], win[:, :, C_K:C_K + 528]).then_inc(w_in_ready, 16)
            sp.wait_ge(w_in_ready, 32)
            load_group_channels(sp, A, S, 0)
            load_group_z(sp, A, S, 0)
            sp.wait_ge(kv_ev, 6)
            for src, op, os in (("k", "k_p", "k_s"), ("v", "v_p", "v_s")):
                o = A[op].rearrange("a b l g d -> (a b l) (g d)")
                sp.dma_start(o[0:256, :].rearrange("(t p) c -> p t c", p=P), S[src][:, 0:2, :]).then_inc(kv_out, 16)
                sp.dma_start(o[256:272, :], S[src][64:80, 2, :]).then_inc(kv_out, 16)
                sp.dma_start(A[os].rearrange("a b l g d -> (a b l) (g d)"), S[src][0:64, 2, :]).then_inc(kv_out, 16)
            sp.wait_ge(dt_ok, 1)
            o = A["lf_p"].rearrange("a b l h -> (a b l) h")
            sp.dma_start(o[0:256, :].rearrange("(t p) c -> p t c", p=P), S["lf"][:, 0:2, :]).then_inc(kv_out, 16)
            sp.dma_start(o[256:272, :], S["lf"][64:80, 2, :]).then_inc(kv_out, 16)
            sp.dma_start(A["lf_s"].rearrange("a b l h -> (a b l) h"), S["lf"][0:64, 2, :]).then_inc(kv_out, 16)
            sp.wait_ge(kv_out, 144)

        @block.gpsimd
        def _(pool):
            pool.memset(S["ident"][:, :], 0.0)
            pool.memset(S["ones"][:, :], 1.0)
            pool.memset(S["mhalf"][:, :], -0.5)
            pool.memset(S["tri_le"][:, :], 1.0)
            pool.memset(S["tri_gt"][:, :], 1.0)
            pool.memset(S["tri_le2"][:, :], 1.0)
            pool.memset(S["tri_gt2"][:, :], 1.0)
            pool.memset(S["tailrow"][:, :], 0.0)
            pool.memset(S["seg8"][:, :], 1.0)
            pool.drain()
            pool.memset(S["tailrow"][64:80, :], 1.0)
            pool.drain()

            def keep(t, pattern, base, cm, fill=0.0, op=ALU.is_ge):
                pool.affine_select(out=t, in_=t, pattern=pattern, compare_op=op, fill=fill, base=base,
                                   channel_multiplier=cm)

            keep(S["ident"][:, :], [[-1, P]], 0, 1, fill=1.0, op=ALU.not_equal)
            keep(S["tri_le"][:, :], [[1, P]], 0, -1)
            keep(S["tri_gt"][:, :], [[-1, P]], -1, 1)
            keep(S["tri_le2"][:, :], [[1, 80]], 0, -1)
            keep(S["tri_gt2"][:, :], [[-1, 80]], -1, 1)
            keep(S["seg8"][:, :], [[-8, 8]], 0, 1)
            pool.drain()
            v8 = S["tri_le2"][:, 0:64].rearrange("k (s j) -> k s j", j=8)
            keep(v8, [[-8, 8], [0, 8]], 0, 1)
            keep(S["tri_le2"][:, 64:80], [[0, 16]], -64, 1)
            keep(S["tri_gt2"][:, 0:64].rearrange("k (s j) -> k s j", j=8), [[8, 8], [0, 8]], 7, -1)
            keep(S["seg8"][:, :], [[8, 8]], 7, -1)
            pool.drain()
            pool.memset(S["mask_d"][:, :], 0.0)
            pool.memset(S["mask_t"][:, :], 0.0)
            pool.drain()
            keep(S["mask_d"][:, 128:256], [[-1, P]], 0, 1, fill=NEG)
            pool.memset(S["mask_t"][:, 256:320], NEG)
            keep(S["mask_t"][:, 320:336], [[-1, 16]], 0, 1, fill=NEG)
            pool.memset(S["self01"][:, :, :], 1.0)
            pool.drain()
            m4 = S["self01"][:, :, :].rearrange("k s (h q) -> k s h q", q=8)
            keep(m4, [[8, 8], [0, 16], [1, 8]], 0, -1)
            pool.drain()
            keep(m4, [[-8, 8], [0, 16], [0, 8]], 0, 1)
            pool.drain()
            pool.memset(ss[:, 3:4], 1.0).then_inc(consts, 1)
            for t, r in enumerate(ROWS):
                pool.wait_ge(ssq, t + 1)
                pool.tensor_scalar(ss[0:r, t:t + 1], ss[0:r, t:t + 1], 1.0 / D, EPS, ALU.mult, ALU.add)
                pool.drain()
                pool.tensor_tensor(ss[0:r, t:t + 1], ss[0:r, t:t + 1], S["mhalf"][0:r, 0:1], ALU.pow).then_inc(rstd_ok, 1)

        @block.scalar
        def _(act):
            act.dma_start(rows64[0:32, :], A["conv_b"].rearrange("a (t p) -> (a t) p", p=P)).then_inc(par_in, 16)
            act.dma_start(rows64[32:48, :], A["ssd_norm_g"].rearrange("a (t p) -> (a t) p", p=P)).then_inc(par_in, 16)
            act.dma_start(rows64[48:56, :], A["norm1_g"].rearrange("a (t p) -> (a t) p", p=P)).then_inc(par_in, 16)
            act.dma_start(rows64[56:64, :], A["norm2_g"].rearrange("a (t p) -> (a t) p", p=P)).then_inc(par_in, 16)
            act.dma_start(convw_rows[:, :], A["conv_w"].rearrange("a w (t p) -> (a w t) p", p=P)).then_inc(par_in, 16)
            act.dma_start(sc_rows[:, :, :], A["state_conv"].rearrange("a s w (t p) -> (a s w t) p", p=P)
                          .rearrange("(r q) p -> q r p", q=P)).then_inc(par_in, 16)
            for i, (n, w) in enumerate((("dt_bias", 32), ("a_log", 32), ("d_skip", 32), ("b_forget", 16))):
                act.dma_start(brow[:, 32 * i:32 * i + w], A[n][0, :].partition_broadcast(P)).then_inc(par_in, 16)
            act.wait_ge(x_in, 80)
            for t, r in enumerate(ROWS):
                act.activation(xsq[0:r, :], S["xtok"][0:r, t, :], ACT.Square,
                               accum_out=ss[0:r, t:t + 1]).then_inc(ssq, 1)
                act.drain()
            act.wait_ge(par_in, 160)
            act.activation(a_neg[:, :], brow[:, 32:64], ACT.Exp).then_inc(ab_exp, 1)
            act.wait_ge(dtf_ev, 1)
            act.activation(sp_e[:, :, :], sp_z[:, :, :], ACT.Exp, scale=-1.0).then_inc(sp_exp, 1)
            act.wait_ge(dtf_ev, 2)
            act.activation(sp_l[:, :, :], sp_w[:, :, :], ACT.Ln).then_inc(sp_ln, 1)
            act.wait_ge(cum_ps, 1)
            for t, r in enumerate(ROWS):
                act.activation(S["eac"][0:r, t, :], ps[0][0:r, 32 * t:32 * t + 32], ACT.Exp)
                act.activation(S["w_end"][0:r, t, :], ps[1][0:r, 32 * t:32 * t + 32], ACT.Exp)
                act.activation(S["dec"][:, t, :], ps[2][:, 32 * t:32 * t + 32], ACT.Exp).then_inc(cum_ev, 1)
            act.wait_ge(cum_ps, 2)
            act.activation(S["dec_s"][:, :, :], ps[3][:, 0:128].rearrange("p (a s) -> p a s", s=8),
                           ACT.Exp).then_inc(cum_ev, 1)

        @block.vector
        def _(v):
            v.wait_ge(consts, 1)
            v.memset(small[:, :, :], 0.0).then_inc(consts, 1)
            for t, r in enumerate(ROWS):
                v.wait_ge(rstd_ok, t + 1)
                v.tensor_scalar(xn[0:r, t, :], S["xtok"][0:r, t, :], ss[0:r, t:t + 1], None,
                                ALU.mult).then_inc(xn_ok, 1)
            v.wait_ge(par_ps, 2)
            v.tensor_scalar(S["conv_bh"][:, :], ps[6][:, 0:32], 0.5, None, ALU.mult)
            v.tensor_copy(S["gcol"][:, :], ps[6][:, 32:64])
            v.tensor_scalar(S["conv_wh"][:, :, :], ps[6][:, 64:192].rearrange("p (w t) -> p w t", w=4), 0.5, None,
                            ALU.mult).then_inc(par_ev, 1)
            scv = S["sc_t"][:, :, :, :].rearrange("p s w t -> p (s w t)")
            v.tensor_copy(scv[:, 0:512], ps[7][:, :])
            v.tensor_copy(scv[:, 512:768], ps[6][:, 192:448]).then_inc(par_ev, 1)
            v.drain()
            for t, r in enumerate(ROWS):
                for h in range(2):
                    v.wait_ge(tr_ps, 2 * t + h + 1)
                    v.tensor_tensor(S["xnT"][:, 4 * h:4 * h + 4, COL[t]:COL[t] + r],
                                    ps[2 * (t % 2) + h][:, :].rearrange("p (k c) -> p k c", c=P)[:, :, 0:r],
                                    bc(S["gcol"][:, 16 + 4 * h:20 + 4 * h].unsqueeze(2), [P, 4, r]),
                                    ALU.mult).then_inc(tr_ev, 1)
            for t, r in enumerate(ROWS):
                v.wait_ge(kv_ps, t + 1)
                v.tensor_copy(S["k"][0:r, t, :], ps[4 + t][0:r, 0:256]).then_inc(kv_ev, 1)
                v.tensor_copy(S["v"][0:r, t, :], ps[4 + t][0:r, 256:512]).then_inc(kv_ev, 1)
            v.wait_ge(dt_ps, 1)
            v.wait_ge(par_in, 160)
            for t, r in enumerate(ROWS):
                v.tensor_tensor(small[0:r, t, 0:32], ps[0][0:r, 64 * t:64 * t + 32], brow[0:r, 0:32], ALU.add)
                v.tensor_tensor(small[0:r, t, 32:48], ps[0][0:r, 64 * t + 32:64 * t + 48], brow[0:r, 96:112], ALU.add)
            v.drain()
            v.tensor_scalar(small[:, :, 32:48], small[:, :, 32:48], -1.0, None, ALU.mult)
            v.drain()
            v.scalar_tensor_tensor(sp_z[:, :, :], small[:, :, :], -1.0, small[:, :, :], ALU.mult,
                                   ALU.max).then_inc(dtf_ev, 1)
            v.wait_ge(sp_exp, 1)
            v.tensor_scalar(sp_w[:, :, :], sp_e[:, :, :], 1.0, None, ALU.add).then_inc(dtf_ev, 1)
            v.drain()
            v.tensor_scalar(sp_d[:, :, :], sp_w[:, :, :], 1.0, 1e-30, ALU.subtract, ALU.max)
            v.drain()
            v.reciprocal(sp_d[:, :, :], sp_d[:, :, :])
            v.tensor_scalar(sp_z[:, :, :], sp_w[:, :, :], 1.0, None, ALU.is_equal)
            v.drain()
            v.wait_ge(sp_ln, 1)
            v.tensor_tensor(sp_l[:, :, :], sp_l[:, :, :], sp_d[:, :, :], ALU.mult)
            v.drain()
            v.tensor_tensor(sp_l[:, :, :], sp_l[:, :, :], sp_z[:, :, :], ALU.add)
            v.drain()
            v.tensor_tensor(sp_l[:, :, :], sp_l[:, :, :], sp_e[:, :, :], ALU.mult)
            v.tensor_scalar(small[:, :, :], small[:, :, :], 0.0, None, ALU.max)
            v.drain()
            v.tensor_tensor(small[:, :, :], small[:, :, :], sp_l[:, :, :], ALU.add)
            v.drain()
            v.tensor_scalar(S["lf"][:, :, :], small[:, :, 32:48], -1.0, None, ALU.mult).then_inc(dt_ok, 1)
            v.tensor_copy(S["dt"][:, :, :], small[:, :, 0:32])
            v.tensor_copy(S["dskip"][:, :], brow[:, 64:96])
            v.wait_ge(ab_exp, 1)
            v.scalar_tensor_tensor(S["dta"][:, :, :], small[:, :, 0:32], -1.0,
                                   bc(a_neg[:, :].unsqueeze(1), [P, 3, 32]), ALU.mult, ALU.mult)
            v.drain()
            v.tensor_copy(dta_rep[:, :, :], bc(S["dta"][0:NS, 2, :].unsqueeze(2), [NS, NH, HP])).then_inc(dt_ok, 1)
            v.wait_ge(cum_ps, 3)
            v.tensor_copy(S["c_q"][:, 0:2, :], ps[7][:, 128:160].rearrange("p (t h) -> p t h", t=2))
            v.tensor_copy(S["c_q"][0:16, 2, :], ps[7][0:16, 160:176])
            v.tensor_scalar(S["ncT"][:, :], ps[4][0:16, 0:336], -1.0, None, ALU.mult)
            v.tensor_copy(S["lf_rep"][:, :, :], bc(S["lf"][0:64, 2, :].unsqueeze(2), [64, 16, 8]))
            v.wait_ge(kt_ps, 1)
            for p in range(2):
                v.tensor_copy(S["kT"][:, p, :], ps[5 + p][:, 0:336])
            v.wait_ge(cum_ev, 3)
            for t, r in enumerate(ROWS):
                v.tensor_tensor(S["w_end"][0:r, t, :], S["w_end"][0:r, t, :], S["dt"][0:r, t, :], ALU.mult)

        @block.tensor
        def _(pe):
            pe.wait_ge(consts, 1)
            pe.wait_ge(par_in, 160)
            pe.transpose(ps[6][:, 0:64], rows64[:, :], S["ident"][0:64, 0:64])
            pe.transpose(ps[6][:, 64:192], convw_rows[:, :], S["ident"][:, :]).then_inc(par_ps, 1)
            for i in range(6):
                o = ps[7][:, P * i:P * i + P] if i < 4 else ps[6][:, 192 + P * (i - 4):320 + P * (i - 4)]
                mm = pe.transpose(o, sc_rows[:, i, :], S["ident"][:, :])
            mm.then_inc(par_ps, 1)
            for t, r in enumerate(ROWS):
                pe.wait_ge(xn_ok, t + 1)
                if t == 2:
                    pe.wait_ge(tr_ev, 2)
                for h in range(2):
                    for k in range(4):
                        mm = pe.transpose(ps[2 * (t % 2) + h][:, P * k:P * k + r],
                                          xn[0:r, t, P * (4 * h + k):P * (4 * h + k + 1)], S["ident"][0:r, 0:r])
                    mm.then_inc(tr_ps, 1)
            pe.wait_ge(w_in_ready, 32)
            pe.wait_ge(tr_ev, 6)
            pe.wait_ge(par_ev, 2)
            for t, r in enumerate(ROWS):
                for k in range(KT):
                    mm = pe.matmul(ps[4 + t][0:r, :], S["xnT"][:, k, COL[t]:COL[t] + r], w_kvf[:, k, 0:512],
                                   start=(k == 0), stop=(k == KT - 1))
                mm.then_inc(kv_ps, 1)
                for w, c0, c1 in ((w_dt, 0, 32), (w_kvf, 512, 528)):
                    o = 64 * t + (0 if w is w_dt else 32)
                    for k in range(KT):
                        mm = pe.matmul(ps[0][0:r, o:o + c1 - c0], S["xnT"][:, k, COL[t]:COL[t] + r],
                                       w[:, k, c0:c1], start=(k == 0), stop=(k == KT - 1))
            mm.then_inc(dt_ps, 1)
            pe.wait_ge(dt_ok, 2)
            le = [S["tri_le"], S["tri_le"], S["tri_le2"]]
            gt = [S["tri_gt"], S["tri_gt"], S["tri_gt2"]]
            tot = [S["ones"], S["ones"], S["tailrow"]]
            for t, r in enumerate(ROWS):
                da = S["dta"][0:r, t, :]
                pe.matmul(ps[0][0:r, 32 * t:32 * t + 32], le[t][0:r, 0:r], da, start=True, stop=True)
                pe.matmul(ps[1][0:r, 32 * t:32 * t + 32], gt[t][0:r, 0:r], da, start=True, stop=True)
                mm = pe.matmul(ps[2][:, 32 * t:32 * t + 32], tot[t][0:r, :], da, start=True, stop=True)
            mm.then_inc(cum_ps, 1)
            for a in range(16):
                mm = pe.matmul(ps[3][:, 8 * a:8 * a + 8], dta_rep[:, 2 * a:2 * a + 2, :], S["seg8"][:, :],
                               start=True, stop=True)
            mm.then_inc(cum_ps, 1)
            lf = S["lf"]
            o = ps[7]
            pe.matmul(o[:, 128:144], S["tri_le"][:, :], lf[:, 0, :], start=True, stop=True)
            pe.matmul(o[:, 144:160], S["ones"][:, :], lf[:, 0, :], start=True, stop=False)
            pe.matmul(o[:, 144:160], S["tri_le"][:, :], lf[:, 1, :], start=False, stop=True)
            pe.matmul(o[0:16, 160:176], S["ones"][:, 0:16], lf[:, 0, :], start=True, stop=False)
            pe.matmul(o[0:16, 160:176], S["ones"][:, 0:16], lf[:, 1, :], start=False, stop=False)
            pe.matmul(o[0:16, 160:176], S["tri_le2"][:, 64:80], lf[0:80, 2, :], start=False, stop=True)
            pe.wait_ge(kv_ev, 2)
            o = ps[4][0:16, :]
            pe.matmul(o[:, 0:128], lf[:, 0, :], S["tri_le"][:, :], start=True, stop=True)
            pe.matmul(o[:, 128:256], lf[:, 0, :], S["ones"][:, :], start=True, stop=False)
            pe.matmul(o[:, 128:256], lf[:, 1, :], S["tri_le"][:, :], start=False, stop=True)
            pe.matmul(o[:, 256:336], lf[:, 0, :], S["ones"][:, 0:80], start=True, stop=False)
            pe.matmul(o[:, 256:336], lf[:, 1, :], S["ones"][:, 0:80], start=False, stop=False)
            pe.matmul(o[:, 256:336], lf[0:80, 2, :], S["tri_le2"][:, :], start=False, stop=True).then_inc(cum_ps, 1)
            pe.wait_ge(kv_ev, 6)
            for p in range(2):
                for t, r in enumerate(ROWS):
                    mm = pe.transpose(ps[5 + p][:, COL[t]:COL[t] + r], S["k"][0:r, t, P * p:P * p + P],
                                      S["ident"][0:r, 0:r])
            mm.then_inc(kt_ps, 1)


def ssd_phase(nc, A, S, sem):
    with ExitStack() as ctx:
        def tsb(name, shape, dt=F32):
            return ctx.enter_context(nc.sbuf_tensor(name, shape, dt))

        wg = S["w_group"]
        zt, zz = tsb("z_tanh", [P, 3, 256]), tsb("z_gate", [P, 3, 256])
        xp = tsb("x_padded", [P, 4, 363])
        xc, xt = tsb("x_conv", [P, 4, 360]), tsb("x_tanh", [P, 4, 360])
        xs = tsb("x_silu", [P, 4, 360])
        xs2 = tsb("x_tile2", [P, 4, 80])
        tok = tsb("x_b_rows", [P, 3, 384])
        h0 = tsb("h0", [P, 2, NSEQ, N])
        h0t = tsb("h0_t", [P, NSEQ, 256])
        cx = tsb("c_spread", [P, 9, 80])
        r4, e4 = tsb("dta_tri", [P, 3, 512]), tsb("decay", [P, 3, 512])
        cbm = tsb("cb_masked", [P, 3, P])
        xdt, xw, dx = tsb("x_dt", [P, 3, 256]), tsb("x_wend", [P, 3, 256]), tsb("x_skip", [P, 3, 256])
        bm = tsb("b_by_seq", [NS, NSEQ, N])
        hp = tsb("h_prompt", [P, 3, 256])
        hpo = tsb("h_prompt_out", [P, 2, N])
        hso = tsb("h_sample_out", [P, 2, NSEQ, N])
        yo, y = tsb("y_off", [P, 3, 256]), tsb("y_rows", [P, 3, 256])
        ysq, yss, cv_p, cv_s = (tsb("y_sq", [P, 256]), tsb("y_ss", [P, 3]), tsb("conv_p_t", [P, 3, 32]),
                                tsb("conv_s_t", [P, NSEQ, 3, 32]))
        cvo = xt[:, :, :].rearrange("p m c -> p (m c)")[:, 0:7 * P].rearrange("p (a n) -> p a n", n=P)
        ps = [ctx.enter_context(nc.psum_tensor(f"psg{i}", [P, 512], F32)) for i in range(8)]
        wf_in, wz_in, h0_in = S["w_channels_in"], S["w_z_in"], sem("h0_in")
        z_ps, z_th, z_ev, f_ps, f_ev, f_pad, tap0, taps, f_th, silu, compact = (
            sem(n) for n in ("z_ps", "z_th", "z_ev", "f_ps", "f_ev", "f_pad", "tap0", "taps", "f_th", "silu",
                             "compact"))
        tok_ps, tok_ev, r4_ok, seg_ps, e4_ok, cb_ps, cbm_ok, m_ok, x_ok, b_ok = (
            sem(n) for n in ("tok_ps", "tok_ev", "r4_ok", "seg_ps", "e4_ok", "cb_ps", "cbm_ok", "m_ok", "x_ok",
                             "b_ok"))
        ht_ps, ht_ev, st_ps, hp_ok, y_ps, y_raw, y_sqd, y_rs, y_n, yt_ps, yt_ev = (
            sem(n) for n in ("ht_ps", "ht_ev", "st_ps", "hp_ok", "y_ps", "y_raw", "y_sqd", "y_rs", "y_n", "yt_ps",
                             "yt_ev"))
        hs_ps, hs_ev, hf_ps, hf_ev, states_sent, cv_ps, cv_ev, cv_sent = (
            sem(n) for n in ("hs_ps", "hs_ev", "hf_ps", "hf_ev", "states_sent", "cv_ps", "cv_ev", "cv_sent"))
        pool_passed = S["pool_passed"]
        zero_ok = sem("zero_ok")
        ssm_in = A["state_ssm"].rearrange("a s h p n -> (a s) (h p) n")
        ssm_s = A["ssm_s"].rearrange("a s h p n -> (a s) (h p) n")
        ssm_p = A["ssm_p"].rearrange("a b h p n -> (a b h p) n")
        le = [S["tri_le"], S["tri_le"], S["tri_le2"]]
        gt = [S["tri_gt"], S["tri_gt"], S["tri_gt2"]]
        block = ctx.enter_context(nc.Block())

        def tile_of(g, m):
            return [2 * g, 2 * g + 1, 16 + g, 24 + g][m]

        @block.sync
        def _(sp):
            sp.sem_inc(states_sent, 48)

            def load_h(g):
                for a in range(2):
                    sp.dma_start(h0[:, a, :, :], ssm_in[:, bass.ds(g * 256 + a * P, P), :]
                                 .rearrange("s q n -> q s n")).then_inc(h0_in, 16)

            def send_h(g):
                sp.wait_ge(hs_ev, 2 * g + 4)
                for a in range(2):
                    sp.dma_start(ssm_s[:, bass.ds(g * 256 + a * P, P), :].rearrange("s q n -> q s n"),
                                 hso[:, a, :, :]).then_inc(states_sent, 16)
                sp.dma_start(ssm_p[bass.ds(g * 256, 256), :].rearrange("(a q) n -> q a n", q=P),
                             hpo[:, :, :]).then_inc(states_sent, 16)

            load_h(0)
            with sp.Fori(1, G) as g:
                sp.wait_ge(f_ps, 4 * g)
                load_group_channels(sp, A, S, g)
                sp.wait_ge(z_ps, 3 * g)
                sp.sem_inc(pool_passed)
                load_group_z(sp, A, S, g)
                sp.wait_ge(hs_ev, 2 * g + 2)
                load_h(g)
                send_h(g - 1)
            send_h(G - 1)
            sp.wait_ge(cv_ev, 2)
            sp.dma_start(A["conv_p"].rearrange("a b w (t p) -> (a b w t) p", p=P), cvo[0:96, 6, :]).then_inc(cv_sent, 16)
            sp.dma_start(A["conv_s"].rearrange("a b w (t p) -> (a b w t) p", p=P)
                         .rearrange("(r q) p -> q r p", q=P), cvo[:, 0:6, :]).then_inc(cv_sent, 16)
            sp.wait_ge(cv_sent, 32)
            sp.wait_ge(states_sent, 48 * (G + 1))
            sp.wait_ge(wf_in, 48 * G)
            sp.wait_ge(wz_in, 16 * G)
            sp.wait_ge(h0_in, 32 * G)

        @block.gpsimd
        def _(pool):
            pool.memset(xp[:, :, 0:3], 0.0)
            pool.memset(cx[:, :, :], 0.0)
            pool.memset(hp[:, 0, :], 0.0)
            pool.drain()
            pool.memset(yss[:, :], 1.0).then_inc(zero_ok, 1)
            with pool.Fori(0, G) as g:
                for t, r in enumerate(ROWS):
                    pool.tensor_tensor(r4[0:r, t, :].rearrange("k (h i) -> k h i", h=4)[:, :, 0:r],
                                       bc(le[t][0:r, 0:r].unsqueeze(1), [r, 4, r]),
                                       bc(S["dta"][0:r, t, bass.ds(4 * g, 4)].unsqueeze(2), [r, 4, r]),
                                       ALU.mult).then_inc(r4_ok, 1)
                for m in range(4):
                    pool.tensor_copy(xp[:, m, 275:363].rearrange("p (s w) -> p s w", w=11)[:, :, 0:3],
                                     S["sc_t"][:, :, :, bass.ds(tile_of(g, m), 1)]
                                     .rearrange("p s w o -> p s (w o)")).then_inc(f_pad, 1)
                pool.wait_ge(f_ev, 4 * g + 4)
                pool.sem_inc(pool_passed)
                for m in range(4):
                    o = tile_of(g, m)
                    pool.tensor_copy(cv_p[:, :, bass.ds(o, 1)].rearrange("p w o -> p (w o)"), xp[:, m, 272:275])
                    pool.tensor_copy(cv_s[:, :, :, bass.ds(o, 1)].rearrange("p s w o -> p s (w o)"),
                                     xp[:, m, 275:363].rearrange("p (s w) -> p s w", w=11)[:, :, 8:11])
                pool.wait_ge(silu, g + 1)
                pool.sem_inc(pool_passed)
                pool.tensor_copy(xs2[:, :, 0:64].rearrange("p m (s j) -> p m s j", j=8),
                                 gapped(xs))
                pool.tensor_copy(xs2[:, :, 64:80], xs[:, :, 256:272]).then_inc(compact, 1)
                pool.drain()
                pool.tensor_copy(diag8(cx), xs2[:, 3, 0:64].rearrange("n (s j) -> n s j", j=8))
                pool.tensor_copy(cx[:, 8, 64:80], xs2[:, 3, 64:80]).then_inc(compact, 1)
                for t, r in enumerate(ROWS):
                    pool.wait_ge(tok_ev, 3 * g + t + 1)
                    x4 = tok[0:r, t, 0:256].rearrange("k (h p) -> k h p", h=4)
                    for dst, by in ((xdt, S["dt"][0:r, t, bass.ds(4 * g, 4)]),
                                    (xw, S["w_end"][0:r, t, bass.ds(4 * g, 4)]),
                                    (dx, S["dskip"][0:r, bass.ds(4 * g, 4)])):
                        i = pool.tensor_tensor(dst[0:r, t, :].rearrange("k (h p) -> k h p", h=4), x4,
                                               bc(by.unsqueeze(2), [r, 4, HP]), ALU.mult)
                    i.then_inc(x_ok, 1)
                pool.tensor_tensor(bm[:, :, :], bc(tok[0:64, 2, 256:384].unsqueeze(1), [NS, NSEQ, N]),
                                   bc(S["seg8"][:, :].unsqueeze(2), [NS, NSEQ, N]), ALU.mult).then_inc(b_ok, 1)
                for t, r in enumerate(ROWS):
                    pool.wait_ge(y_sqd, 3 * g + t + 1)
                    pool.sem_inc(pool_passed)
                    pool.tensor_scalar(yss[0:r, t:t + 1], yss[0:r, t:t + 1], 1.0 / 256, EPS, ALU.mult, ALU.add)
                    pool.drain()
                    pool.tensor_tensor(yss[0:r, t:t + 1], yss[0:r, t:t + 1], S["mhalf"][0:r, 0:1],
                                       ALU.pow).then_inc(y_rs, 1)

        @block.scalar
        def _(act):
            act.wait_ge(zero_ok, 1)

            def channels_out(g):
                for m in range(4):
                    act.wait_ge(f_ps, 4 * g + m + 1)
                    act.activation(xp[:, m, 3:259], ps[m][:, 0:256], ACT.Copy)
                    act.activation(xp[:, m, 259:275], ps[m][:, 320:336], ACT.Copy)
                    act.activation(xp[:, m, 275:363].rearrange("p (s w) -> p s w", w=11)[:, :, 3:11],
                                   ps[m][:, 256:320].rearrange("p (s j) -> p s j", j=8), ACT.Copy).then_inc(f_ev, 1)
                    act.drain()
                    act.wait_ge(f_pad, 4 * g + m + 1)
                    o = tile_of(g, m)
                    act.activation(xc[:, m, :], xp[:, m, 0:360], ACT.Identity,
                                   bias=S["conv_bh"][:, bass.ds(o, 1)],
                                   scale=S["conv_wh"][:, 0, bass.ds(o, 1)]).then_inc(tap0, 1)

            def chunks(g):
                act.wait_ge(taps, 4 * g + 4)
                act.activation(xt[:, :, :], xc[:, :, :], ACT.Tanh).then_inc(f_th, 1)
                for t, r in enumerate(ROWS):
                    act.wait_ge(z_ps, 3 * g + max(t + 1, 2))
                    src = ps[4 + t // 2][0:r, 256 * (t % 2):256 * (t % 2) + 256]
                    act.activation(zt[0:r, t, :], src, ACT.Tanh, scale=0.5).then_inc(z_th, 1)
                for t, r in enumerate(ROWS):
                    act.wait_ge(tok_ps, 3 * g + t + 1)
                    act.activation(tok[0:r, t, :], ps[t][0:r, 0:384], ACT.Copy).then_inc(tok_ev, 1)
                for t, r in enumerate(ROWS):
                    act.wait_ge(seg_ps, 3 * g + t + 1)
                    act.activation(e4[0:r, t, :].rearrange("k (h i) -> k h i", h=4)[:, :, 0:r],
                                   ps[4 + t][0:r, 0:4 * r].rearrange("k (h i) -> k h i", h=4),
                                   ACT.Exp).then_inc(e4_ok, 1)
                for b in range(4):
                    act.wait_ge(ht_ps, 4 * g + b + 1)
                    act.activation(h0t[:, 2 * b:2 * b + 2, :], ps[(b + 3) % 4][:, :], ACT.Copy).then_inc(ht_ev, 1)
                for t, r in enumerate(ROWS):
                    act.wait_ge(y_raw, 3 * g + t + 1)
                    act.activation(ysq[0:r, :], y[0:r, t, :], ACT.Square,
                                   accum_out=yss[0:r, t:t + 1]).then_inc(y_sqd, 1)
                    act.drain()

            def y_out(g):
                for h in range(2):
                    act.wait_ge(yt_ps, 2 * g + h + 1)
                    act.activation(S["yT"][:, bass.ds(2 * g + h, 1), :], ps[6 + h][:, 0:T].unsqueeze(1), ACT.Identity,
                                   scale=S["gcol"][:, bass.ds(2 * g + h, 1)]).then_inc(yt_ev, 1)

            channels_out(0)
            with act.Fori(0, G - 1) as g:
                chunks(g)
                channels_out(g + 1)
                y_out(g)
            chunks(G - 1)
            y_out(G - 1)

        @block.vector
        def _(v):
            v.sem_inc(hs_ev, 2)
            v.wait_ge(zero_ok, 1)
            with v.Fori(0, G) as g:
                for m in range(4):
                    o = tile_of(g, m)
                    v.wait_ge(tap0, 4 * g + m + 1)
                    for w in range(1, 4):
                        i = v.scalar_tensor_tensor(xc[:, m, :], xp[:, m, w:w + 360],
                                                   S["conv_wh"][:, w, bass.ds(o, 1)], xc[:, m, :], ALU.mult, ALU.add)
                        if w == 3:
                            i.then_inc(taps, 1)
                        v.drain()
                v.wait_ge(f_th, g + 1)
                v.scalar_tensor_tensor(xs[:, :, :], xt[:, :, :], 1.0, xc[:, :, :], ALU.add, ALU.mult).then_inc(silu, 1)
                for t, r in enumerate(ROWS):
                    v.wait_ge(z_th, 3 * g + max(t + 1, 2))
                    src = ps[4 + t // 2][0:r, 256 * (t % 2):256 * (t % 2) + 256]
                    v.scalar_tensor_tensor(zz[0:r, t, :], zt[0:r, t, :], 1.0, src, ALU.add,
                                           ALU.mult).then_inc(z_ev, 1)
                for t, r in enumerate(ROWS):
                    v.wait_ge(cb_ps, 3 * g + 3)
                    v.tensor_tensor(cbm[0:r, t, 0:r], ps[7][0:r, P * t:P * t + r], le[t][0:r, 0:r],
                                    ALU.mult).then_inc(cbm_ok, 1)
                v.drain()
                for t, r in enumerate(ROWS):
                    v.wait_ge(e4_ok, 3 * g + t + 1)
                    e = e4[0:r, t, :].rearrange("k (h i) -> k h i", h=4)[:, :, 0:r]
                    v.tensor_tensor(e, e, bc(cbm[0:r, t, 0:r].unsqueeze(1), [r, 4, r]), ALU.mult).then_inc(m_ok, 1)
                for t in range(3):
                    v.wait_ge(st_ps, 3 * g + max(t + 1, 2))
                    src = ps[7][:, 256 * t:256 * t + 256] if t < 2 else ps[3][:, 0:256]
                    if t == 0:
                        v.tensor_copy(hp[:, 0, :], src).then_inc(hp_ok, 1)
                        v.drain()
                    else:
                        v.tensor_tensor(hp[:, t, :].rearrange("n (h p) -> n h p", h=4),
                                        hp[:, t - 1, :].rearrange("n (h p) -> n h p", h=4),
                                        bc(S["dec"][:, t, bass.ds(4 * g, 4)].unsqueeze(2), [P, 4, HP]), ALU.mult)
                        v.drain()
                        v.tensor_tensor(hp[:, t, :], hp[:, t, :], src, ALU.add).then_inc(hp_ok, 1)
                        v.drain()
                for t, r in enumerate(ROWS):
                    v.wait_ge(y_ps, 3 * g + t + 1)
                    if t == 0:
                        v.tensor_tensor(y[0:r, t, :], ps[4 + t][0:r, 0:256], dx[0:r, t, :], ALU.add)
                    else:
                        v.tensor_tensor(yo[0:r, t, :].rearrange("k (h p) -> k h p", h=4),
                                        ps[4 + t][0:r, 256:512].rearrange("k (h p) -> k h p", h=4),
                                        bc(S["eac"][0:r, t, bass.ds(4 * g, 4)].unsqueeze(2), [r, 4, HP]), ALU.mult)
                        v.drain()
                        v.tensor_tensor(y[0:r, t, :], ps[4 + t][0:r, 0:256], yo[0:r, t, :], ALU.add)
                        v.drain()
                        v.tensor_tensor(y[0:r, t, :], y[0:r, t, :], dx[0:r, t, :], ALU.add)
                    v.drain()
                    v.scalar_tensor_tensor(y[0:r, t, :], y[0:r, t, :], 0.5, zz[0:r, t, :], ALU.mult,
                                           ALU.mult).then_inc(y_raw, 1)
                v.wait_ge(h0_in, 32 * g + 32)
                v.wait_ge(states_sent, 48 * g + 48)
                v.wait_ge(hf_ps, g + 1)
                v.tensor_copy(hpo[:, :, :], ps[3][:, 256:512].rearrange("p (a n) -> p a n", a=2)).then_inc(hf_ev, 1)
                for a in range(2):
                    v.tensor_tensor(hso[:, a, :, :], h0[:, a, :, :],
                                    bc(S["dec_s"][:, bass.ds(2 * g + a, 1), :].rearrange("p o s -> p (o s)")
                                       .unsqueeze(2), [P, NSEQ, N]), ALU.mult)
                    v.drain()
                    for b in range(2):
                        v.wait_ge(hs_ps, 4 * g + 2 * a + b + 1)
                        i = v.tensor_tensor(hso[:, a, 4 * b:4 * b + 4, :], hso[:, a, 4 * b:4 * b + 4, :],
                                            ps[(2 * a + b)][:, :].rearrange("p (s n) -> p s n", n=N), ALU.add)
                    i.then_inc(hs_ev, 1)
                for t, r in enumerate(ROWS):
                    v.wait_ge(y_rs, 3 * g + t + 1)
                    v.tensor_scalar(y[0:r, t, :], y[0:r, t, :], yss[0:r, t:t + 1], None, ALU.mult).then_inc(y_n, 1)
            v.wait_ge(cv_ps, 1)
            v.tensor_copy(cvo[:, 0:4, :], ps[0][:, :].rearrange("p (a n) -> p a n", n=P)).then_inc(cv_ev, 1)
            v.tensor_copy(cvo[:, 4:6, :], ps[1][:, 0:256].rearrange("p (a n) -> p a n", n=P))
            v.tensor_copy(cvo[0:96, 6, :], ps[1][0:96, 256:384]).then_inc(cv_ev, 1)

        @block.tensor
        def _(pe):
            idn = S["ident"]

            def channels(g):
                pe.wait_ge(wf_in, 48 * g + 48)
                for m in range(4):
                    if m % 2 == 0:
                        pe.wait_ge(hs_ev, 2 * g + m // 2 + 1)
                    for k in range(KT):
                        mm = pe.matmul(ps[m][:, 0:T], wg[:, k, P * m:P * m + P], S["xnT"][:, k, :],
                                       start=(k == 0), stop=(k == KT - 1))
                    mm.then_inc(f_ps, 1)

            def chunks(g):
                pe.wait_ge(wz_in, 16 * g + 16)
                for t, r in enumerate(ROWS):
                    for k in range(KT):
                        mm = pe.matmul(ps[4 + t // 2][0:r, 256 * (t % 2):256 * (t % 2) + 256],
                                       S["xnT"][:, k, COL[t]:COL[t] + r], wg[:, k, 512:768],
                                       start=(k == 0), stop=(k == KT - 1))
                    mm.then_inc(z_ps, 1)
                pe.wait_ge(f_ev, 4 * g + 4)
                pe.wait_ge(silu, g + 1)
                for t, r in enumerate(ROWS):
                    if t == 2:
                        pe.wait_ge(compact, 2 * g + 1)
                    for m in range(3):
                        src = xs[:, m, COL[t]:COL[t] + r] if t < 2 else xs2[:, m, :]
                        mm = pe.transpose(ps[t][0:r, P * m:P * m + P], src, idn[:, :])
                    mm.then_inc(tok_ps, 1)
                for t, r in enumerate(ROWS):
                    b_, c_ = ((xs[:, m, COL[t]:COL[t] + r] if t < 2 else xs2[:, m, :]) for m in (2, 3))
                    mm = pe.matmul(ps[7][0:r, P * t:P * t + r], b_, c_, start=True, stop=True)
                    mm.then_inc(cb_ps, 1)
                pe.wait_ge(z_ev, 3 * g + 3)
                for t, r in enumerate(ROWS):
                    pe.wait_ge(r4_ok, 3 * g + t + 1)
                    pe.matmul(ps[4 + t][0:r, 0:4 * r], gt[t][0:r, 0:r],
                              r4[0:r, t, :].rearrange("k (h i) -> k h i", h=4)[:, :, 0:r],
                              start=True, stop=True).then_inc(seg_ps, 1)
                pe.wait_ge(h0_in, 32 * g + 32)
                for b in range(4):
                    if b:
                        pe.wait_ge(tok_ev, 3 * g + b)
                    for s in (2 * b, 2 * b + 1):
                        for a in range(2):
                            o = 256 * (s % 2) + P * a
                            mm = pe.transpose(ps[(b + 3) % 4][:, o:o + P], h0[:, a, s, :], idn[:, :])
                    mm.then_inc(ht_ps, 1)
                pe.wait_ge(cbm_ok, 3 * g + 3)
                pe.wait_ge(ht_ev, 4 * g + 1)
                for t, r in enumerate(ROWS):
                    pe.wait_ge(x_ok, 3 * g + t + 1)
                    k0 = 64 if t == 2 else 0
                    o = ps[7][:, 256 * t:256 * t + 256] if t < 2 else ps[3][:, 0:256]
                    pe.matmul(o, tok[k0:r, t, 256:384], xw[k0:r, t, :], start=True, stop=True).then_inc(st_ps, 1)
                for t, r in enumerate(ROWS):
                    pe.wait_ge(m_ok, 3 * g + t + 1)
                    for h in range(4):
                        mm = pe.matmul(ps[4 + t][0:r, HP * h:HP * h + HP], e4[0:r, t, P * h:P * h + r],
                                       xdt[0:r, t, HP * h:HP * h + HP], start=True, stop=True)
                    if t == 1:
                        pe.wait_ge(hp_ok, 3 * g + 1)
                        mm = pe.matmul(ps[5][:, 256:512], xs[:, 3, P:2 * P], hp[:, 0, :], start=True, stop=True)
                    if t == 2:
                        pe.wait_ge(compact, 2 * g + 2)
                        pe.wait_ge(hp_ok, 3 * g + 2)
                        pe.wait_ge(ht_ev, 4 * g + 4)
                        pe.matmul(ps[6][64:80, 256:512], cx[:, 8, 64:80], hp[:, 1, :], start=True, stop=True)
                        for s in range(NSEQ // 2):
                            for q in range(2):
                                mm = pe.matmul(ps[6][32 * q:32 * q + 32, 256:512], cx[:, 4 * q + s, 32 * q:32 * q + 32],
                                               h0t[:, 4 * q + s, :], start=(s == 0), stop=(s == NSEQ // 2 - 1))
                    mm.then_inc(y_ps, 1)
                pe.wait_ge(hp_ok, 3 * g + 3)
                for a in range(2):
                    mm = pe.transpose(ps[3][:, 256 + P * a:256 + P * a + P], hp[:, 2, P * a:P * a + P], idn[:, :])
                mm.then_inc(hf_ps, 1)
                pe.wait_ge(b_ok, g + 1)
                for a in range(2):
                    for b in range(2):
                        if 2 * a + b == 3:
                            pe.wait_ge(hf_ev, g + 1)
                        q = slice(32 * b, 32 * b + 32)
                        pe.matmul(ps[2 * a + b][:, :], xw[q, 2, P * a:P * a + P], bm[q, 4 * b:4 * b + 4, :],
                                  start=True, stop=True).then_inc(hs_ps, 1)

            def turn_y(g):
                for h in range(2):
                    for t, r in enumerate(ROWS):
                        pe.wait_ge(y_n, 3 * g + t + 1)
                        mm = pe.transpose(ps[6 + h][:, COL[t]:COL[t] + r], y[0:r, t, P * h:P * h + P],
                                          idn[0:r, 0:r])
                    mm.then_inc(yt_ps, 1)

            channels(0)
            with pe.Fori(0, G - 1) as g:
                chunks(g)
                channels(g + 1)
                turn_y(g)
            chunks(G - 1)
            turn_y(G - 1)
            pe.wait_ge(yt_ev, 2 * G)
            for i in range(6):
                o = ps[i // 4][:, P * (i % 4):P * (i % 4) + P]
                pe.transpose(o, cv_s[:, :, :, :].rearrange("p s w t -> p (s w t)")[:, P * i:P * i + P], idn[:, :])
            pe.transpose(ps[1][0:96, 256:384], cv_p[:, :, :].rearrange("p w t -> p (w t)"),
                         idn[:, :]).then_inc(cv_ps, 1)


def load_group_channels(eng, A, S, g):
    win = A["w_in"].rearrange("a (t p) c -> p (a t) c", p=P)
    for d, c, w in ((0, C_X, 256), (256, C_B, 128), (384, C_C, 128)):
        eng.dma_start(S["w_group"][:, :, d:d + w], win[:, :, bass.ds(g * w + c, w)]).then_inc(S["w_channels_in"], 16)


def load_group_z(eng, A, S, g):
    win = A["w_in"].rearrange("a (t p) c -> p (a t) c", p=P)
    eng.dma_start(S["w_group"][:, :, 512:768], win[:, :, bass.ds(g * 256 + C_Z, 256)]).then_inc(S["w_z_in"], 16)


def gapped(xs):
    return xs[:, :, 272:360].rearrange("p m (s w) -> p m s w", w=11)[:, :, :, 3:11]


def diag8(cx):
    return cx[:, :, :].rearrange("n s c -> n (s c)")[:, 0:704].rearrange("n (s q) -> n s q", q=88)[:, :, 0:8]


def attention_phase(nc, A, S, sem):
    with ExitStack() as ctx:
        def tsb(name, shape, dt=F32):
            return ctx.enter_context(nc.sbuf_tensor(name, shape, dt))

        wq = tsb("w_q", [P, KT, 2, HD])
        qpad = tsb("q_pad", [P, 2, T])
        kx = tsb("k_and_c", [P, 2, 2, T])
        qblk = tsb("q_blocks", [P, NSEQ, 2, P])
        sc = tsb("scores", [P, 2, 3, T])
        nm, rs = tsb("neg_max", [P, 6]), tsb("row_sum", [P, 6])
        pt = tsb("p_t", [P, 2, 432])
        ptab = tsb("page_table", [1, NSEQ * NPG], I32)
        lfp = tsb("logf_pages", [P, NPG, NSEQ, 16])
        rall = tsb("r_past", [P, PAST])
        kpg, vpg = tsb("k_pages", [P, 2, NPG, 256]), tsb("v_pages", [P, 2, NPG, 256])
        kts = tsb("k_pages_t", [P, 2, PAST])
        selfneg = tsb("self_neg", [NS, NSEQ, P])
        ntri = tsb("neg_tri2", [NS, NS])
        qcur, mcur, scur, lcur = (tsb("q_cur", [P, 2, P]), tsb("mask_cur", [NS, P]), tsb("sel_cur", [P, P]),
                                  tsb("lf_cur", [NS, P]))
        pr = tsb("p_rows", [P, PAST + NS])
        pts, ptself = tsb("p_pages_t", [P, NPG, P]), tsb("p_self_t", [NS, P])
        mx, sm = tsb("maxes", [P, 8]), tsb("sums", [P, 4])
        oe = tsb("o_seq", [P, P])
        ps = [ctx.enter_context(nc.psum_tensor(f"psa{i}", [P, 512], F32)) for i in range(4)]
        psc = ctx.enter_context(nc.psum_tensor("psa_s", [P, 2, 512], F32))
        ps += [psc[:, 0, :], psc[:, 1, :]]
        ps += [ctx.enter_context(nc.psum_tensor(f"psa{i}", [P, 512], F32)) for i in (6, 7)]
        (wq_in, tab_in, lf_in, q_ps, q_ev, q_blk, pick_ok, s_ps, nm_ok, p_ok, pn_ok, pt_ps, pt_ev, o_ps,
         o_ev, kx_ok, zero_ok) = (sem(n) for n in (
             "wq_in", "tab_in", "lf_in", "q_ps", "q_ev", "q_blk", "pick_ok", "s_ps", "nm_ok",
             "p_ok", "p_normed", "pt_ps", "pt_ev", "o_ps", "o_ev", "kx_ok", "azero_ok"))
        (r_ps, r_ev, kt_ps2, kt_ev, kt_evb, cur_ok, ss_ps, m_ok2, e_ok, pp_ps, pp_ev, so_ps, so_ev, sot_ps,
         sot_ev) = (sem(n) for n in (
             "r_ps", "r_ev", "ktp_ps", "ktp_ev", "ktp_evb", "cur_ok", "ss_ps", "smax_ok", "sexp_ok", "pp_ps", "pp_ev",
             "so_ps", "so_ev", "sot_ps", "sot_ev"))
        cur_free = sem("cur_free")
        kv_half = [sem("kv_in_even"), sem("kv_in_odd")]
        blank, blank_out = S["mixT"].rearrange("p k t -> p (k t)")[:, 0:D], sem("blank_out")
        gate = S["pool_passed"]
        win = A["w_in"].rearrange("a (t p) c -> p (a t) c", p=P)
        ck = A["cache_k"].rearrange("a n s g d -> s (a n) (g d)")
        cv = A["cache_v"].rearrange("a n s g d -> s (a n) (g d)")
        cl = A["cache_logf"].rearrange("a n s h -> s (a n) h")
        idn = S["ident"]
        keys = [128, 256, T]
        qrows = [128, 128, TAIL]
        qcol = [0, 128, TAIL_COL]

        def head(t, g2):
            return (t // 4) * 8 + 4 * g2 + t % 4

        def score_bank(g2, t):
            b = ps[1 + 2 * g2] if t < 2 else ps[2 + 2 * g2]
            c = 128 if t == 1 else 0
            return b[0:qrows[t], c:c + keys[t]]

        block = ctx.enter_context(nc.Block())

        def load_wq(eng, t):
            for g2 in range(2):
                eng.dma_start(wq[:, :, g2, :], win[:, :, bass.ds(head(t, g2) * HD + C_Q, HD)]).then_inc(wq_in, 16)

        @block.sync
        def _(sp):
            sp.dma_start(ptab[:, :], A["page_table"].rearrange("(a s) b -> a (s b)", a=1)).then_inc(tab_in, 16)
            sp.wait_ge(tab_in, 16)

            def load_kv(s, half, wait):
                pages = [sp.value_load(ptab[0:1, bass.ds(s * NPG + b, 1)], min_val=0, max_val=POOL - 1)
                         for b in range(NPG)]
                if wait:
                    sp.wait_ge(kt_ps2, 4 * s - 4)
                for b, pg in enumerate(pages):
                    sp.dma_start(kpg[:, half, b, :].unsqueeze(1), ck[:, bass.ds(pg, 1), :]).then_inc(kv_half[half], 16)
                if wait:
                    sp.wait_ge(so_ps, s - 1)
                for b, pg in enumerate(pages):
                    sp.dma_start(vpg[:, half, b, :].unsqueeze(1), cv[:, bass.ds(pg, 1), :]).then_inc(kv_half[half], 16)

            with sp.Fori(0, NSEQ) as s:
                for b in range(NPG):
                    pg = sp.value_load(ptab[0:1, bass.ds(s * NPG + b, 1)], min_val=0, max_val=POOL - 1)
                    sp.dma_start(lfp[:, b, bass.ds(s, 1), :], cl[:, bass.ds(pg, 1), :]).then_inc(lf_in, 16)
            for half in range(2):
                load_kv(half, half, False)
            sp.wait_ge(kx_ok, 1)
            sp.dma_start(S["ydram"][LEAST_BLK * BLK:SLOTS, :].rearrange("(b p) d -> p b d", p=P),
                         bc(blank.unsqueeze(1), [P, (NBLK - LEAST_BLK) * BLK // P, D])).then_inc(blank_out, 16)
            with sp.Fori(1, NSEQ // 2) as i:
                for half in range(2):
                    load_kv(2 * i + half, half, True)
            sp.wait_ge(blank_out, 16)

        @block.gpsimd
        def _(pool):
            load_wq(pool, 0)
            pool.memset(qpad[:, :, :], 0.0).then_inc(zero_ok, 1)
            pool.memset(qblk[:, :, :, :], 0.0)
            pool.drain()
            pool.memset(mx[:, :], 0.0).then_inc(zero_ok, 1)
            with pool.Fori(1, 8) as t:
                pool.wait_ge(q_ps, t)
                load_wq(pool, t)
            pool.tensor_scalar(ntri[:, :], S["tri_le2"][0:64, 0:64], -1.0, None, ALU.mult)
            pool.tensor_scalar(selfneg[:, :, :], S["self01"][:, :, :], 1.0, -NEG, ALU.subtract, ALU.mult)
            pool.drain()
            pool.wait_ge(q_blk, 16)
            with pool.Fori(0, NSEQ) as s:
                pool.wait_ge(cur_free, s + 1)
                pool.sem_inc(gate)
                pool.tensor_copy(qcur[:, :, :], qblk[:, bass.ds(s, 1), :, :].rearrange("p o a c -> p (o a) c"))
                pool.tensor_copy(mcur[:, :], selfneg[:, bass.ds(s, 1), :].rearrange("k o c -> k (o c)"))
                pool.tensor_copy(scur[:, :].rearrange("k (h q) -> k h q", q=8),
                                 bc(idn[:, bass.ds(16 * s, 16)].unsqueeze(2), [P, 16, 8]))
                pool.tensor_tensor(lcur[:, :], S["lf_rep"][:, :, :].rearrange("k h q -> k (h q)"),
                                   S["self01"][:, bass.ds(s, 1), :].rearrange("k o c -> k (o c)"),
                                   ALU.mult).then_inc(cur_ok, 1)

        @block.scalar
        def _(act):
            act.sem_inc(o_ev, 1)
            act.wait_ge(zero_ok, 1)

            def q_out(t):
                act.wait_ge(q_ps, t + 1)
                for g2 in range(2):
                    q_ = slice(64 * g2, 64 * g2 + 64)
                    act.activation(qpad[q_, g2, :], ps[0][q_, 0:T], ACT.Copy, scale=HD ** -0.5).then_inc(q_ev, 1)

            def probs(t):
                for g2 in range(2):
                    for c in range(3):
                        k = 3 * g2 + c
                        r = qrows[c]
                        act.wait_ge(nm_ok, 6 * t + k + 1)
                        act.activation(sc[0:r, g2, c, 0:keys[c]], sc[0:r, g2, c, 0:keys[c]], ACT.Exp,
                                       bias=nm[0:r, k:k + 1], accum_out=rs[0:r, k:k + 1]).then_inc(p_ok, 1)
                for g2 in range(2):
                    act.wait_ge(pt_ps, 2 * t + g2 + 1)
                    act.activation(pt[:, g2, 0:416], ps[5 + 2 * g2][:, 0:416], ACT.Copy)
                    act.activation(pt[0:80, g2, 416:432], ps[5 + 2 * g2][0:80, 416:432], ACT.Copy).then_inc(pt_ev, 1)

            def o_out(t):
                act.wait_ge(o_ps, t + 1)
                act.activation(S["oT"][:, bass.ds(t, 1), 0:256], ps[6][:, 0:256].unsqueeze(1), ACT.Copy)
                act.activation(S["oT"][:, bass.ds(t, 1), 320:336], ps[6][:, 256:272].unsqueeze(1),
                               ACT.Copy).then_inc(o_ev, 1)

            q_out(0)
            with act.Fori(0, 7) as t:
                probs(t)
                q_out(t + 1)
                o_out(t)
            probs(7)
            o_out(7)

            def keys_out(s):
                for b in range(2):
                    act.wait_ge(kt_ps2, 4 * s + b + 1)
                    act.activation(kts[:, 0, 512 * b:512 * b + 512], ps[b][:, :], ACT.Copy).then_inc(kt_ev, 1)

            def seq(s):
                act.wait_ge(m_ok2, s + 1)
                act.activation(pr[:, 0:PAST].rearrange("p (a c) -> p a c", a=2), psc[:, :, :], ACT.Exp,
                               bias=mx[:, 4:5], accum_out=sm[:, 0:1]).then_inc(e_ok, 1)
                act.activation(pr[:, PAST:PAST + NS], ps[6][:, 0:NS], ACT.Exp, bias=mx[:, 4:5],
                               accum_out=sm[:, 1:2]).then_inc(e_ok, 1)
                act.wait_ge(pp_ps, 3 * s + 1)
                act.activation(pts[:, 0:4, :], psc[:, 0, :].rearrange("p (b c) -> p b c", c=P), ACT.Copy)
                act.drain()
                act.wait_ge(pp_ps, 3 * s + 3)
                act.activation(ptself[:, :], ps[6][0:NS, P:2 * P], ACT.Copy).then_inc(pp_ev, 1)

            keys_out(0)
            with act.Fori(0, NSEQ - 1) as s:
                seq(s)
                keys_out(s + 1)
            seq(NSEQ - 1)

        @block.vector
        def _(v):
            v.sem_inc(cur_free, 1)
            v.memset(kx[:, :, :, :], 0.0)
            v.memset(sc[:, :, :, :], 0.0)
            v.memset(blank, 0.0)
            v.drain()
            for g2 in range(2):
                o = 64 - 64 * g2
                for u in range(2):
                    v.tensor_copy(kx[64 * g2:64 * g2 + 64, g2, u, :], S["kT"][64 * g2:64 * g2 + 64, u, :])
                    v.tensor_copy(kx[o:o + 16, g2, u, :], S["ncT"][:, :]).then_inc(kx_ok, 1)
            v.wait_ge(zero_ok, 2)
            with v.Fori(0, 8) as t:
                for g2 in range(2):
                    o = 64 - 64 * g2
                    h = head(t, g2)
                    v.tensor_scalar(qpad[o:o + 16, g2, :], bc(S["ones"][o:o + 16, 0:1], [16, T]),
                                    idn[o:o + 16, bass.ds(h + o, 1)], None, ALU.mult).then_inc(pick_ok, 1)
                for g2 in range(2):
                    q_ = slice(64 * g2, 64 * g2 + 64)
                    v.wait_ge(q_ev, 2 * t + g2 + 1)
                    v.tensor_copy(qblk[q_, :, :, :].rearrange("p s a c -> p s (a c)")[
                        :, :, bass.ds((t // 4) * 192 + (t % 4) * 8 + 32 * g2, 8)],
                        qpad[q_, g2, 256:320].rearrange("p (s q) -> p s q", q=8)).then_inc(q_blk, 1)
                for g2 in range(2):
                    h = head(t, g2)
                    v.wait_ge(s_ps, 2 * t + g2 + 1)
                    for c in range(3):
                        r, n = qrows[c], keys[c]
                        mask = (S["mask_d"][:, 128:256], S["mask_d"][:, :], S["mask_t"][:, :])[c]
                        v.scalar_tensor_tensor(sc[0:r, g2, c, 0:n], score_bank(g2, c),
                                               S["c_q"][0:r, c, bass.ds(h, 1)], mask, ALU.add, ALU.add)
                    v.drain()
                    for c in range(3):
                        r, n = qrows[c], keys[c]
                        v.tensor_reduce(nm[0:r, 3 * g2 + c:3 * g2 + c + 1], sc[0:r, g2, c, 0:n], AX.X, ALU.max,
                                        negate=True).then_inc(nm_ok, 1)
                for g2 in range(2):
                    v.wait_ge(p_ok, 6 * t + 3 * g2 + 3)
                    for c in range(3):
                        k = 3 * g2 + c
                        v.reciprocal(rs[0:qrows[c], k:k + 1], rs[0:qrows[c], k:k + 1])
                    v.drain()
                    for c in range(3):
                        k = 3 * g2 + c
                        r, n = qrows[c], keys[c]
                        i = v.tensor_scalar(sc[0:r, g2, c, 0:n], sc[0:r, g2, c, 0:n], rs[0:r, k:k + 1], None, ALU.mult)
                    i.then_inc(pn_ok, 1)
            for b in range(2):
                v.wait_ge(r_ps, 1)
                v.tensor_copy(rall[:, 512 * b:512 * b + 512], psc[:, b, :]).then_inc(r_ev, 1)
            def keys_out(s):
                for b in range(2):
                    v.wait_ge(kt_ps2, 4 * s + b + 3)
                    v.tensor_copy(kts[:, 1, 512 * b:512 * b + 512], ps[2 + b][:, :]).then_inc(kt_evb, 1)

            def o_out(s):
                v.wait_ge(sot_ps, s + 1)
                for g2 in range(2):
                    q_ = slice(64 * g2, 64 * g2 + 64)
                    v.tensor_copy(S["oT"][q_, :, bass.ds(8 * s + 256, 8)].rearrange("p (a r) q -> p a r q", a=2),
                                  ps[7][q_, 256:384].rearrange("p (a g r q) -> p a g r q", a=2, g=2, q=8)[:, :, g2]
                                  ).then_inc(sot_ev, 1)

            def seq(s, last, next_):
                v.wait_ge(ss_ps, s + 1)
                v.tensor_reduce(mx[:, 0:1], psc[:, :, :].rearrange("p a c -> p (a c)"), AX.X,
                                ALU.max).then_inc(cur_free, 1)
                v.tensor_reduce(mx[:, 1:2], ps[6][:, 0:NS], AX.X, ALU.max)
                v.tensor_copy(mx[:, 2:3], ps[6][:, NS:NS + 1])
                v.drain()
                v.scalar_tensor_tensor(mx[:, 3:4], mx[:, 0:1], mx[:, 1:2], mx[:, 2:3], ALU.max, ALU.add)
                v.drain()
                v.tensor_tensor(mx[:, 4:5], mx[:, 2:3], mx[:, 3:4], ALU.subtract).then_inc(m_ok2, 1)
                if next_:
                    keys_out(s + 1)
                if last:
                    o_out(s - 1)
                v.wait_ge(pp_ps, 3 * s + 2)
                v.tensor_copy(pts[:, 4:8, :], psc[:, 1, :].rearrange("p (b c) -> p b c", c=P)).then_inc(pp_ev, 1)
                v.wait_ge(e_ok, 2 * s + 2)
                v.tensor_tensor(sm[:, 2:3], sm[:, 0:1], sm[:, 1:2], ALU.add)
                v.drain()
                v.reciprocal(sm[:, 2:3], sm[:, 2:3])
                v.drain()
                v.wait_ge(so_ps, s + 1)
                v.tensor_scalar(oe[:, :], ps[7][:, 0:P], sm[:, 2:3], None, ALU.mult).then_inc(so_ev, 1)

            keys_out(0)
            seq(0, False, True)
            with v.Fori(1, NSEQ - 1) as s:
                seq(s, True, True)
            seq(NSEQ - 1, True, False)
            o_out(NSEQ - 1)

        @block.tensor
        def _(pe):
            def project_q(t):
                pe.wait_ge(wq_in, 32 * t + 32)
                for k in range(KT):
                    mm = pe.matmul(ps[0][:, 0:T], wq[:, k, :, :], S["xnT"][:, k, :], start=(k == 0),
                                   stop=(k == KT - 1))
                mm.then_inc(q_ps, 1)

            def scores(t):
                pe.wait_ge(q_ev, 2 * t + 2)
                pe.wait_ge(pick_ok, 2 * t + 2)
                for g2 in range(2):
                    for c in range(3):
                        r, n = qrows[c], keys[c]
                        o = score_bank(g2, c)
                        kt = kx[:, g2, bass.ds(t // 4, 1), 0:n].rearrange("p o c -> p (o c)")
                        mm = pe.matmul(o, qpad[:, g2, qcol[c]:qcol[c] + r], kt, start=True, stop=True)
                    mm.then_inc(s_ps, 1)

            def outputs(t, u):
                for g2 in range(2):
                    pe.wait_ge(pn_ok, 2 * t + g2 + 1)
                    b = ps[5 + 2 * g2]
                    pe.transpose(b[:, 0:128], sc[:, g2, 0, 0:128], idn[:, :])
                    for j in range(2):
                        pe.transpose(b[:, 128 + 144 * j:256 + 144 * j], sc[:, g2, 1, P * j:P * j + P], idn[:, :])
                        pe.transpose(b[:, 256 + 144 * j:272 + 144 * j], sc[0:16, g2, 2, P * j:P * j + P],
                                     idn[0:16, 0:16])
                    pe.transpose(b[0:80, 416:432], sc[0:16, g2, 2, 256:336], idn[0:16, 0:16]).then_inc(pt_ps, 1)
                pe.wait_ge(pt_ev, 2 * t + 2)
                pe.wait_ge(o_ev, t + 1)
                for c, r in enumerate(ROWS):
                    for g2 in range(2):
                        col, n, to = ((0, 272, 0), (272, 144, 128), (416, 16, 256))[c]
                        mm = pe.matmul(ps[6][64 * g2:64 * g2 + 64, to:272], S["v"][0:r, c, P * u + HD * g2:P * u + HD * g2 + HD],
                                       pt[0:r, g2, col:col + n], start=(c == 0), stop=(c == 2))
                mm.then_inc(o_ps, 1)

            pe.wait_ge(kx_ok, 4)
            project_q(0)
            for u in range(2):
                with pe.Fori(4 * u, 4 + 3 * u) as t:
                    scores(t)
                    project_q(t + 1)
                    outputs(t, u)
            scores(7)
            outputs(7, 1)
            pe.wait_ge(o_ev, 9)
            pe.wait_ge(lf_in, 16 * NSEQ * NPG)
            for b in range(NPG):
                o = psc[:, b // 4, P * (b % 4):P * (b % 4) + P]
                mm = pe.matmul(o, lfp[:, b, :, :], S["tri_gt"][:, :], start=True, stop=(b == NPG - 1))
                for b2 in range(b + 1, NPG):
                    mm = pe.matmul(o, lfp[:, b2, :, :], S["ones"][:, :], start=False, stop=(b2 == NPG - 1))
            mm.then_inc(r_ps, 1)
            pe.wait_ge(r_ev, 2)
            def turn_keys(i, half):
                pe.wait_ge(kv_half[half], 32 * NPG * i + 32 * NPG)
                for a in range(2):
                    for hb in range(2):
                        for b in range(4):
                            mm = pe.transpose(ps[2 * a + hb][:, P * b:P * b + P],
                                              kpg[:, half, 4 * hb + b, P * a:P * a + P], idn[:, :])
                        mm.then_inc(kt_ps2, 1)

            def seq_scores(s):
                pe.wait_ge(cur_ok, s + 1)
                sf = ps[6][:, 0:NS]
                for a in range(2):
                    pe.matmul(sf, qcur[:, a, :], S["kT"][:, a, 256:320], start=(a == 0), stop=False)
                pe.matmul(sf, S["lf_rep"][:, :, :].rearrange("k h q -> k (h q)"), ntri[:, :], start=False,
                          stop=False)
                pe.matmul(sf, mcur[:, :], idn[0:NS, 0:NS], start=False, stop=True)
                pe.matmul(ps[6][:, NS:NS + 1], lcur[:, :], S["ones"][0:NS, 0:1], start=True, stop=True)
                for b in range(2):
                    pe.matmul(psc[:, b, :], scur[:, :], rall[:, 512 * b:512 * b + 512], start=True, stop=False)
                pe.wait_ge(kt_ev, 2 * s + 2)
                pe.wait_ge(kt_evb, 2 * s + 2)
                for b in range(2):
                    for a in range(2):
                        q_ = slice(64 * a, 64 * a + 64)
                        mm = pe.matmul(psc[q_, b, :], qcur[:, a, q_], kts[:, a, 512 * b:512 * b + 512],
                                       start=False, stop=True)
                mm.then_inc(ss_ps, 1)

            def seq_outputs(s, half, last):
                pe.wait_ge(e_ok, 2 * s + 2)
                for hb in range(2):
                    for b in range(4):
                        c = P * (4 * hb + b)
                        mm = pe.transpose(psc[:, hb, P * b:P * b + P], pr[:, c:c + P], idn[:, :])
                    mm.then_inc(pp_ps, 1)
                pe.transpose(ps[6][0:NS, P:2 * P], pr[:, PAST:PAST + NS], idn[:, :]).then_inc(pp_ps, 1)
                pe.wait_ge(pp_ev, 2 * s + 2)
                if last:
                    pe.wait_ge(sot_ev, 2 * s)
                for b in range(NPG + 1):
                    for a in range(2):
                        q_, d = slice(64 * a, 64 * a + 64), slice(P * a, P * a + P)
                        if b < NPG:
                            pe.matmul(ps[7][q_, 0:P], pts[:, b, q_], vpg[:, half, b, d], start=(b == 0), stop=False)
                        else:
                            mm = pe.matmul(ps[7][q_, 0:P], ptself[:, q_], S["v"][0:NS, 2, d], start=False, stop=True)
                mm.then_inc(so_ps, 1)

            def turn_rows(s):
                pe.wait_ge(so_ev, s + 1)
                pe.transpose(ps[7][:, 256:384], oe[:, :], idn[:, :]).then_inc(sot_ps, 1)

            turn_keys(0, 0)
            seq_scores(0)
            turn_keys(0, 1)
            seq_outputs(0, 0, False)
            with pe.Fori(0, NSEQ // 2 - 1) as i:
                for u in range(2):
                    s = 2 * i + u + 1
                    seq_scores(s)
                    turn_keys(i + 1, u)
                    turn_rows(s - 1)
                    seq_outputs(s, 1 - u, True)
            seq_scores(NSEQ - 1)
            turn_rows(NSEQ - 2)
            seq_outputs(NSEQ - 1, 1, True)
            turn_rows(NSEQ - 1)
            pe.wait_ge(sot_ev, 2 * NSEQ)


def merge_phase(nc, A, S, sem):
    with ExitStack() as ctx:
        def tsb(name, shape, dt=F32):
            return ctx.enter_context(nc.sbuf_tensor(name, shape, dt))

        wm = [tsb(f"w_merge{h}", [P, 40, P]) for h in range(2)]
        wo = tsb("w_out_sb", [P, KT, D])
        th2 = tsb("gate_tanh", [P, 2, 2, T])
        th = [th2[:, h, :, :] for h in range(2)]
        xsq = th2[:, :, :, :].rearrange("p a j t -> p (a j t)")[:, 0:D]
        mx_ = [tsb(f"mix_part{h}", [P, 2, T]) for h in range(2)]
        mixT = S["mixT"]
        ss = tsb("ss2", [P, 4])
        wr = tsb("w_router", [P, KT, 36])
        ps = [ctx.enter_context(nc.psum_tensor(f"psm{i}", [P, 512], F32)) for i in range(8)]
        wg_half = [sem("merge_gates_even"), sem("merge_gates_odd")]
        wb_half = [sem("merge_branches_even"), sem("merge_branches_odd")]
        wo_in, wr_in, g_ps, g_th, b_ps, mix_ok, h_ps, h_ev, hn_ok, tr_ps, tr_ev, lg_ps = (
            sem(n) for n in ("wo_in", "wr_in", "gate_ps", "gate_th", "branch_ps", "mix_ok", "h_ps", "h_ev",
                             "hn_ok", "hnt_ps", "hnt_ev", "logit_ps"))
        ssq, rs_ok = S["row_squares_ok"], S["row_rstd_ok"]
        mix_used = sem("mix_banks_free")
        win = A["w_in"].rearrange("a (t p) c -> p (a t) c", p=P)
        wsb = A["w_ssd_br"].rearrange("a (t p) c -> p (a t) c", p=P)
        wab = A["w_attn_br"].rearrange("a (u g r d) c -> g d (a u) r c", u=2, g=2, r=4)
        block = ctx.enter_context(nc.Block())

        @block.sync
        def _(sp):
            def load(m, h):
                sp.dma_start(wm[h][:, 0:8, :], win[:, :, bass.ds(m * P + C_GS, P)]).then_inc(wg_half[h], 16)
                sp.dma_start(wm[h][:, 8:16, :], win[:, :, bass.ds(m * P + C_GS + D, P)]).then_inc(wg_half[h], 16)
                sp.dma_start(wm[h][:, 16:32, :], wsb[:, :, bass.ds(m * P, P)]).then_inc(wb_half[h], 16)
                for g2 in range(2):
                    for u in range(2):
                        sp.dma_start(wm[h][64 * g2:64 * g2 + 64, 32 + 4 * u:36 + 4 * u, :],
                                     wab[g2, :, u, :, bass.ds(m * P, P)]).then_inc(wb_half[h], 16)

            load(0, 0)
            load(1, 1)
            sp.dma_start(wo[:, :, :], A["w_out"].rearrange("a (t p) c -> p (a t) c", p=P)).then_inc(wo_in, 16)
            sp.dma_start(wr[:, :, 0:4], A["w_router_group"].rearrange("a (t p) c -> p (a t) c", p=P)).then_inc(wr_in, 16)
            sp.dma_start(wr[:, :, 4:36], A["w_router_expert"].rearrange("a (t p) c -> p (a t) c", p=P)).then_inc(wr_in, 16)
            sp.dma_start(S["rbias"][:, 0:4], A["b_router_group"][0, :].partition_broadcast(P)).then_inc(wr_in, 16)
            sp.dma_start(S["rbias"][:, 4:36], A["b_router_expert"][0, :].partition_broadcast(P)).then_inc(wr_in, 16)
            with sp.Fori(1, 4) as i:
                for h in range(2):
                    sp.wait_ge(b_ps, 2 * i + h - 1)
                    load(2 * i + h, h)
            load_gate_up(sp, A, S, 0, 0, S["gate_up_in"][0])
            load_down(sp, A, S, 0, 0, S["down_in"][0])

        @block.gpsimd
        def _(pool):
            for t, r in enumerate(ROWS):
                pool.wait_ge(ssq, 3 + t + 1)
                pool.tensor_scalar(ss[0:r, t:t + 1], ss[0:r, t:t + 1], 1.0 / D, EPS, ALU.mult, ALU.add)
                pool.drain()
                pool.tensor_tensor(ss[0:r, t:t + 1], ss[0:r, t:t + 1], S["mhalf"][0:r, 0:1], ALU.pow).then_inc(rs_ok, 1)

        @block.scalar
        def _(act):
            with act.Fori(0, 4) as i:
                for h in range(2):
                    m = 2 * i + h
                    for j in range(2):
                        act.wait_ge(g_ps, 2 * m + j + 1)
                        act.activation(th[h][:, j, :], ps[4 * h + j][:, 0:T], ACT.Tanh, scale=0.5).then_inc(g_th, 1)
            for t, r in enumerate(ROWS):
                act.wait_ge(h_ev, 2 * t + 2)
                act.activation(xsq[0:r, :], S["xtok"][0:r, t, :], ACT.Square,
                               accum_out=ss[0:r, t:t + 1]).then_inc(ssq, 1)
                act.drain()

        @block.vector
        def _(v):
            v.sem_inc(mix_used, 2)
            with v.Fori(0, 4) as i:
                for h in range(2):
                    m = 2 * i + h
                    v.wait_ge(g_th, 2 * m + 2)
                    v.wait_ge(b_ps, m + 1)
                    for j in range(2):
                        k = v.scalar_tensor_tensor(mx_[h][:, j, :], th[h][:, j, :], 1.0, ps[4 * h + 2 + j][:, 0:T],
                                                   ALU.add, ALU.mult)
                    k.then_inc(mix_used, 1)
                    v.drain()
                    v.tensor_tensor(mixT[:, bass.ds(m, 1), :], mx_[h][:, 0, :].unsqueeze(1),
                                    mx_[h][:, 1, :].unsqueeze(1), ALU.add).then_inc(mix_ok, 1)
            for t, r in enumerate(ROWS):
                for h in range(2):
                    v.wait_ge(h_ps, 2 * t + h + 1)
                    x = S["xtok"][0:r, t, 512 * h:512 * h + 512]
                    v.scalar_tensor_tensor(x, ps[2 * t + h][0:r, :], 0.5, x, ALU.mult, ALU.add).then_inc(h_ev, 1)
            for t, r in enumerate(ROWS):
                v.wait_ge(rs_ok, 3 + t + 1)
                v.tensor_scalar(S["hn"][0:r, t, :], S["xtok"][0:r, t, :], ss[0:r, t:t + 1], None,
                                ALU.mult).then_inc(hn_ok, 1)
            for t, r in enumerate(ROWS):
                for h in range(2):
                    v.wait_ge(tr_ps, 2 * t + h + 1)
                    v.tensor_tensor(S["hnT"][:, 4 * h:4 * h + 4, COL[t]:COL[t] + r],
                                    ps[2 * t + h][:, :].rearrange("p (k c) -> p k c", c=P)[:, :, 0:r],
                                    bc(S["gcol"][:, 24 + 4 * h:28 + 4 * h].unsqueeze(2), [P, 4, r]),
                                    ALU.mult).then_inc(tr_ev, 1)
            v.memset(S["lg"][:, :, :], 0.0)
            v.drain()
            v.wait_ge(lg_ps, 1)
            for t, r in enumerate(ROWS):
                v.tensor_tensor(S["lg"][0:r, t, :], ps[6][0:r, 64 * t:64 * t + 36], S["rbias"][0:r, :],
                                ALU.add)

        @block.tensor
        def _(pe):
            with pe.Fori(0, 4) as i:
                for h in range(2):
                    m = 2 * i + h
                    pe.wait_ge(wg_half[h], 32 * i + 32)
                    pe.wait_ge(mix_used, m + 1)
                    for j in range(2):
                        for k in range(KT):
                            mm = pe.matmul(ps[4 * h + j][:, 0:T], wm[h][:, 8 * j + k, :], S["xnT"][:, k, :],
                                           start=(k == 0), stop=(k == KT - 1))
                        mm.then_inc(g_ps, 1)
                    pe.wait_ge(wb_half[h], 80 * i + 80)
                    for k in range(16):
                        pe.matmul(ps[4 * h + 2][:, 0:T], wm[h][:, 16 + k, :], S["yT"][:, k, :], start=(k == 0),
                                  stop=(k == 15))
                    for k in range(8):
                        mm = pe.matmul(ps[4 * h + 3][:, 0:T], wm[h][:, 32 + k, :], S["oT"][:, k, :], start=(k == 0),
                                       stop=(k == 7))
                    mm.then_inc(b_ps, 1)
            pe.wait_ge(wo_in, 16)
            pe.wait_ge(mix_ok, 8)
            for t, r in enumerate(ROWS):
                for h in range(2):
                    for k in range(KT):
                        mm = pe.matmul(ps[2 * t + h][0:r, :], mixT[:, k, COL[t]:COL[t] + r],
                                       wo[:, k, 512 * h:512 * h + 512], start=(k == 0), stop=(k == KT - 1))
                    mm.then_inc(h_ps, 1)
            pe.wait_ge(h_ev, 6)
            for t, r in enumerate(ROWS):
                pe.wait_ge(hn_ok, t + 1)
                for h in range(2):
                    for k in range(4):
                        mm = pe.transpose(ps[2 * t + h][:, P * k:P * k + r],
                                          S["hn"][0:r, t, P * (4 * h + k):P * (4 * h + k + 1)], S["ident"][0:r, 0:r])
                    mm.then_inc(tr_ps, 1)
            pe.wait_ge(tr_ev, 6)
            pe.wait_ge(wr_in, 64)
            for t, r in enumerate(ROWS):
                for k in range(KT):
                    mm = pe.matmul(ps[6][0:r, 64 * t:64 * t + 36], S["hnT"][:, k, COL[t]:COL[t] + r], wr[:, k, :],
                                   start=(k == 0), stop=(k == KT - 1))
            mm.then_inc(lg_ps, 1)


def route_phase(nc, A, S, sem):
    with ExitStack() as ctx:
        def tsb(name, shape, dt=F32):
            return ctx.enter_context(nc.sbuf_tensor(name, shape, dt))

        it32i, it32 = tsb("iota32_i", [P, 32], I32), tsb("iota32", [P, 32])
        it64i, itbi, itb = tsb("iota64_i", [P, BLK], I32), tsb("iota_blk_i", [1, NBLK], I32), tsb("iota_blk", [1, NBLK])
        g4, gm, eg, cand, cm = (tsb("g4", [P, 3, 4]), tsb("gmax", [P, 3]), tsb("g_exp", [P, 3, 4]),
                                tsb("cand", [P, 3, 32]), tsb("cmin", [P, 3]))
        og, pen = tsb("g_onehot", [P, 3, 4]), tsb("g_penalty", [P, 3, 4])
        el, l1, l2, oh = tsb("el", [P, 3, 32]), tsb("l1", [P, 3]), tsb("l2", [P, 3]), tsb("e_onehot", [P, 2, 3, 32])
        pg, dd, ee = tsb("p_group", [P, 3]), tsb("l_diff", [P, 3]), tsb("l_exp", [P, 3])
        mm_, rank, cnt, nb, pend, start = (tsb("pair_mask", [P, 3, 32]), tsb("rank", [P, 3, 32]), tsb("cnt", [P, 32]),
                                           tsb("n_blocks", [P, 32]), tsb("blocks_end", [P, 32]),
                                           tsb("blocks_start", [P, 32]))
        tmp, cmpb, bef, tri_lt = (tsb("slot_tmp", [P, 3, 32]), tsb("blk_cmp", [1, NBLK, 32]), tsb("blk_e_f", [1, NBLK]),
                                  tsb("tri_lt", [P, P]))
        ps = [ctx.enter_context(nc.psum_tensor(f"psr{i}", [P, 512], F32)) for i in range(2)]
        io_ok, gx, ge, lx, le_, mk, rk_ps = (sem(n) for n in ("iotas", "g_in", "g_exp_ok", "l_in", "l_exp_ok",
                                                                     "mask_ok", "rank_ps"))
        block = ctx.enter_context(nc.Block())

        @block.sync
        def _(sp):
            load_gate_up(sp, A, S, 1, 1, S["gate_up_in"][1])
            load_down(sp, A, S, 1, 1, S["down_in"][1])
            load_gate_up(sp, A, S, 2, 2, S["gate_up_in"][2])

        @block.gpsimd
        def _(pool):
            pool.iota(it32i[:, :], pattern=[[1, 32]], base=0, channel_multiplier=0)
            pool.iota(it64i[:, :], pattern=[[1, BLK]], base=0, channel_multiplier=0)
            pool.iota(itbi[:, :], pattern=[[1, NBLK]], base=0, channel_multiplier=0)
            pool.drain()
            pool.tensor_copy(it32[:, :], it32i[:, :])
            pool.tensor_copy(S["iota"][:, :], it64i[:, :])
            pool.tensor_copy(itb[:, :], itbi[:, :])
            pool.tensor_tensor(tri_lt[:, :], S["tri_le"][:, :], S["ident"][:, :], ALU.subtract).then_inc(io_ok, 1)

        @block.scalar
        def _(act):
            act.wait_ge(gx, 1)
            act.activation(eg[:, :, :], g4[:, :, :], ACT.Exp).then_inc(ge, 1)
            act.wait_ge(lx, 1)
            act.activation(ee[:, :], dd[:, :], ACT.Exp).then_inc(le_, 1)

        @block.tensor
        def _(pe):
            pe.wait_ge(mk, 1)
            m = [mm_[0:r, t, :] for t, r in enumerate(ROWS)]
            o = S["ones"]
            pe.matmul(ps[0][:, 0:32], tri_lt[:, :], m[0], start=True, stop=True)
            pe.matmul(ps[0][:, 32:64], o[:, :], m[0], start=True, stop=False)
            pe.matmul(ps[0][:, 32:64], tri_lt[:, :], m[1], start=False, stop=True)
            pe.matmul(ps[0][0:80, 64:96], o[:, 0:80], m[0], start=True, stop=False)
            pe.matmul(ps[0][0:80, 64:96], o[:, 0:80], m[1], start=False, stop=False)
            pe.matmul(ps[0][0:80, 64:96], tri_lt[0:80, 0:80], m[2], start=False, stop=True)
            pe.matmul(ps[1][:, 0:32], o[:, :], m[0], start=True, stop=False)
            pe.matmul(ps[1][:, 0:32], o[:, :], m[1], start=False, stop=False)
            pe.matmul(ps[1][:, 0:32], o[0:80, :], m[2], start=False, stop=True).then_inc(rk_ps, 1)

        @block.vector
        def _(v):
            lg = S["lg"]
            b3 = lambda a, n: bc(a.unsqueeze(2), [P, 3, n])
            i32_ = bc(it32[:, :].unsqueeze(1), [P, 3, 32])
            v.tensor_reduce(gm[:, :], lg[:, :, 0:4], AX.X, ALU.max)
            v.drain()
            v.tensor_tensor(g4[:, :, :], lg[:, :, 0:4], b3(gm[:, :], 4), ALU.subtract).then_inc(gx, 1)
            v.tensor_tensor(og[:, :, :], lg[:, :, 0:4], b3(gm[:, :], 4), ALU.is_equal)
            v.wait_ge(io_ok, 1)

            def first(onehot, eq, n):
                v.drain()
                v.scalar_tensor_tensor(cand[:, :, 0:n], eq, -100.0, bc(it32[:, 0:n].unsqueeze(1), [P, 3, n]),
                                       ALU.mult, ALU.add)
                v.drain()
                v.tensor_reduce(cm[:, :], cand[:, :, 0:n], AX.X, ALU.min)
                v.drain()
                v.tensor_tensor(onehot, cand[:, :, 0:n], b3(cm[:, :], n), ALU.is_equal)
                v.drain()

            first(og[:, :, :], og[:, :, :], 4)
            v.tensor_scalar(pen[:, :, :], og[:, :, :], 1.0, -NEG, ALU.subtract, ALU.mult)
            v.tensor_tensor(el[:, :, :].rearrange("p t (g e) -> p t g e", g=4),
                            lg[:, :, 4:36].rearrange("p t (g e) -> p t g e", g=4),
                            bc(og[:, :, :].unsqueeze(3), [P, 3, 4, 8]), ALU.mult)
            v.drain()
            v.tensor_tensor(el[:, :, :].rearrange("p t (g e) -> p t g e", g=4),
                            el[:, :, :].rearrange("p t (g e) -> p t g e", g=4),
                            bc(pen[:, :, :].unsqueeze(3), [P, 3, 4, 8]), ALU.add)
            v.drain()
            v.tensor_reduce(l1[:, :], el[:, :, :], AX.X, ALU.max)
            v.drain()
            v.tensor_tensor(oh[:, 0, :, :], el[:, :, :], b3(l1[:, :], 32), ALU.is_equal)
            first(oh[:, 0, :, :], oh[:, 0, :, :], 32)
            v.scalar_tensor_tensor(el[:, :, :], oh[:, 0, :, :], 3 * NEG, el[:, :, :], ALU.mult, ALU.add)
            v.drain()
            v.tensor_reduce(l2[:, :], el[:, :, :], AX.X, ALU.max)
            v.drain()
            v.tensor_tensor(dd[:, :], l2[:, :], l1[:, :], ALU.subtract).then_inc(lx, 1)
            v.tensor_tensor(oh[:, 1, :, :], el[:, :, :], b3(l2[:, :], 32), ALU.is_equal)
            first(oh[:, 1, :, :], oh[:, 1, :, :], 32)
            v.tensor_tensor(mm_[:, :, :], oh[:, 0, :, :], oh[:, 1, :, :], ALU.add).then_inc(mk, 1)
            v.wait_ge(ge, 1)
            v.tensor_reduce(pg[:, :], eg[:, :, :], AX.X, ALU.add)
            v.wait_ge(le_, 1)
            v.drain()
            v.reciprocal(pg[:, :], pg[:, :])
            v.tensor_scalar(dd[:, :], ee[:, :], 1.0, None, ALU.add)
            v.drain()
            v.reciprocal(dd[:, :], dd[:, :])
            v.drain()
            v.tensor_tensor(S["topw"][:, :, 0], pg[:, :], dd[:, :], ALU.mult)
            v.drain()
            v.tensor_tensor(S["topw"][:, :, 1], S["topw"][:, :, 0], ee[:, :], ALU.mult)
            v.wait_ge(rk_ps, 1)
            v.memset(rank[:, :, :], 0.0)
            v.drain()
            v.tensor_copy(rank[:, 0:2, :], ps[0][:, 0:64].rearrange("p (t e) -> p t e", t=2))
            v.tensor_copy(rank[0:80, 2, :], ps[0][0:80, 64:96])
            v.tensor_copy(cnt[:, :], ps[1][:, 0:32])
            v.drain()
            v.tensor_scalar(nb[:, :], cnt[:, :], 0.5, None, ALU.is_gt)
            v.drain()
            for k in range(1, -(-T // BLK)):
                v.scalar_tensor_tensor(nb[:, :], cnt[:, :], BLK * k + 0.5, nb[:, :], ALU.is_gt, ALU.add)
                v.drain()
            v.tensor_tensor_scan(pend[:, :], S["ones"][:, 0:32], nb[:, :], 0.0, ALU.mult, ALU.add)
            v.drain()
            v.tensor_tensor(start[:, :], pend[:, :], nb[:, :], ALU.subtract)
            v.drain()
            v.scalar_tensor_tensor(rank[:, :, :], bc(start[:, :].unsqueeze(1), [P, 3, 32]), float(BLK),
                                   rank[:, :, :], ALU.mult, ALU.add)
            v.drain()
            for j in range(2):
                v.tensor_tensor(tmp[:, :, :], oh[:, j, :, :], rank[:, :, :], ALU.mult)
                v.drain()
                v.tensor_reduce(S["slot"][:, :, j:j + 1], tmp[:, :, :], AX.X, ALU.add)
                v.drain()
            v.tensor_copy(S["slot_i"][:, :, :], S["slot"][:, :, :])
            v.tensor_tensor(cmpb[:, :, :], bc(pend[0:1, :].unsqueeze(1), [1, NBLK, 32]),
                            bc(itb[:, :].unsqueeze(2), [1, NBLK, 32]), ALU.is_le)
            v.drain()
            v.tensor_reduce(bef[:, :], cmpb[:, :, :], AX.X, ALU.add)
            v.drain()
            v.tensor_scalar(S["blk_e"][:, 0:NBLK], bef[:, :], float(NE - 1), None, ALU.min)
            v.tensor_copy(S["blk_e"][:, NBLK:NBLK + 1], pend[0:1, NE - 1:NE])


def load_gate_up(eng, A, S, h, e, done):
    for j, w in enumerate(("w_exp_gate", "w_exp_up")):
        eng.dma_start(S["w_gate_up"][h][:, j, :, :], A[w].rearrange("a e (t p) f -> p (a e) t f", p=P)[
            :, bass.ds(e, 1)].rearrange("p o t f -> p (o t) f")).then_inc(done, 16)


def load_down(eng, A, S, h, e, done):
    eng.dma_start(S["w_down"][h][:, :, :], A["w_exp_down"].rearrange("a e (t p) d -> p (a e) t d", p=P)[
        :, bass.ds(e, 1)].rearrange("p o t d -> p (o t) d")).then_inc(done, 16)


def moe_phase(nc, A, S, sem):
    with ExitStack() as ctx:
        def tsb(name, shape, dt=F32):
            return ctx.enter_context(nc.sbuf_tensor(name, shape, dt))

        w_gu, w_dn, gu_in, dn_in = S["w_gate_up"], S["w_down"], S["gate_up_in"], S["down_in"]
        rel = tsb("slot_rel", [P, 3, 2])
        eq = tsb("slot_eq", [P, 3, 2, BLK])
        sel = tsb("block_rows", [P, 3, BLK])
        xrow = tsb("x_rows", [P, 512])
        xg = tsb("x_gathered", [P, 4, 2, BLK])
        th, hg, hrow = tsb("h_tanh", [P, 256]), tsb("h_gate", [P, 256]), tsb("h_rows", [P, 256])
        ht = tsb("h_t", [P, 2, 2, BLK])
        yr = [tsb(f"y_block{h}", [P, 512]) for h in range(2)]
        px, pxt, ph, pht = (ctx.enter_context(nc.psum_tensor(n, [P, 512], F32)) for n in ("px", "pxt", "ph", "pht"))
        py = [ctx.enter_context(nc.psum_tensor(f"py{h}", [P, 512], F32)) for h in range(2)]
        sel_ok, xr_ps, xr_ev, xt_ps, xt_ok, gu_ps, th_ok, hb_ok, ht_ps, ht_ok, y_ps, y_ev, gu_free = (
            sem(n) for n in ("sel_ok", "xrow_ps", "xrow_ev", "xt_ps", "xt_ok", "gu_ps", "hth_ok", "h_ok", "ht_t_ps",
                             "ht_ok", "yb_ps", "yb_ev", "gate_up_free"))
        w_ok = sem("weights_checked")
        again = sem("reloaded")
        y_sent = [sem("y_sent_even"), sem("y_sent_odd")]
        ydram = S["ydram"].rearrange("s (j d) -> s j d", j=2)
        block = ctx.enter_context(nc.Block())

        def blocks_of(eng):
            return eng.value_load(S["blk_e"][0:1, NBLK:NBLK + 1], min_val=1, max_val=NBLK)

        @block.sync
        def _(sp):
            nblk = blocks_of(sp)
            sp.sem_inc(y_sent[0], 32)
            sp.sem_inc(y_sent[1], 32)
            for h in range(3):
                e = sp.value_load(S["blk_e"][0:1, h:h + 1], min_val=0, max_val=NE - 1)
                sp.wait_ge(gu_in[h], 32)
                if h < 2:
                    sp.wait_ge(dn_in[h], 16)
                with sp.If(e != h):
                    load_gate_up(sp, A, S, h, e, again)
                    if h < 2:
                        load_down(sp, A, S, h, e, again)
                    else:
                        sp.sem_inc(again, 16)
                with sp.If(e == h):
                    sp.sem_inc(again, 48)
                sp.wait_ge(again, 48 * h + 48)
                sp.sem_inc(w_ok, 1)

            def load(b, h):
                with sp.If(b < nblk):
                    e = sp.value_load(S["blk_e"][0:1, bass.ds(b, 1)], min_val=0, max_val=NE - 1)
                    sp.wait_ge(y_ev, b + 1)
                    load_down(sp, A, S, h % 2, e, dn_in[h % 2])
                with sp.If(b + 2 < nblk):
                    e = sp.value_load(S["blk_e"][0:1, bass.ds(b + 2, 1)], min_val=0, max_val=NE - 1)
                    sp.wait_ge(gu_free, b)
                    load_gate_up(sp, A, S, (h + 2) % 3, e, gu_in[(h + 2) % 3])
                    sp.sem_inc(w_ok, 1)

            e = sp.value_load(S["blk_e"][0:1, 3:4], min_val=0, max_val=NE - 1)
            sp.wait_ge(gu_free, 1)
            load_gate_up(sp, A, S, 0, e, gu_in[0])
            sp.sem_inc(w_ok, 1)
            for h in range(2, 6):
                load(h, h)
            with sp.Fori(1, NBLK // 6) as i:
                for h in range(6):
                    load(6 * i + h, h)

        @block.scalar
        def _(act):
            nblk = blocks_of(act)
            act.sem_inc(y_ev, 2)

            def rows_out(n):
                act.wait_ge(xr_ps, n)
                act.activation(xrow[:, :], px[:, :], ACT.Copy).then_inc(xr_ev, 1)

            rows_out(1)
            with act.Fori(0, NBLK // 6) as i:
                for u in range(6):
                    b, h = 6 * i + u, u % 2
                    with act.If(b < nblk):
                        act.wait_ge(gu_ps, b + 1)
                        act.activation(th[:, :], ph[:, 0:256], ACT.Tanh, scale=0.5).then_inc(th_ok, 1)
                        rows_out(b + 2)
                        act.wait_ge(y_ps, b + 1)
                        act.wait_ge(y_sent[h], 96 * i + 32 * (u // 2) + 32)
                        act.activation(yr[h][:, :], py[h][:, :], ACT.Copy).then_inc(y_ev, 1)
                        act.drain()
                        for j in range(2):
                            act.dma_start(ydram[bass.ds(BLK * b, BLK), j, :], yr[h][64 * j:64 * j + 64, :]
                                          ).then_inc(y_sent[h], 16)
            for h in range(2):
                act.wait_ge(y_sent[h], 32 * ((nblk + (1 - h)) // 2) + 32)
                act.sem_inc(S["pool_passed"])

        @block.vector
        def _(v):
            nblk = blocks_of(v)
            v.tensor_copy(rel[:, :, :], S["slot"][:, :, :])

            def pick():
                v.drain()
                v.tensor_tensor(eq[:, :, :, :].rearrange("p t j c -> p (t j) c"),
                                bc(S["iota"][:, :].unsqueeze(1), [P, 6, BLK]),
                                bc(rel[:, :, :].rearrange("p t j -> p (t j)").unsqueeze(2), [P, 6, BLK]),
                                ALU.is_equal)
                v.drain()
                v.tensor_tensor(sel[:, :, :], eq[:, :, 0, :], eq[:, :, 1, :], ALU.add).then_inc(sel_ok, 1)
                v.tensor_scalar(rel[:, :, :], rel[:, :, :], -float(BLK), None, ALU.add)

            def gathered(n):
                v.wait_ge(xt_ps, n)
                v.tensor_tensor(xg[:, :, :, :], pxt[:, :].rearrange("p (c j s) -> p c j s", c=4, j=2),
                                bc(S["gcol"][:, 24:32].rearrange("p (j c) -> p c j", j=2).unsqueeze(3),
                                   [P, 4, 2, BLK]), ALU.mult).then_inc(xt_ok, 1)

            pick()
            gathered(1)
            with v.Fori(0, NBLK // 2) as i:
                for u in range(2):
                    b = 2 * i + u
                    with v.If(b < nblk):
                        pick()
                        v.wait_ge(th_ok, b + 1)
                        v.scalar_tensor_tensor(hg[:, :], th[:, :], 1.0, ph[:, 0:256], ALU.add,
                                               ALU.mult).then_inc(gu_free, 1)
                        v.drain()
                        v.scalar_tensor_tensor(hrow[:, :], hg[:, :], 0.5, ph[:, 256:512], ALU.mult,
                                               ALU.mult).then_inc(hb_ok, 1)
                        v.wait_ge(ht_ps, b + 1)
                        v.tensor_copy(ht[:, :, :, :], pht[:, 0:256].rearrange("p (c j s) -> p c j s", c=2, j=2)
                                      ).then_inc(ht_ok, 1)
                        gathered(b + 2)

        @block.tensor
        def _(pe):
            nblk = blocks_of(pe)

            def gather_rows(n):
                pe.wait_ge(sel_ok, n)
                for t, r in enumerate(ROWS):
                    for j in range(2):
                        mm = pe.matmul(px[64 * j:64 * j + 64, :], sel[0:r, t, :], S["hn"][0:r, t, 512 * j:512 * j + 512],
                                       start=(t == 0), stop=(t == 2))
                mm.then_inc(xr_ps, 1)

            def gather_turn(n):
                pe.wait_ge(xr_ev, n)
                for c in range(4):
                    mm = pe.transpose(pxt[:, P * c:P * c + P], xrow[:, P * c:P * c + P], S["ident"][:, :])
                mm.then_inc(xt_ps, 1)

            gather_rows(1)
            gather_turn(1)
            with pe.Fori(0, NBLK // 6) as i:
                for u in range(6):
                    b, h, w = 6 * i + u, u % 2, u % 3
                    with pe.If(b < nblk):
                        pe.wait_ge(xt_ok, b + 1)
                        pe.wait_ge(w_ok, b + 1)
                        pe.wait_ge(gu_in[w], 64 * i + 32 * (u // 3) + 32)
                        for k in range(KT):
                            for j in range(2):
                                mm = pe.matmul(ph[64 * j:64 * j + 64, :], xg[:, k % 4, k // 4, :],
                                               w_gu[w][:, :, k, 256 * j:256 * j + 256],
                                               start=(k == 0), stop=(k == KT - 1))
                        mm.then_inc(gu_ps, 1)
                        gather_rows(b + 2)
                        pe.wait_ge(hb_ok, b + 1)
                        for c in range(2):
                            mm = pe.transpose(pht[:, P * c:P * c + P], hrow[:, P * c:P * c + P], S["ident"][:, :])
                        mm.then_inc(ht_ps, 1)
                        gather_turn(b + 2)
                        pe.wait_ge(ht_ok, b + 1)
                        pe.wait_ge(dn_in[h], 48 * i + 16 * (u // 2) + 16)
                        pe.wait_ge(y_ev, b + 1)
                        for k in range(4):
                            for j in range(2):
                                mm = pe.matmul(py[h][64 * j:64 * j + 64, :], ht[:, k % 2, k // 2, :],
                                               w_dn[h][:, k, 512 * j:512 * j + 512], start=(k == 0), stop=(k == 3))
                        mm.then_inc(y_ps, 1)


def final_phase(nc, A, S, sem):
    with ExitStack() as ctx:
        def tsb(name, shape, dt=F32):
            return ctx.enter_context(nc.sbuf_tensor(name, shape, dt))

        ye = tsb("y_expert", [P, 3, 2, D])
        fg = tsb("final_g", [P, D])
        xsq, ss, out = tsb("xsq3", [P, D]), tsb("ss3", [P, 4]), tsb("y_final", [P, 3, D])
        ssq, rs_ok = S["row_squares_ok"], S["row_rstd_ok"]
        ye_in = [sem("y_expert_in0"), sem("y_expert_in12")]
        g_in, h_ok, out_ok, sent = (sem(n) for n in (
            "final_g_in", "h2_ok", "out_ok", "sent"))
        block = ctx.enter_context(nc.Block())

        @block.sync
        def _(sp):
            sp.dma_start(fg[:, :], A["final_norm_g"].partition_broadcast(P)).then_inc(g_in, 16)
            yp = A["y_p"].rearrange("a s d -> (a s) d")
            sp.wait_ge(out_ok, 1)
            sp.dma_start(yp[0:112, :], out[16:128, 0, :]).then_inc(sent, 16)
            sp.wait_ge(out_ok, 2)
            sp.dma_start(yp[112:240, :], out[:, 1, :]).then_inc(sent, 16)
            sp.wait_ge(out_ok, 3)
            sp.dma_start(A["y_s"].rearrange("a s d -> (a s) d"), out[0:64, 2, :]).then_inc(sent, 16)
            sp.dma_start(yp[240:256, :], out[64:80, 2, :]).then_inc(sent, 16)
            sp.wait_ge(sent, 64)

        @block.gpsimd
        def _(pool):
            for t, r in enumerate(ROWS):
                for j in range(2):
                    pool.indirect_dma_start(ye[0:r, t, j, :], None, S["ydram"],
                                            bass.IndirectOffsetOnAxis(ap=S["slot_i"][0:r, t, j:j + 1], axis=0)
                                            ).then_inc(ye_in[min(t, 1)], 16)
            for t, r in enumerate(ROWS):
                pool.wait_ge(ssq, 6 + t + 1)
                pool.tensor_scalar(ss[0:r, t:t + 1], ss[0:r, t:t + 1], 1.0 / D, EPS, ALU.mult, ALU.add)
                pool.drain()
                pool.tensor_tensor(ss[0:r, t:t + 1], ss[0:r, t:t + 1], S["mhalf"][0:r, 0:1], ALU.pow).then_inc(rs_ok, 1)

        @block.scalar
        def _(act):
            for t, r in enumerate(ROWS):
                act.wait_ge(h_ok, t + 1)
                act.activation(xsq[0:r, :], S["xtok"][0:r, t, :], ACT.Square,
                               accum_out=ss[0:r, t:t + 1]).then_inc(ssq, 1)
                act.drain()

        @block.vector
        def _(v):
            for t, r in enumerate(ROWS):
                v.wait_ge(ye_in[min(t, 1)], 64 if t else 32)
                v.tensor_scalar(ye[0:r, t, 0, :], ye[0:r, t, 0, :], S["topw"][0:r, t, 0:1], None, ALU.mult)
                v.drain()
                v.scalar_tensor_tensor(ye[0:r, t, 1, :], ye[0:r, t, 1, :], S["topw"][0:r, t, 1:2], ye[0:r, t, 0, :],
                                       ALU.mult, ALU.add)
                v.drain()
                v.tensor_tensor(S["xtok"][0:r, t, :], S["xtok"][0:r, t, :], ye[0:r, t, 1, :], ALU.add).then_inc(h_ok, 1)
            v.wait_ge(g_in, 16)
            for t, r in enumerate(ROWS):
                v.wait_ge(rs_ok, 6 + t + 1)
                v.scalar_tensor_tensor(out[0:r, t, :], S["xtok"][0:r, t, :], ss[0:r, t:t + 1], fg[0:r, :], ALU.mult,
                                       ALU.mult).then_inc(out_ok, 1)


def build_layer(nc, A):
    with ExitStack() as ctx:
        S = {}

        def sem(name):
            return ctx.enter_context(nc.semaphore(name))

        def sb(name, shape, dt=F32, stack=ctx):
            S[name] = stack.enter_context(nc.sbuf_tensor(name, shape, dt))

        for name, shape in (("ident", [P, P]), ("ones", [P, P]), ("mhalf", [P, 4]), ("gcol", [P, 32]),
                            ("xtok", [P, 3, D]), ("yT", [P, 16, T]), ("topw", [P, 3, 2]), ("slot", [P, 3, 2]),
                            ("iota", [P, BLK])):
            sb(name, shape)
        sb("slot_i", [P, 3, 2], U32)
        sb("blk_e", [1, NBLK + 2], I32)
        S["hn"] = S["yT"][:, :, :].rearrange("p k t -> p (k t)")[:, 0:3 * D].rearrange("p (t d) -> p t d", t=3)
        S["ydram"] = nc.dram_tensor("expert_rows", [SLOTS, D], F32, kind="Internal").ap()
        for name in ("pool_passed", "row_squares_ok", "row_rstd_ok", "w_channels_in", "w_z_in"):
            S[name] = sem(name)
        S["gate_up_in"] = [sem(f"gate_up_in{h}") for h in range(3)]
        S["down_in"] = [sem("down_even"), sem("down_odd")]
        with ExitStack() as front:
            sb("tri_le", [P, P], stack=front)
            sb("stretch", [P, KT * (T + 768)], stack=front)
            S["xnT"] = S["stretch"][:, 0:KT * T].rearrange("p (k t) -> p k t", k=KT)
            wg = S["stretch"][:, KT * T:KT * (T + 768)]
            S["w_group"] = wg.rearrange("p (k c) -> p k c", k=KT)
            S["oT"] = wg[:, 0:8 * T].rearrange("p (k t) -> p k t", k=8)
            S["mixT"] = wg[:, 8 * T:16 * T].rearrange("p (k t) -> p k t", k=KT)
            S["hnT"] = S["xnT"]
            with ExitStack() as mixers:
                for name, shape in (
                        ("tri_gt", [P, P]), ("tri_le2", [80, 80]), ("tri_gt2", [80, 80]),
                        ("tailrow", [80, P]), ("seg8", [NS, 8]), ("mask_d", [P, 256]), ("mask_t", [16, 336]),
                        ("self01", [NS, NSEQ, P]), ("conv_wh", [P, 4, 32]), ("conv_bh", [P, 32]),
                        ("sc_t", [P, NSEQ, 3, 32]), ("k", [P, 3, 256]), ("v", [P, 3, 256]),
                        ("kT", [P, 2, T]), ("lf", [P, 3, 16]), ("c_q", [P, 3, 16]), ("ncT", [16, T]),
                        ("lf_rep", [NS, 16, 8]), ("dt", [P, 3, 32]), ("dta", [P, 3, 32]), ("eac", [P, 3, 32]),
                        ("w_end", [P, 3, 32]), ("dec", [P, 3, 32]), ("dec_s", [P, 16, 8]), ("dskip", [P, 32])):
                    sb(name, shape, stack=mixers)
                setup_phase(nc, A, S, sem)
                ssd_phase(nc, A, S, sem)
                attention_phase(nc, A, S, sem)
            with ExitStack() as experts:
                sb("lg", [P, 3, 36], stack=experts)
                sb("rbias", [P, 36], stack=experts)
                S["w_gate_up"] = [experts.enter_context(nc.sbuf_tensor("w_gate_up0", [P, 2, KT, DE], F32))]
                S["w_down"] = [experts.enter_context(nc.sbuf_tensor("w_down0", [P, DE // P, D], F32))]
                merge_phase(nc, A, S, sem)
                S["w_gate_up"].append(experts.enter_context(nc.sbuf_tensor("w_gate_up1", [P, 2, KT, DE], F32)))
                S["w_down"].append(experts.enter_context(nc.sbuf_tensor("w_down1", [P, DE // P, D], F32)))
                S["w_gate_up"].append(S["stretch"][:, 0:2 * KT * DE].rearrange("p (j k f) -> p j k f", j=2, k=KT))
                route_phase(nc, A, S, sem)
                moe_phase(nc, A, S, sem)
        final_phase(nc, A, S, sem)


_INS = ['x_prompt', 'x_sample', 'cache_k', 'cache_v', 'cache_logf', 'state_ssm', 'state_conv', 'page_table',
        'meta_tokens', 'norm1_g', 'w_in', 'conv_w', 'conv_b', 'dt_bias', 'a_log', 'd_skip', 'ssd_norm_g',
        'b_forget', 'w_ssd_br', 'w_attn_br', 'w_out', 'norm2_g', 'w_router_group', 'b_router_group',
        'w_router_expert', 'b_router_expert', 'w_exp_gate', 'w_exp_up', 'w_exp_down', 'final_norm_g']
_OUTS = [("y_p", (1, 256, 1024)), ("y_s", (8, 8, 1024)), ("k_p", (1, 1, 272, 4, 64)), ("v_p", (1, 1, 272, 4, 64)),
         ("lf_p", (1, 1, 272, 16)), ("ssm_p", (1, 1, 32, 64, 128)), ("conv_p", (1, 1, 3, 4096)),
         ("k_s", (1, 8, 8, 4, 64)), ("v_s", (1, 8, 8, 4, 64)), ("lf_s", (1, 8, 8, 16)),
         ("ssm_s", (1, 8, 32, 64, 128)), ("conv_s", (1, 8, 3, 4096))]


def kernel(**inputs):
    import numpy as _np
    import concourse.bacc as _bacc
    from concourse import mybir as _mybir
    from concourse.bass_utils import run_bass_kernel_spmd as _run

    nc = _bacc.Bacc("TRN2", target_bir_lowering=False, num_devices=1)
    arrays, aps = {}, {}
    for name in _INS:
        a = _np.ascontiguousarray(inputs[name])
        arrays[f"in_{name}"] = a
        aps[name] = nc.dram_tensor(f"in_{name}", a.shape, _mybir.dt.from_np(a.dtype), kind="ExternalInput").ap()
    for name, shape in _OUTS:
        aps[name] = nc.dram_tensor(f"out_{name}", shape, _mybir.dt.float32, kind="ExternalOutput").ap()
    build_layer(nc, aps)
    r = _run(nc, [arrays], core_ids=[0])
    return tuple(r.results[0][f"out_{name}"] for name, _ in _OUTS)
```
